# Optimizing a Trainium2 kernel written in Bass

```python
import math
import jax
import jax.numpy as jnp
from jax import lax
import numpy as np

D_MODEL = 1024
BATCH = 1
SEQ = 1024
DEPTH = 4

F32 = jnp.float32
GRID_W = 64
CTX_LEN = 256
N_MIXERS = 3
N_LAYERS_RWKV = (DEPTH + 2) // 3
N_LAYERS_NA = (DEPTH + 1) // 3
N_LAYERS_S5 = DEPTH // 3
D_INNER = D_MODEL
NORM_EPS = 1e-6

RWKV_HEAD_DIM = 64
RWKV_HEADS = D_INNER // RWKV_HEAD_DIM
RWKV_DECAY_LORA = 64
RWKV_ICLR_LORA = 64
RWKV_GN_EPS = 64e-5
RWKV_N_MIX = 6

NA_HEAD_DIM = 64
NA_HEADS = D_INNER // NA_HEAD_DIM
NA_KH_MAX = 8
NA_KW = 16

S5_GROUP = 16
S5_GROUPS = D_INNER // S5_GROUP
S5_STATE = 64
S5_DT_MIN = 1e-3
S5_DT_MAX = 1e-1

kernel_name = "hybrid_rwkv7_natten_s5_prefix_block"

def _rms_norm(x, g):
    xf = x.astype(F32)
    y = xf * lax.rsqrt(jnp.mean(xf * xf, axis=-1, keepdims=True) + NORM_EPS)
    return (y * g.astype(F32)).astype(x.dtype)

def _head_rms(x, g):
    xf = x.astype(F32)
    y = xf * lax.rsqrt(jnp.mean(xf * xf, axis=-1, keepdims=True) + NORM_EPS)
    return (y * g.astype(F32)).astype(x.dtype)

def _head_l2norm(x, n_heads):
    xf = x.astype(F32).reshape(x.shape[:-1] + (n_heads, -1))
    n = jnp.sqrt(jnp.sum(xf * xf, axis=-1, keepdims=True))
    return (xf / jnp.maximum(n, 1e-12)).reshape(x.shape)

def _centred_shift(h):
    prev = jnp.pad(h[:, :-1], ((0, 0), (1, 0), (0, 0)))
    nxt = jnp.pad(h[:, 1:], ((0, 0), (0, 1), (0, 0)))
    return 0.5 * (prev + nxt)

def _seg_flip(a, n_ctx, axis):
    a_c, a_l = jnp.split(a, [n_ctx], axis=axis)
    return jnp.concatenate([jnp.flip(a_c, axis), jnp.flip(a_l, axis)], axis=axis)

def _rwkv7_step(state, inp):
    r, w, k, v, kk, a = inp
    sa = jnp.einsum("dbhvk,dbhk->dbhv", state, kk)
    state = (state * w[..., None, :] - sa[..., None] * (kk * a)[..., None, :]
             + v[..., None] * k[..., None, :])
    return state, jnp.einsum("dbhvk,dbhk->dbhv", state, r)

def _complex_affine_combine(e1, e2):
    a1r, a1i, b1r, b1i = e1
    a2r, a2i, b2r, b2i = e2
    return (a2r * a1r - a2i * a1i,
            a2r * a1i + a2i * a1r,
            a2r * b1r - a2i * b1i + b2r,
            a2r * b1i + a2i * b1r + b2i)

def _rwkv7_mixer(hc, hx, mu, w_rkvg, w0, w1, w2, a0, a1, a2, k_k, k_a, r_k,
                 ln_w, ln_b, w_out, need_ctx):
    dt = hx.dtype
    n_ctx = hc.shape[1]
    h = jnp.concatenate([hc, hx], axis=1)
    bsz, t_all, _ = h.shape
    xx = jnp.concatenate([_centred_shift(hc), _centred_shift(hx)], axis=1) - h
    xs = h[None] + xx[None] * mu[:, None, None, :]
    r, k, v, g = jnp.einsum("nbtd,nde->nbte", xs[:4], w_rkvg)
    dec_lora = jnp.einsum("sbtr,sre->sbte",
                          jnp.tanh(jnp.einsum("btd,sdr->sbtr", xs[4], w1)), w2)
    w_log = -jax.nn.softplus(-(w0[:, None, None, :] + dec_lora).astype(F32)) - 0.5
    decay = jnp.exp(-jnp.exp(w_log))
    iclr = jax.nn.sigmoid((a0[:, None, None, :] + jnp.einsum(
        "sbtr,sre->sbte", jnp.einsum("btd,sdr->sbtr", xs[5], a1), a2)).astype(F32))
    kk = _head_l2norm(k * k_k, RWKV_HEADS)
    k_dir = k.astype(F32)[None] * (1.0 + (iclr - 1.0) * k_a.astype(F32))

    def to_scan(a):
        a = jnp.stack([a[0], _seg_flip(a[1], n_ctx, 1)]).astype(F32)
        return a.reshape(2, bsz, t_all, RWKV_HEADS, RWKV_HEAD_DIM).transpose(2, 0, 1, 3, 4)

    def shared(a):
        return to_scan(jnp.stack([a, a]))

    s0 = jnp.zeros((2, bsz, RWKV_HEADS, RWKV_HEAD_DIM, RWKV_HEAD_DIM), F32)
    _, y = lax.scan(_rwkv7_step, s0, (shared(r), to_scan(decay), to_scan(k_dir),
                                      shared(v), shared(kk), to_scan(iclr)))
    y = y.transpose(1, 2, 0, 3, 4)
    y = y[0] + _seg_flip(y[1], n_ctx, 1)
    if not need_ctx:
        y, r, k, v, g = (a[:, n_ctx:] for a in (y, r, k, v, g))

    def heads(a):
        return a.astype(F32).reshape(a.shape[0], a.shape[1], RWKV_HEADS, RWKV_HEAD_DIM)

    mean = jnp.mean(y, axis=-1, keepdims=True)
    var = jnp.mean(jnp.square(y - mean), axis=-1, keepdims=True)
    yn = ((y - mean) * lax.rsqrt(var + RWKV_GN_EPS)
          * ln_w.astype(F32).reshape(RWKV_HEADS, RWKV_HEAD_DIM)
          + ln_b.astype(F32).reshape(RWKV_HEADS, RWKV_HEAD_DIM))
    bonus = jnp.sum(heads(r) * heads(k) * r_k.astype(F32), axis=-1, keepdims=True) * heads(v)
    o = (yn + bonus).reshape(bsz, -1, D_INNER) * jax.nn.silu(g.astype(F32))
    o = o.astype(dt) @ w_out
    if need_ctx:
        return o[:, :n_ctx], o[:, n_ctx:]
    return None, o

def _na_mixer(hc, hx, w_in, q_g, k_g, rpb, w_out, need_ctx):
    dt = hx.dtype
    bsz, n_lat, _ = hx.shape
    n_ctx = hc.shape[1]
    rows = n_lat // GRID_W
    kh = min(NA_KH_MAX, rows)
    n_nb = kh * NA_KW
    scale = NA_HEAD_DIM ** -0.5

    def project(h):
        q, k, v, z = jnp.split(h @ w_in, 4, axis=-1)
        split = lambda a: a.reshape(a.shape[0], a.shape[1], NA_HEADS, NA_HEAD_DIM)
        return _head_rms(split(q), q_g), _head_rms(split(k), k_g), split(v), z

    qc, kc, vc, zc = project(hc)
    qx, kx, vx, zx = project(hx)
    kc_h = kc.transpose(0, 2, 1, 3)
    vc_h = vc.transpose(0, 2, 1, 3)
    grid = lambda a: a.reshape(bsz, rows, GRID_W, NA_HEADS, NA_HEAD_DIM).transpose(0, 3, 1, 2, 4)
    qg, kg, vg = grid(qx), grid(kx), grid(vx)

    row_start = jnp.clip(jnp.arange(rows) - kh // 2, 0, rows - kh)
    cols = jnp.arange(GRID_W)
    col_idx = (jnp.clip(cols - NA_KW // 2, 0, GRID_W - NA_KW)[:, None]
               + jnp.arange(NA_KW)[None, :])
    rpb_cols = rpb[:, :, col_idx - cols[:, None] + NA_KW - 1].astype(F32)

    def row_block(i):
        r0 = row_start[i]
        qi = lax.dynamic_index_in_dim(qg, i, axis=2, keepdims=False)
        k_nb = lax.dynamic_slice_in_dim(kg, r0, kh, axis=2)[:, :, :, col_idx]
        v_nb = lax.dynamic_slice_in_dim(vg, r0, kh, axis=2)[:, :, :, col_idx]
        bias = jnp.take(rpb_cols, r0 + jnp.arange(kh) - i + NA_KH_MAX - 1,
                        axis=1).transpose(0, 2, 1, 3)
        s_nb = jnp.einsum("bhqd,bhrqcd->bhqrc", qi, k_nb).astype(F32) * scale + bias[None]
        s_ctx = jnp.einsum("bhqd,bhld->bhql", qi, kc_h).astype(F32) * scale
        p = jax.nn.softmax(jnp.concatenate(
            [s_nb.reshape(bsz, NA_HEADS, GRID_W, n_nb), s_ctx], axis=-1), axis=-1).astype(dt)
        p_nb = p[..., :n_nb].reshape(bsz, NA_HEADS, GRID_W, kh, NA_KW)
        return (jnp.einsum("bhqrc,bhrqcd->bhqd", p_nb, v_nb)
                + jnp.einsum("bhql,bhld->bhqd", p[..., n_nb:], vc_h))

    o_x = lax.map(row_block, jnp.arange(rows))
    o_x = o_x.transpose(1, 0, 3, 2, 4).reshape(bsz, n_lat, D_INNER)
    out_x = (o_x * jax.nn.silu(zx)) @ w_out
    if not need_ctx:
        return None, out_x
    qc_h = qc.transpose(0, 2, 1, 3)
    p_c = jax.nn.softmax(jnp.einsum("bhqd,bhkd->bhqk", qc_h, kc_h).astype(F32) * scale,
                         axis=-1).astype(dt)
    o_c = jnp.einsum("bhqk,bhkd->bhqd", p_c, vc_h).transpose(0, 2, 1, 3).reshape(bsz, n_ctx, D_INNER)
    return (o_c * jax.nn.silu(zc)) @ w_out, out_x

def _s5_mixer(hc, hx, w_in, lam_re, lam_im, log_dt, b_re, b_im, c_re, c_im, d_skip,
              w_glu, b_glu, w_out, need_ctx):
    dt = hx.dtype
    n_ctx = hc.shape[1]
    h = jnp.concatenate([hc, hx], axis=1)
    bsz, t_all, _ = h.shape
    u, z = jnp.split(h @ w_in, 2, axis=-1)
    u_t = jnp.swapaxes(u.astype(F32).reshape(bsz, t_all, S5_GROUPS, S5_GROUP), 0, 1)
    br, bi = b_re.astype(F32), b_im.astype(F32)
    cr, ci = c_re.astype(F32), c_im.astype(F32)
    y = jnp.zeros_like(u_t)
    for s in range(2):
        lr, li = lam_re[s].astype(F32), lam_im[s].astype(F32)
        step = jnp.exp(log_dt[s].astype(F32))[:, None]
        mag = jnp.exp(lr * step)
        ar, ai = mag * jnp.cos(li * step), mag * jnp.sin(li * step)
        den = lr * lr + li * li
        qr = ((ar - 1.0) * lr + ai * li) / den
        qi = (ai * lr - (ar - 1.0) * li) / den
        bbr = qr[..., None] * br - qi[..., None] * bi
        bbi = qr[..., None] * bi + qi[..., None] * br
        u_s = u_t if s == 0 else _seg_flip(u_t, n_ctx, 0)
        bu_r = jnp.einsum("gpc,tbgc->tbgp", bbr, u_s)
        bu_i = jnp.einsum("gpc,tbgc->tbgp", bbi, u_s)
        a_shape = (t_all, 1, S5_GROUPS, S5_STATE)
        _, _, xr, xi = lax.associative_scan(
            _complex_affine_combine,
            (jnp.broadcast_to(ar, a_shape), jnp.broadcast_to(ai, a_shape), bu_r, bu_i), axis=0)
        y_s = jnp.einsum("gcp,tbgp->tbgc", cr, xr) - jnp.einsum("gcp,tbgp->tbgc", ci, xi)
        y = y + (y_s if s == 0 else _seg_flip(y_s, n_ctx, 0))
    y = jnp.swapaxes(y, 0, 1).reshape(bsz, t_all, D_INNER) + d_skip.astype(F32) * u.astype(F32)
    if not need_ctx:
        y, z = y[:, n_ctx:], z[:, n_ctx:]
    y = jax.nn.gelu(y).astype(dt)
    y = y * jax.nn.sigmoid(y @ w_glu + b_glu)
    o = (y * jax.nn.silu(z)) @ w_out
    if need_ctx:
        return o[:, :n_ctx], o[:, n_ctx:]
    return None, o

def setup_inputs(seed: int = 0) -> dict:
    key = jax.random.key(seed)
    keys = iter(jax.random.split(key, 64))
    nrm = lambda shape, s: jax.random.normal(next(keys), shape, F32) * s
    D, E = D_MODEL, D_INNER
    na, nb, nc = N_LAYERS_RWKV, N_LAYERS_NA, N_LAYERS_S5
    inp = {}
    inp["x"] = nrm((BATCH, SEQ, D), 1.0)
    inp["c"] = nrm((BATCH, D), 1.0)
    inp["ctx"] = nrm((BATCH, CTX_LEN, D), 1.0)
    inp["c_ctx"] = nrm((D,), 1.0)
    inp["norm_g"] = 1.0 + nrm((DEPTH, D), 0.02)
    inp["w_mod"] = nrm((DEPTH, D, 3 * D), 0.5 * D ** -0.5)
    inp["b_mod"] = nrm((DEPTH, 3 * D), 0.02)
    inp["rwkv_mu"] = jax.random.uniform(next(keys), (na, RWKV_N_MIX, D), F32)
    inp["rwkv_w_rkvg"] = nrm((na, 4, D, E), D ** -0.5)
    ramp = -6.0 + 5.0 * jnp.linspace(0.0, 1.0, E, dtype=F32)
    inp["rwkv_w0"] = ramp[None, None, :] + nrm((na, 2, E), 0.1)
    inp["rwkv_w1"] = nrm((na, 2, D, RWKV_DECAY_LORA), D ** -0.5)
    inp["rwkv_w2"] = nrm((na, 2, RWKV_DECAY_LORA, E), 0.1 * RWKV_DECAY_LORA ** -0.5)
    inp["rwkv_a0"] = nrm((na, 2, E), 0.1)
    inp["rwkv_a1"] = nrm((na, 2, D, RWKV_ICLR_LORA), D ** -0.5)
    inp["rwkv_a2"] = nrm((na, 2, RWKV_ICLR_LORA, E), 0.1 * RWKV_ICLR_LORA ** -0.5)
    inp["rwkv_k_k"] = 0.85 + nrm((na, E), 0.02)
    inp["rwkv_k_a"] = 1.0 + nrm((na, E), 0.02)
    inp["rwkv_r_k"] = nrm((na, RWKV_HEADS, RWKV_HEAD_DIM), 0.1)
    inp["rwkv_ln_w"] = 1.0 + nrm((na, E), 0.02)
    inp["rwkv_ln_b"] = nrm((na, E), 0.02)
    inp["rwkv_w_out"] = nrm((na, E, D), E ** -0.5)
    inp["na_w_in"] = nrm((nb, D, 4 * E), D ** -0.5)
    inp["na_q_g"] = 1.0 + nrm((nb, NA_HEAD_DIM), 0.02)
    inp["na_k_g"] = 1.0 + nrm((nb, NA_HEAD_DIM), 0.02)
    inp["na_rpb"] = nrm((nb, NA_HEADS, 2 * NA_KH_MAX - 1, 2 * NA_KW - 1), 0.1)
    inp["na_w_out"] = nrm((nb, E, D), E ** -0.5)
    inp["s5_w_in"] = nrm((nc, D, 2 * E), D ** -0.5)
    inp["s5_lam_re"] = -0.5 + nrm((nc, 2, S5_GROUPS, S5_STATE), 0.01)
    inp["s5_lam_im"] = (math.pi * jnp.arange(S5_STATE, dtype=F32))[None, None, None, :] + nrm(
        (nc, 2, S5_GROUPS, S5_STATE), 0.01)
    inp["s5_log_dt"] = jax.random.uniform(next(keys), (nc, 2, S5_GROUPS), F32,
                                          math.log(S5_DT_MIN), math.log(S5_DT_MAX))
    inp["s5_b_re"] = nrm((nc, S5_GROUPS, S5_STATE, S5_GROUP), (2 * S5_GROUP) ** -0.5)
    inp["s5_b_im"] = nrm((nc, S5_GROUPS, S5_STATE, S5_GROUP), (2 * S5_GROUP) ** -0.5)
    inp["s5_c_re"] = nrm((nc, S5_GROUPS, S5_GROUP, S5_STATE), S5_STATE ** -0.5)
    inp["s5_c_im"] = nrm((nc, S5_GROUPS, S5_GROUP, S5_STATE), S5_STATE ** -0.5)
    inp["s5_d"] = nrm((nc, E), 0.5)
    inp["s5_w_glu"] = nrm((nc, E, E), E ** -0.5)
    inp["s5_b_glu"] = nrm((nc, E), 0.02)
    inp["s5_w_out"] = nrm((nc, E, D), E ** -0.5)
    return inp

def reference(x, c, ctx, c_ctx, norm_g, w_mod, b_mod,
              rwkv_mu, rwkv_w_rkvg, rwkv_w0, rwkv_w1, rwkv_w2, rwkv_a0, rwkv_a1, rwkv_a2,
              rwkv_k_k, rwkv_k_a, rwkv_r_k, rwkv_ln_w, rwkv_ln_b, rwkv_w_out,
              na_w_in, na_q_g, na_k_g, na_rpb, na_w_out,
              s5_w_in, s5_lam_re, s5_lam_im, s5_log_dt, s5_b_re, s5_b_im, s5_c_re, s5_c_im,
              s5_d, s5_w_glu, s5_b_glu, s5_w_out):
    dt = x.dtype
    silu_c = jax.nn.silu(c.astype(F32))
    silu_cc = jax.nn.silu(c_ctx.astype(F32))
    for i in range(DEPTH):
        kind, j = i % N_MIXERS, i // N_MIXERS
        need_ctx = i < DEPTH - 1
        wm, bm = w_mod[i].astype(F32), b_mod[i].astype(F32)
        mod_x = (silu_c @ wm + bm).astype(dt)
        mod_c = (silu_cc @ wm + bm).astype(dt)
        shift_x, scale_x, gate_x = jnp.split(mod_x[:, None, :], 3, axis=-1)
        shift_c, scale_c, gate_c = jnp.split(mod_c, 3, axis=-1)
        hx = _rms_norm(x, norm_g[i]) * (1.0 + scale_x) + shift_x
        hc = _rms_norm(ctx, norm_g[i]) * (1.0 + scale_c) + shift_c
        if kind == 0:
            oc, ox = _rwkv7_mixer(hc, hx, rwkv_mu[j], rwkv_w_rkvg[j], rwkv_w0[j], rwkv_w1[j],
                                  rwkv_w2[j], rwkv_a0[j], rwkv_a1[j], rwkv_a2[j], rwkv_k_k[j],
                                  rwkv_k_a[j], rwkv_r_k[j], rwkv_ln_w[j], rwkv_ln_b[j],
                                  rwkv_w_out[j], need_ctx)
        elif kind == 1:
            oc, ox = _na_mixer(hc, hx, na_w_in[j], na_q_g[j], na_k_g[j], na_rpb[j],
                               na_w_out[j], need_ctx)
        else:
            oc, ox = _s5_mixer(hc, hx, s5_w_in[j], s5_lam_re[j], s5_lam_im[j], s5_log_dt[j],
                               s5_b_re[j], s5_b_im[j], s5_c_re[j], s5_c_im[j], s5_d[j],
                               s5_w_glu[j], s5_b_glu[j], s5_w_out[j], need_ctx)
        x = x + gate_x * ox
        if need_ctx:
            ctx = ctx + gate_c * oc
    return x


_drawn_inputs = setup_inputs


def setup_inputs(seed=0):
    import zlib

    import numpy as np

    out = dict(_drawn_inputs(seed))
    spreads = {}
    factors = {'norm_g': 6.587,
     'b_mod': 2.731,
     'rwkv_w1': 8.0,
     'rwkv_w2': 8.0,
     'rwkv_a0': 22.873,
     'rwkv_a1': 7.574,
     'rwkv_a2': 7.522,
     'rwkv_k_k': 47.648,
     'rwkv_k_a': 50.04,
     'rwkv_ln_w': 64.0,
     'rwkv_ln_b': 64.0,
     'na_q_g': 21.951,
     'na_k_g': 8.0,
     'na_rpb': 40.288,
     's5_lam_re': 64.0,
     's5_lam_im': 37.024,
     's5_log_dt': 50.512,
     's5_b_re': 54.064,
     's5_b_im': 52.728,
     's5_c_re': 51.64,
     's5_c_im': 51.856,
     's5_w_glu': 8.0,
     's5_b_glu': 200.0}
    for name, (base, spread) in spreads.items():
        noise = np.random.default_rng([zlib.crc32(name.encode()), seed]).standard_normal(out[name].shape)
        drawn = base * np.exp(spread * noise) if base else spread * noise
        out[name] = jnp.asarray(drawn.astype(out[name].dtype))
    for name, factor in factors.items():
        out[name] = (out[name] * factor).astype(out[name].dtype)
    return out
```

```python
import numpy as np
import concourse.bass as bass
from concourse import mybir
from contextlib import ExitStack

F32 = mybir.dt.float32
I32 = mybir.dt.int32
ALU = mybir.AluOpType
ACT = mybir.ActivationFunctionType
AXX = mybir.AxisListType.X

D = 1024
P = 128
KT = D // P
NCTX, NLAT = 256, 1024
T = NCTX + NLAT
SEGS = [(0, NCTX), (NCTX, T)]
BANK = 512
CHUNKS = [(0, 512), (512, 1024), (1024, T)]
EPS = 1e-6
GN_EPS = 64e-5
DECAY = float(np.exp(-0.5))
C = 64
NCH = T // C
W = 128
NPAR = 15
(P_MU, P_W0, P_A0, P_KK, P_KA, P_RK, P_LNW, P_LNB) = (0, 6, 8, 10, 11, 12, 13, 14)


class Arena:

    def __init__(self, tensor, cols):
        self.tensor, self.cols, self.at = tensor, cols, 0

    def take(self, *shape):
        n = int(np.prod(shape))
        assert self.at + n <= self.cols, f"arena: {self.at} + {n} > {self.cols}"
        v = self.tensor[:, self.at:self.at + n]
        self.at += n
        if len(shape) == 2:
            v = v.rearrange("p (a b) -> p a b", b=shape[1])
        if len(shape) == 3:
            v = v.rearrange("p (a b c) -> p a b c", b=shape[1], c=shape[2])
        if len(shape) == 4:
            v = v.rearrange("p (a b c d) -> p a b c d", b=shape[1], c=shape[2], d=shape[3])
        return v


class Phase:

    def __init__(self, nc):
        self.nc, self.sems, self.credits, self.stack = nc, [], [], ExitStack()

    def __enter__(self):
        return self

    def semaphore(self, name, credit=0):
        self.sems.append(self.stack.enter_context(self.nc.semaphore(name)))
        if credit:
            self.credits.append((self.sems[-1], credit))
        return self.sems[-1]

    def block(self):
        for s, credit in self.credits:
            self.nc.gpsimd.sem_inc(s, credit)
        self.region = self.nc.Block()
        return self.region.__enter__()

    def __exit__(self, *error):
        self.region.__exit__(*error)
        if error[0] is None:
            for s in self.sems:
                self.nc.gpsimd.sem_clear(s)
        self.stack.__exit__(*error)


class Ctx:
    pass


def hold(k, eng):
    eng.sem_inc(k.held, 1)


def flat(v):
    return v.rearrange("p a b -> p (a b)")


def dram_tile(ap, i):
    return ap[bass.ds(i, 1)].rearrange("o p c -> (o p) c")


def load_constants(nc, loads):
    with Phase(nc) as es:
        loaded = es.semaphore("constants_loaded")
        block = es.block()

        @block.sync
        def _(sp):
            for dst, src in loads:
                sp.dma_start(dst, src).then_inc(loaded, 16)
            sp.wait_ge(loaded, 16 * len(loads))


def modulation(nc, k, mark):
    k.arena.at = mark
    strips = k.arena.take(4, KT * P)
    cond = k.arena.take(KT, 2)
    sig = k.arena.take(KT, 2)
    n_iter = k.n_mod // 4
    with Phase(nc) as es:
        sem = lambda n, credit=0: es.semaphore(n, credit)
        cond_in, sig_done, cond_done = sem("cond_in"), sem("sig_done"), sem("cond_done")
        w_in = [sem(f"mod_w_in{u}") for u in range(4)]
        mm_done = [sem(f"mod_mm_done{u}", 1) for u in range(4)]
        ev_done = [sem(f"mod_ev_done{u}", 1) for u in range(4)]
        block = es.block()

        @block.sync
        def _(sp):
            sp.dma_start(cond, k.cond_d.rearrange("p (a b) -> p a b", b=2)).then_inc(cond_in, 16)
            with sp.Fori(0, n_iter) as i:
                for u in range(4):
                    sp.wait_ge(mm_done[u], i + 1)
                    sp.dma_start(strips[:, u, :], dram_tile(k.w_mod, i * 4 + u)).then_inc(w_in[u], 16)

        @block.scalar
        def _(act):
            act.wait_ge(cond_in, 16)
            nc.scalar.activation(sig, cond, ACT.Sigmoid).then_inc(sig_done, 1)

        @block.vector
        def _(dve):
            dve.wait_ge(sig_done, 1)
            nc.vector.tensor_tensor(cond, cond, sig, ALU.mult).then_inc(cond_done, 1)
            with dve.Fori(0, n_iter) as i:
                for u in range(4):
                    dve.wait_ge(mm_done[u], i + 2)
                    nc.vector.tensor_scalar(k.mod[:, bass.ds(i * 4 + u, 1), :].rearrange("p a b -> p (a b)"),
                                            k.ps[:, u, 0:2], k.b_mod[:, bass.ds(i * 4 + u, 1)], None,
                                            ALU.add).then_inc(ev_done[u], 1)
            dve.drain()
            for l in range(k.depth):
                for s in range(2):
                    sc = k.mod[:, l * 24 + 8:l * 24 + 16, s]
                    nc.vector.scalar_tensor_tensor(sc, sc, 1.0, k.norm_g[:, l * 8:l * 8 + 8],
                                                   ALU.add, ALU.mult)

        @block.tensor
        def _(pe):
            pe.wait_ge(cond_done, 1)
            with pe.Fori(0, n_iter) as i:
                for u in range(4):
                    pe.wait_ge(w_in[u], i * 16 + 16)
                    pe.wait_ge(ev_done[u], i + 1)
                    for c in range(KT):
                        last = nc.tensor.matmul(k.ps[:, u, 0:2], strips[:, u, c * P:(c + 1) * P], cond[:, c, :],
                                                start=(c == 0), stop=(c == KT - 1))
                    last.then_inc(mm_done[u], 1)


def norm(nc, k, layer, h, src):
    sq = k.arena.take(2, T)
    rstd = k.arena.take(T)
    with Phase(nc) as es:
        sem = lambda n: es.semaphore(n)
        x_in = [sem(f"x_in{c}") for c in range(KT)]
        sq_done, mm_done, ms_done, root_done = sem("sq_done"), sem("ss_mm"), sem("ms_done"), sem("root_done")
        scaled, final = sem("scaled"), sem("final")
        block = es.block()

        @block.sync
        def _(sp):
            for c in range(KT):
                sp.dma_start(h[:, c, :], src[c]).then_inc(x_in[c], 16)

        @block.scalar
        def _(act):
            for c in range(KT):
                act.wait_ge(x_in[c], 16)
                if c >= 2:
                    act.wait_ge(mm_done, c - 1)
                nc.scalar.activation(sq[:, c % 2, :], h[:, c, :], ACT.Square).then_inc(sq_done, 1)
            act.wait_ge(ms_done, 1)
            nc.scalar.activation(rstd, rstd, ACT.Sqrt).then_inc(root_done, 1)
            for c in range(KT):
                act.wait_ge(scaled, c + 1)
                for s, (a, b) in enumerate(SEGS):
                    nc.scalar.activation(h[:, c, a:b], h[:, c, a:b], ACT.Identity,
                                         bias=k.mod[:, layer * 24 + c, s:s + 1],
                                         scale=k.mod[:, layer * 24 + 8 + c, s:s + 1]).then_inc(final, 1)

        @block.tensor
        def _(pe):
            for c in range(KT):
                pe.wait_ge(sq_done, c + 1)
                for n, (a, b) in enumerate(CHUNKS):
                    last = nc.tensor.matmul(k.ps[:, n, 0:b - a], k.ones, sq[:, c % 2, a:b],
                                            start=(c == 0), stop=(c == KT - 1))
                last.then_inc(mm_done, 1)

        @block.vector
        def _(dve):
            dve.wait_ge(mm_done, KT)
            nc.vector.tensor_scalar(rstd, k.psf[:, 0:T], 1.0 / D, EPS, ALU.mult, ALU.add).then_inc(ms_done, 1)
            dve.wait_ge(root_done, 1)
            nc.vector.reciprocal(rstd, rstd)
            dve.drain()
            for c in range(KT):
                nc.vector.tensor_tensor(h[:, c, :], h[:, c, :], rstd, ALU.mult).then_inc(scaled, 1)


def strip_matmuls(nc, k, u, w, src):
    for n, (a, b) in enumerate(CHUNKS):
        for c in range(KT):
            last = nc.tensor.matmul(k.ps[:, 3 * u + n, 0:b - a], w[:, c * P:(c + 1) * P], src[:, c, a:b],
                                    start=(c == 0), stop=(c == KT - 1))
    return last


def acc(k, u):
    return k.psf[:, 3 * u * BANK:3 * u * BANK + T]


def dense_to_dram(nc, k, h, weights, n_strips, dst, chunked=False):
    strips, stage = k.arena.take(2, KT * P), k.arena.take(2, T)
    with Phase(nc) as es:
        sem = lambda n, credit=0: es.semaphore(n, credit)
        w_in = [sem(f"w_in{u}") for u in range(2)]
        mm_done = [sem(f"mm_done{u}", 1) for u in range(2)]
        ev_done = [sem(f"ev_done{u}", 1) for u in range(2)]
        stored = [sem(f"stored{u}", 16) for u in range(2)]
        block = es.block()

        @block.sync
        def _(sp):
            with sp.Fori(0, n_strips // 2) as i:
                for u in range(2):
                    sp.wait_ge(mm_done[u], i + 1)
                    sp.dma_start(strips[:, u, :], dram_tile(weights, i * 2 + u)).then_inc(w_in[u], 16)

        @block.tensor
        def _(pe):
            with pe.Fori(0, n_strips // 2) as i:
                for u in range(2):
                    pe.wait_ge(w_in[u], i * 16 + 16)
                    pe.wait_ge(ev_done[u], i + 1)
                    strip_matmuls(nc, k, u, strips[:, u, :], h).then_inc(mm_done[u], 1)

        @block.scalar
        def _(act):
            with act.Fori(0, n_strips // 2) as i:
                for u in range(2):
                    act.wait_ge(mm_done[u], i + 2)
                    act.wait_ge(stored[u], i * 16 + 16)
                    out, in_ = stage[:, u, :], acc(k, u)
                    if chunked:
                        out = out.rearrange("p (s j) -> p j s", s=S)
                        in_ = in_.rearrange("p (j s) -> p j s", s=S)
                    nc.scalar.copy(out, in_).then_inc(ev_done[u], 1)
                    act.wait_ge(ev_done[u], i + 2)
                    act.dma_start(dram_tile(dst, i * 2 + u), stage[:, u, :]).then_inc(stored[u], 16)
            for u in range(2):
                act.wait_ge(stored[u], n_strips // 2 * 16 + 16)


def dense_residual(nc, k, layer, o, weights, src, dst, chunked=False):
    strips, stage, xin = k.arena.take(2, KT * P), k.arena.take(2, T), k.arena.take(2, T)
    n = KT // 2
    with Phase(nc) as es:
        sem = lambda n, credit=0: es.semaphore(n, credit)
        w_in = [sem(f"w_in{u}") for u in range(2)]
        x_in = [sem(f"x_in{u}") for u in range(2)]
        mm_done = [sem(f"mm_done{u}", 1) for u in range(2)]
        ev_done = [sem(f"ev_done{u}", 1) for u in range(2)]
        stored = [sem(f"stored{u}", 16) for u in range(2)]
        block = es.block()

        @block.sync
        def _(sp):
            with sp.Fori(0, n) as i:
                for u in range(2):
                    sp.wait_ge(mm_done[u], i + 1)
                    sp.dma_start(strips[:, u, :], dram_tile(weights, i * 2 + u)).then_inc(w_in[u], 16)
                    sp.wait_ge(ev_done[u], i + 1)
                    sp.dma_start(xin[:, u, :], dram_tile(src, i * 2 + u)).then_inc(x_in[u], 16)

        @block.tensor
        def _(pe):
            with pe.Fori(0, n) as i:
                for u in range(2):
                    pe.wait_ge(w_in[u], i * 16 + 16)
                    pe.wait_ge(ev_done[u], i + 1)
                    strip_matmuls(nc, k, u, strips[:, u, :], o).then_inc(mm_done[u], 1)

        @block.vector
        def _(dve):
            with dve.Fori(0, n) as i:
                for u in range(2):
                    dve.wait_ge(mm_done[u], i + 2)
                    dve.wait_ge(x_in[u], i * 16 + 16)
                    dve.wait_ge(stored[u], i * 16 + 16)
                    for s, (a, b) in enumerate(SEGS):
                        gate = k.mod[:, bass.ds(i * 2 + (layer * 24 + 16 + u), 1), s]
                        out, prod, x = stage[:, u, a:b], acc(k, u)[:, a:b], xin[:, u, a:b]
                        if chunked:
                            out, x = (v.rearrange("p (j s) -> p j s", s=S) for v in (out, x))
                            prod = acc(k, u).rearrange("p (s j) -> p j s", s=S)[:, a // S:b // S, :]
                        last = nc.vector.scalar_tensor_tensor(out, prod, gate, x, ALU.mult, ALU.add)
                    last.then_inc(ev_done[u], 1)

        @block.scalar
        def _(act):
            with act.Fori(0, n) as i:
                for u in range(2):
                    act.wait_ge(ev_done[u], i + 2)
                    act.dma_start(dram_tile(dst, i * 2 + u), stage[:, u, :]).then_inc(stored[u], 16)
            for u in range(2):
                act.wait_ge(stored[u], n * 16 + 16)


GRID, ROWS, KH, KW = 64, NLAT // 64, 8, 16
NA_BIAS = 15 * GRID


def na_windows():
    units = []
    for r in range(ROWS):
        r0 = min(max(r - KH // 2, 0), ROWS - KH)
        units.append((NCTX + r * GRID, NCTX + r0 * GRID, (r0 - r + 7) * GRID))
    return units + [(q * GRID, None, 0) for q in range(NCTX // GRID)]


def na_attention(nc, k, o, qkvz):
    take = k.arena.take
    raw, bias = take(4, T), take(NA_BIAS)
    sq, rstd = take(T), take(T)
    v_even, v_odd = take(10, P), take(7, P)
    s_sb, p_sb = take(2, 768), take(768)
    pt = take(2, 768)
    mx, sm = take(2, 1), take(2, 1)
    units = na_windows()
    NU = len(units)
    blocks = [(None, list(range(2)))]
    qg, kg = k.na_g[:, 0:1], k.na_g[:, 1:2]

    def value_blocks(key):
        ctx = [v_even[:, b, :] for b in range(2)]
        if key is None:
            return ctx
        b = (key - NCTX) // GRID
        return [(v_odd if b % 2 else v_even[:, 2:10, :])[:, b // 2 + n, :] for n in range(4)] + ctx

    with Phase(nc) as es:
        sem = lambda n, credit=0: es.semaphore(n, credit)
        tile_in, sq_ready, ms_mm, ms_ev, root, normed = (sem(x) for x in
            ("na_tile_in", "na_sq_ready", "na_ms_mm", "na_ms_ev", "na_root", "na_normed"))
        vt_mm, vt_ev, tile_done = sem("na_vt_mm"), sem("na_vt_ev"), sem("na_tile_done", 1)
        s_mm, s_ev, s_ctx, s_max, p_exp, p_ready, o_mm = (sem("na_" + x) for x in
            ("s_mm", "s_ev", "s_ctx", "s_max", "p_exp", "p_ready", "o_mm"))
        pt_mm, pt_ev, o_ev = (sem("na_" + x, 1) for x in ("pt_mm", "pt_ev", "o_ev"))
        gate_sig = sem("na_gate_sig")
        block = es.block()

        @block.sync
        def _(sp):
            with sp.Fori(0, KT) as e:
                sp.wait_ge(tile_done, e * 2 + 1)
                for n in range(4):
                    sp.dma_start(raw[:, n, :], dram_tile(qkvz, e + n * KT)).then_inc(tile_in, 16)
                sp.dma_start(bias, dram_tile(k.na_bias, e)).then_inc(tile_in, 16)

        @block.tensor
        def _(pe):
            with pe.Fori(0, KT) as e:
                for n in range(2):
                    pe.wait_ge(sq_ready, e * 2 + n + 1)
                    for m, (a, b) in enumerate(CHUNKS):
                        last = nc.tensor.matmul(k.ps[:, 3 * n + m, 0:b - a], k.head_ones, sq[:, a:b],
                                                start=True, stop=True)
                    last.then_inc(ms_mm, 1)
                for n in range(17):
                    t0 = n * P if n < 10 else NCTX + GRID + (n - 10) * P
                    if n >= 2:
                        pe.wait_ge(vt_ev, e * 17 + n - 1)
                    if n == 0:
                        pe.wait_ge(tile_in, e * 80 + 80)
                        pe.wait_ge(o_ev, e * NU + 1)
                    nc.tensor.transpose(k.ps[:, 6 + n % 2, 0:P], raw[:, 2, t0:t0 + P], k.ident).then_inc(vt_mm, 1)
                pe.wait_ge(vt_ev, e * 17 + 17)
                pe.wait_ge(normed, e * 2 + 2)

                def scores(n):
                    q, key, _ = units[n]
                    if n >= 2:
                        pe.wait_ge(s_ev, e * ROWS + min(n - 1, ROWS))
                        pe.wait_ge(s_ctx, e * NU + n - 1)
                        hold(k, pe)
                    for h in range(2):
                        hp = slice(64 * h, 64 * h + 64)
                        if key is not None:
                            nc.tensor.matmul(k.ps[hp, 2 * (n % 2), :], raw[hp, 0, q:q + 64], raw[hp, 1, key:key + 512],
                                             start=True, stop=True)
                        last = nc.tensor.matmul(k.ps[hp, 2 * (n % 2) + 1, 0:NCTX], raw[hp, 0, q:q + 64],
                                                raw[hp, 1, 0:NCTX], start=True, stop=True)
                    last.then_inc(s_mm, 1)

                def attend(n):
                    key = units[n][1]
                    vb = value_blocks(key)
                    off = 0 if key is not None else 512
                    pe.wait_ge(p_ready, e * NU + n + 1)
                    if n >= 1:
                        pe.wait_ge(pt_ev, e * NU + n + 1)
                    for m in range(len(vb)):
                        last = nc.tensor.transpose(k.psf[:, 4 * BANK + m * P:4 * BANK + (m + 1) * P],
                                                   p_sb[:, off + m * P:off + (m + 1) * P], k.ident)
                    last.then_inc(pt_mm, 1)
                    if n + 2 < NU:
                        scores(n + 2)
                    pe.wait_ge(pt_ev, e * NU + n + 2)
                    if n >= 2:
                        pe.wait_ge(o_ev, e * NU + n)
                    for m, v in enumerate(vb):
                        last = nc.tensor.matmul(k.ps[:, 6 + n % 2, 0:P], v, pt[:, n % 2, m * P:(m + 1) * P],
                                                start=(m == 0), stop=(m == len(vb) - 1))
                    last.then_inc(o_mm, 1)

                pe.wait_ge(ms_ev, e * 2 + 2)
                hold(k, pe)
                scores(0)
                scores(1)
                for n in range(NU):
                    attend(n)
                pe.drain().then_inc(tile_done, 1)

        @block.scalar
        def _(act):
            with act.Fori(0, KT) as e:
                act.wait_ge(tile_in, e * 80 + 80)
                act.wait_ge(o_ev, e * NU + 1)
                for n in range(2):
                    if n == 1:
                        act.wait_ge(ms_mm, e * 2 + 1)
                    nc.scalar.activation(sq, raw[:, n, :], ACT.Square).then_inc(sq_ready, 1)
                    act.wait_ge(ms_ev, e * 2 + n + 1)
                    nc.scalar.activation(rstd, rstd, ACT.Sqrt).then_inc(root, 1)
                act.wait_ge(normed, e * 2 + 2)
                nc.scalar.activation(rstd, raw[:, 3, :], ACT.Sigmoid).then_inc(gate_sig, 1)
                for n in range(17):
                    dst = v_even[:, n, :] if n < 10 else v_odd[:, n - 10, :]
                    act.wait_ge(vt_mm, e * 17 + n + 1)
                    nc.scalar.copy(dst, k.ps[:, 6 + n % 2, 0:P]).then_inc(vt_ev, 1)
                for n in range(NU):
                    key = units[n][1]
                    off = 0 if key is not None else 512
                    act.wait_ge(s_mm, e * NU + n + 1)
                    nc.scalar.mul(s_sb[:, n % 2, 512:768], k.ps[:, 2 * (n % 2) + 1, 0:NCTX], NA_SCALE).then_inc(s_ctx, 1)
                    act.wait_ge(s_max, e * NU + n + 1)
                    if n >= 1:
                        act.wait_ge(pt_mm, e * NU + n + 1)
                    nc.scalar.activation(p_sb[:, off:768], s_sb[:, n % 2, off:768], ACT.Exp, bias=mx[:, n % 2, :],
                                         accum_out=sm[:, n % 2, :]).then_inc(p_exp, 1)
                    act.wait_ge(pt_mm, e * NU + n + 2)
                    nb = 768 - off
                    if n >= 2:
                        act.wait_ge(o_mm, e * NU + n - 1)
                    nc.scalar.copy(pt[:, n % 2, 0:nb], k.psf[:, 4 * BANK:4 * BANK + nb]).then_inc(pt_ev, 1)

        @block.vector
        def _(dve):
            with dve.Fori(0, KT) as e:
                for n, g in enumerate((qg, kg)):
                    dve.wait_ge(ms_mm, e * 2 + n + 1)
                    nc.vector.tensor_scalar(rstd, k.psf[:, 3 * n * BANK:3 * n * BANK + T], 1.0 / 64, EPS,
                                            ALU.mult, ALU.add).then_inc(ms_ev, 1)
                    dve.wait_ge(root, e * 2 + n + 1)
                    nc.vector.reciprocal(rstd, rstd)
                    dve.drain()
                    nc.vector.scalar_tensor_tensor(raw[:, n, :], raw[:, n, :], g, rstd, ALU.mult, ALU.mult)
                    dve.drain().then_inc(normed, 1)
                dve.wait_ge(gate_sig, e + 1)
                nc.vector.tensor_tensor(raw[:, 3, :], raw[:, 3, :], rstd, ALU.mult)
                dve.drain()

                def outputs(n):
                    q = units[n][0]
                    dve.wait_ge(o_mm, e * NU + n + 1)
                    for h in range(2):
                        hp = slice(64 * h, 64 * h + 64)
                        last = nc.vector.tensor_tensor(o[hp, bass.ds(e, 1), q:q + 64].rearrange("p a b -> p (a b)"),
                                                       k.ps[hp, 6 + n % 2, 64 * h:64 * h + 64], raw[hp, 3, q:q + 64], ALU.mult)
                    last.then_inc(o_ev, 1)

                for n in range(NU):
                    key, bcol = units[n][1:]
                    off = 0 if key is not None else 512
                    dve.wait_ge(s_mm, e * NU + n + 1)
                    if key is not None:
                        nc.vector.scalar_tensor_tensor(s_sb[:, n % 2, 0:512], k.ps[:, 2 * (n % 2), :], NA_SCALE,
                                                       bias[:, bcol:bcol + 512], ALU.mult, ALU.add).then_inc(s_ev, 1)
                        dve.drain()
                    dve.wait_ge(s_ctx, e * NU + n + 1)
                    if n >= 2:
                        dve.wait_ge(p_exp, e * NU + n - 1)
                    nc.vector.reduce_max(mx[:, n % 2, :], s_sb[:, n % 2, off:768], AXX)
                    dve.drain()
                    nc.vector.tensor_scalar(mx[:, n % 2, :], mx[:, n % 2, :], -1.0, None, ALU.mult).then_inc(s_max, 1)
                    if n >= 1:
                        outputs(n - 1)
                    dve.wait_ge(p_exp, e * NU + n + 1)
                    nc.vector.reciprocal(sm[:, n % 2, :], sm[:, n % 2, :])
                    dve.drain()
                    nc.vector.tensor_scalar(p_sb[:, off:768], p_sb[:, off:768], sm[:, n % 2, :], None,
                                            ALU.mult).then_inc(p_ready, 1)
                outputs(NU - 1)
                dve.drain().then_inc(tile_done, 1)


NA_SCALE = 64 ** -0.5


S = 8
NJ = T // S
JC = NCTX // S
G, GP, NS = 64, 32, 64
TWO_PI = 2 * np.pi
PI_A, PI_B = 6.28125, float(np.float32(TWO_PI - 6.28125) // 2 ** -21 * 2 ** -21)
PI_C = float(TWO_PI - PI_A - PI_B)




def s5_discretise(nc, k, s5):
    take = k.arena.take
    N = 2 * GP
    t = [take(N) for _ in range(12)]
    (lr, li, step, th, y, em, mag, sn, cs, hs, den, tmp) = t
    turns = take(N)
    qr, qi, ar1, ai = (take(N) for _ in range(4))
    V = nc.vector
    with Phase(nc) as es:
        sem = lambda n: es.semaphore(n)
        par_in, stepped, angle, waves, disc = (sem("s5_" + x) for x in ("par_in", "stepped", "angle", "waves", "disc"))
        block = es.block()

        @block.sync
        def _(sp):
            for dst, src in ((lr, "s5_lr"), (li, "s5_li"), (step, "s5_dt"), (flat(s5.br), "s5_br"),
                             (flat(s5.bi), "s5_bi"), (flat(s5.cr), "s5_cr"), (flat(s5.ci), "s5_ci"), (s5.dsk, "s5_dsk")):
                sp.dma_start(dst, k.A[src]).then_inc(par_in, 16)

        @block.scalar
        def _(act):
            act.wait_ge(par_in, 128)
            nc.scalar.activation(step, step, ACT.Exp).then_inc(stepped, 1)
            act.wait_ge(angle, 1)
            nc.scalar.activation(mag, y, ACT.Exp).then_inc(waves, 1)
            nc.scalar.activation(sn, th, ACT.Sin).then_inc(waves, 1)
            nc.scalar.activation(cs, tmp, ACT.Sin).then_inc(waves, 1)
            nc.scalar.activation(hs, th, ACT.Sin, scale=0.5).then_inc(waves, 1)

        @block.vector
        def _(dve):
            def tt(out, a, b, op):
                V.tensor_tensor(out, a, b, op)
                dve.drain()

            def ts(out, a, s1, s2, o1, o2=ALU.bypass):
                V.tensor_scalar(out, a, s1, s2, o1, o2)
                dve.drain()

            def stt(out, a, s, b, o1, o2):
                V.scalar_tensor_tensor(out, a, s, b, o1, o2)
                dve.drain()

            def wrap(x, scratch):
                ts(scratch, x, float(np.pi), TWO_PI, ALU.is_gt, ALU.mult)
                tt(x, x, scratch, ALU.subtract)
                ts(scratch, x, -float(np.pi), TWO_PI, ALU.is_lt, ALU.mult)
                tt(x, x, scratch, ALU.add)

            dve.wait_ge(stepped, 1)
            tt(y, lr, step, ALU.mult)
            tt(th, li, step, ALU.mult)
            ts(tmp, th, 1 / TWO_PI, None, ALU.mult)
            V.tensor_copy(turns.bitcast(I32), tmp)
            dve.drain()
            V.tensor_copy(tmp, turns.bitcast(I32))
            dve.drain()
            for part in (PI_A, PI_B, PI_C):
                stt(th, tmp, -part, th, ALU.mult, ALU.add)
            wrap(th, tmp)
            ts(tmp, th, float(np.pi / 2), None, ALU.add)
            wrap(tmp, den)
            lim = float(np.float32(3.1415925))
            ts(th, th, lim, -lim, ALU.min, ALU.max)
            V.tensor_scalar(tmp, tmp, lim, -lim, ALU.min, ALU.max).then_inc(angle, 1)
            V.memset(em, 1.0)
            dve.drain()
            for n in range(9, 1, -1):
                tt(em, em, y, ALU.mult)
                ts(em, em, 1.0 / n, 1.0, ALU.mult, ALU.add)
            tt(em, em, y, ALU.mult)
            dve.wait_ge(waves, 4)
            ts(mag, mag, -1.0, None, ALU.add)
            tt(den, y, y, ALU.mult)
            ts(turns.bitcast(I32), den, 0.25, None, ALU.is_ge)
            V.copy_predicated(em, turns.bitcast(I32), mag)
            dve.drain()
            ts(mag, em, 1.0, None, ALU.add)
            tt(ai, mag, sn, ALU.mult)
            tt(hs, hs, hs, ALU.mult)
            tt(ar1, em, cs, ALU.mult)
            stt(ar1, hs, -2.0, ar1, ALU.mult, ALU.add)
            tt(den, lr, lr, ALU.mult)
            tt(tmp, li, li, ALU.mult)
            tt(den, den, tmp, ALU.add)
            V.reciprocal(den, den)
            dve.drain()
            tt(qr, ar1, lr, ALU.mult)
            tt(tmp, ai, li, ALU.mult)
            tt(qr, qr, tmp, ALU.add)
            tt(qr, qr, den, ALU.mult)
            tt(qi, ai, lr, ALU.mult)
            tt(tmp, ar1, li, ALU.mult)
            tt(qi, qi, tmp, ALU.subtract)
            tt(qi, qi, den, ALU.mult)
            V.memset(s5.AR[:, 0, :], 1.0)
            V.memset(s5.AI[:, 0, :], 0.0)
            ts(s5.AR[:, 1, :], ar1, 1.0, None, ALU.add)
            V.tensor_copy(s5.AI[:, 1, :], ai)
            dve.drain()
            for n in range(2, S + 1):
                a, b = n // 2, n - n // 2
                tt(s5.AR[:, n, :], s5.AR[:, a, :], s5.AR[:, b, :], ALU.mult)
                tt(tmp, s5.AI[:, a, :], s5.AI[:, b, :], ALU.mult)
                tt(s5.AR[:, n, :], s5.AR[:, n, :], tmp, ALU.subtract)
                tt(s5.AI[:, n, :], s5.AR[:, a, :], s5.AI[:, b, :], ALU.mult)
                tt(tmp, s5.AI[:, a, :], s5.AR[:, b, :], ALU.mult)
                tt(s5.AI[:, n, :], s5.AI[:, n, :], tmp, ALU.add)
            V.tensor_copy(s5.coef[:, 0, 0, :], s5.AR[:, S, :])
            V.tensor_copy(s5.coef[:, 0, 1, :], s5.AR[:, S, :])
            V.tensor_copy(s5.coef[:, 1, 0, :], s5.AI[:, S, :])
            ts(s5.coef[:, 1, 1, :], s5.AI[:, S, :], -1.0, None, ALU.mult)
            for d in range(2):
                q_r = qr[:, d * GP:(d + 1) * GP].unsqueeze(2).to_broadcast([P, GP, 16])
                q_i = qi[:, d * GP:(d + 1) * GP].unsqueeze(2).to_broadcast([P, GP, 16])
                bbr, bbi = s5.bb[:, 0, d * GP:(d + 1) * GP, :], s5.bb[:, 1, d * GP:(d + 1) * GP, :]
                tt(bbr, s5.br, q_r, ALU.mult)
                tt(s5.tmpb, s5.bi, q_i, ALU.mult)
                tt(bbr, bbr, s5.tmpb, ALU.subtract)
                tt(bbi, s5.bi, q_r, ALU.mult)
                tt(s5.tmpb, s5.br, q_i, ALU.mult)
                tt(bbi, bbi, s5.tmpb, ALU.add)


def s5_matrices(nc, k, s5, u_d):
    take = k.arena.take
    ca, zb, zbt = take(2, 4, P), take(2, 4, P), take(2, 4, P)
    prod = take(2, P)
    prod2 = take(2, P)
    carried = take(2, 4, 16)
    kst = take(2, BANK)
    upair = take(2, 2, NJ)
    zero = take(P)
    V, SC = nc.vector, nc.scalar
    with Phase(nc) as es:
        sem = lambda n, credit=0: es.semaphore(n, credit)
        u_in, zeroed, zero_out = sem("s5_u_in"), sem("s5_zeroed"), sem("s5_zero_out")
        par = [sem(f"s5_pair_par{u}") for u in range(2)]
        ca_ready = [sem(f"s5_ca_ready{u}") for u in range(2)]
        zb_ready = [sem(f"s5_zb_ready{u}", 1) for u in range(2)]
        ca_out = [sem(f"s5_ca_out{u}", 16) for u in range(2)]
        k_mm = [sem(f"s5_k_mm{u}", 1) for u in range(2)]
        k_ev = [sem(f"s5_k_ev{u}", 1) for u in range(2)]
        k_out = [sem(f"s5_k_out{u}", 32) for u in range(2)]
        zt_mm = [sem(f"s5_zt_mm{u}", 1) for u in range(2)]
        zt_ev = [sem(f"s5_zt_ev{u}", 1) for u in range(2)]
        z_mm = [sem(f"s5_z_mm{u}", 1) for u in range(2)]
        z_ev = [sem(f"s5_z_ev{u}", 1) for u in range(2)]
        block = es.block()

        @block.sync
        def _(sp):
            for s in range(S):
                sp.dma_start(s5.u[16 * s:16 * s + 16, :, :],
                             u_d[0:KT].rearrange("k q t -> (k q) t").rearrange("(g c) (s j) -> s c g j", c=16, s=S)[s]).then_inc(u_in, 16)
            sp.wait_ge(zeroed, 1)
            for d in range(2):
                side = s5.kd[d][:, :, :, d * P:(d + 1) * P]
                sp.dma_start(side.rearrange("q h c l -> (q h c) l").rearrange("(a b) l -> b a l", b=P),
                             zero.unsqueeze(1).to_broadcast([P, GP * 2 * 16 // P, P])).then_inc(zero_out, 16)
            with sp.Fori(0, GP // 2) as i:
                for u in range(2):
                    sp.wait_ge(ca_ready[u], i + 1)
                    sp.dma_start(dram_tile(s5.cad, i * 2 + u), ca[:, u].rearrange("p a b -> p (a b)")).then_inc(ca_out[u], 16)
                    sp.wait_ge(k_ev[u], i + 2)
                    for d in range(2):
                        sp.dma_start(s5.kd[d][bass.ds(i * 2 + u, 1), :, :, (1 - d) * P:(2 - d) * P]
                                     .rearrange("q h c l -> (q c) h l"),
                                     kst[0:16, u, d * 2 * P:(d + 1) * 2 * P].rearrange("c (h l) -> c h l", h=2)).then_inc(k_out[u], 16)
            for u in range(2):
                sp.wait_ge(ca_out[u], 16 * GP // 2 + 16)
                sp.wait_ge(k_out[u], 32 * GP // 2 + 32)
            sp.wait_ge(zero_out, 32)

        def row(v, n):
            return v.unsqueeze(1).to_broadcast([P, n, 16])

        def lag(v):
            return v.unsqueeze(2).to_broadcast([P, v.shape[1], 16])

        @block.vector
        def _(dve):
            V.memset(zero, 0.0).then_inc(zeroed, 1)
            with dve.Fori(0, GP // 2) as i:
                for u in range(2):
                    dve.wait_ge(par[u], i + 1)
                    dve.wait_ge(ca_out[u], i * 16 + 16)
                    dve.wait_ge(k_mm[u], i + 1)
                    for d in range(2):
                        pr = s5.pw[:, u, d, 0, :]
                        pi = s5.pw[:, u, d, 1, :]
                        e_r, e_i = (pr[:, 1:9], pi[:, 1:9]) if d == 0 else (pr[:, 8:0:-1], pi[:, 8:0:-1])
                        cr, ci = row(s5.cpair[:, u, 0, :], S), row(s5.cpair[:, u, 1, :], S)
                        o_r = ca[:, u, 2 * d, :].rearrange("p (s c) -> p s c", c=16)
                        o_i = ca[:, u, 2 * d + 1, :].rearrange("p (s c) -> p s c", c=16)
                        t0 = prod[:, 0, :].rearrange("p (s c) -> p s c", c=16)
                        t1 = prod[:, 1, :].rearrange("p (s c) -> p s c", c=16)
                        t2 = prod2[:, 0, :].rearrange("p (s c) -> p s c", c=16)
                        t3 = prod2[:, 1, :].rearrange("p (s c) -> p s c", c=16)
                        V.tensor_tensor(t0, cr, lag(e_r), ALU.mult)
                        V.tensor_tensor(t1, ci, lag(e_i), ALU.mult)
                        V.tensor_tensor(t2, cr, lag(e_i), ALU.mult)
                        V.tensor_tensor(t3, ci, lag(e_r), ALU.mult)
                        dve.drain()
                        V.tensor_tensor(o_r, t0, t1, ALU.subtract)
                        V.scalar_tensor_tensor(o_i, t2, -1.0, t3, ALU.mult, ALU.subtract)
                        dve.drain()
                        e_r, e_i = (pr[:, 0:8], pi[:, 0:8]) if d == 0 else (pr[:, 7::-1], pi[:, 7::-1])
                        o_r = s5.cl[:, u, 2 * d, :].rearrange("p (s c) -> p s c", c=16)
                        o_i = s5.cl[:, u, 2 * d + 1, :].rearrange("p (s c) -> p s c", c=16)
                        V.tensor_tensor(t0, cr, lag(e_r), ALU.mult)
                        V.tensor_tensor(t1, ci, lag(e_i), ALU.mult)
                        V.tensor_tensor(t2, cr, lag(e_i), ALU.mult)
                        V.tensor_tensor(t3, ci, lag(e_r), ALU.mult)
                        dve.drain()
                        V.tensor_tensor(o_r, t0, t1, ALU.subtract)
                        V.scalar_tensor_tensor(o_i, t2, -1.0, t3, ALU.mult, ALU.subtract)
                        dve.drain()
                    dve.nop().then_inc(ca_ready[u], 1)
                    dve.wait_ge(zt_mm[u], i + 1)
                    for d in range(2):
                        pr = s5.pw[:, u, d, 0, :]
                        pi = s5.pw[:, u, d, 1, :]
                        e_r, e_i = (pr[:, 7::-1], pi[:, 7::-1]) if d == 0 else (pr[:, 0:8], pi[:, 0:8])
                        br, bi = row(carried[:, u, 2 * d, :], S), row(carried[:, u, 2 * d + 1, :], S)
                        o_r = zb[:, u, 2 * d, :].rearrange("p (s c) -> p s c", c=16)
                        o_i = zb[:, u, 2 * d + 1, :].rearrange("p (s c) -> p s c", c=16)
                        t0 = prod[:, 0, :].rearrange("p (s c) -> p s c", c=16)
                        t1 = prod[:, 1, :].rearrange("p (s c) -> p s c", c=16)
                        t2 = prod2[:, 0, :].rearrange("p (s c) -> p s c", c=16)
                        t3 = prod2[:, 1, :].rearrange("p (s c) -> p s c", c=16)
                        V.tensor_tensor(t0, br, lag(e_r), ALU.mult)
                        V.tensor_tensor(t1, bi, lag(e_i), ALU.mult)
                        V.tensor_tensor(t2, br, lag(e_i), ALU.mult)
                        V.tensor_tensor(t3, bi, lag(e_r), ALU.mult)
                        dve.drain()
                        V.tensor_tensor(o_r, t0, t1, ALU.subtract)
                        V.tensor_tensor(o_i, t2, t3, ALU.add)
                        dve.drain()
                    dve.nop().then_inc(zb_ready[u], 1)

        @block.scalar
        def _(act):
            def pair_parameters(i, u):
                gp = i * 2 + u
                for d in range(2):
                    for r in range(2):
                        SC.copy(carried[:, u, 2 * d + r, :], s5.bb[:, r, bass.ds(gp + d * GP, 1), :].rearrange("p a b -> p (a b)"))
                        SC.copy(s5.pw[:, u, d, r, :], (s5.AR, s5.AI)[r][:, :, bass.ds(gp + d * GP, 1)].rearrange("p a b -> p (a b)"))
                SC.copy(s5.cpair[:, u, 0, :], s5.cr[:, bass.ds(gp, 1), :].rearrange("p a b -> p (a b)"))
                SC.copy(s5.cpair[:, u, 1, :], s5.ci[:, bass.ds(gp, 1), :].rearrange("p a b -> p (a b)"))
                SC.copy(upair[:, u], s5.u[:, bass.ds(gp * 2, 2), :])
                act.drain().then_inc(par[u], 1)

            act.wait_ge(u_in, 16 * S)
            hold(k, act)
            with act.Fori(0, GP // 2) as i:
                for u in range(2):
                    act.wait_ge(zb_ready[u], i + 1)
                    act.wait_ge(k_mm[u], i + 1)
                    act.wait_ge(z_mm[u], i + 1)
                    hold(k, act)
                    pair_parameters(i, u)
                for u in range(2):
                    gp = i * 2 + u
                    act.wait_ge(k_mm[u], i + 2)
                    act.wait_ge(k_out[u], i * 32 + 32)
                    for g in range(2):
                        last = SC.copy(kst[0:16, u, :].rearrange("p (d h l) -> p d h l", d=2, h=2)[:, :, g, :],
                                       k.ps[0:16, 4 * u + g, 0:2 * P].rearrange("p (d l) -> p d l", d=2))
                    last.then_inc(k_ev[u], 1)
                    act.wait_ge(zt_mm[u], i + 2)
                    SC.copy(zbt[:, u, :, :].rearrange("p a b -> p (a b)"), k.ps[:, 4 * u + 1, :]).then_inc(zt_ev[u], 1)
                    act.wait_ge(z_mm[u], i + 2)
                    zf = k.ps[:, 4 * u + 2, 0:2 * NJ].rearrange("p (r j) -> p r j", r=2)
                    zr = k.ps[:, 4 * u + 3, 0:2 * NJ].rearrange("p (r j) -> p r j", r=2)
                    hold(k, act)
                    SC.copy(s5.X[:, :, bass.ds(gp, 1), 1:NJ + 1].rearrange("p r g j -> p r (g j)"), zf)
                    SC.copy(s5.X[:, :, bass.ds(gp + GP, 1), 1:JC + 1].rearrange("p r g j -> p r (g j)"), zr[:, :, JC - 1::-1])
                    SC.copy(s5.X[:, :, bass.ds(gp + GP, 1), JC + 1:NJ + 1].rearrange("p r g j -> p r (g j)"),
                            zr[:, :, NJ - 1:JC - 1:-1])
                    act.drain().then_inc(z_ev[u], 1)

        @block.tensor
        def _(pe):
            pe.wait_ge(u_in, 16 * S)
            with pe.Fori(0, GP // 2) as i:
                for u in range(2):
                    gp = i * 2 + u
                    pe.wait_ge(ca_ready[u], i + 1)
                    pe.wait_ge(k_ev[u], i + 1)
                    pe.wait_ge(zt_ev[u], i + 1)
                    hold(k, pe)
                    for d in range(2):
                        for g in range(2):
                            hp = slice(64 * g, 64 * g + 64)
                            for r in range(2):
                                last = nc.tensor.matmul(k.ps[0:16, 4 * u + g, d * P:(d + 1) * P],
                                                        carried[hp, u, 2 * d + r, :], s5.cl[hp, u, 2 * d + r, :],
                                                        start=(r == 0), stop=(r == 1))
                    last.then_inc(k_mm[u], 1)
                    pe.wait_ge(zb_ready[u], i + 2)
                    pe.wait_ge(k_ev[u], i + 2)
                    for q in range(4):
                        last = nc.tensor.transpose(k.ps[:, 4 * u + 1, q * P:(q + 1) * P], zb[:, u, q, :], k.ident)
                    last.then_inc(zt_mm[u], 1)
                    pe.wait_ge(zt_ev[u], i + 2)
                    pe.wait_ge(z_ev[u], i + 1)
                    hold(k, pe)
                    for d in range(2):
                        for r in range(2):
                            for g in range(2):
                                last = nc.tensor.matmul(
                                    k.ps[64 * g:64 * g + 64, 4 * u + 2 + d, r * NJ:(r + 1) * NJ],
                                    zbt[:, u, 2 * d + r, 64 * g:64 * g + 64],
                                    upair[:, u, g, :], start=True, stop=True)
                    last.then_inc(z_mm[u], 1)


def s5_scan(nc, k, s5):
    term = k.arena.take(4, 2 * GP)
    sw = k.arena.take(2, 2 * GP)
    V = nc.vector
    with Phase(nc) as es:
        t_in = es.semaphore("s5_toeplitz_in")
        block = es.block()

        @block.sync
        def _(sp):
            for d in range(2):
                for s in range(S):
                    at = (S - s if d == 0 else S - 1 - s) * 16
                    sp.dma_start(s5.T[16 * s:16 * s + 16, d],
                                 s5.kd[d][:, :, :, at:at + P].rearrange("q h c l -> c (q h) l")).then_inc(t_in, 16)
            sp.wait_ge(t_in, 16 * 2 * S)

        @block.vector
        def _(dve):
            V.memset(s5.X[:, :, :, 0:1], 0.0)
            dve.drain()
            with dve.Fori(0, NJ) as i:
                prev = s5.X[:, :, :, bass.ds(i, 1)].rearrange("p r g j -> p r (g j)")
                nxt = s5.X[:, :, :, bass.ds(i + 1, 1)].rearrange("p r g j -> p r (g j)")
                V.tensor_tensor(term[:, 0:2, :], prev, s5.coef[:, 0, :, :], ALU.mult)
                V.tensor_tensor(term[:, 3:1:-1, :], prev, s5.coef[:, 1, :, :], ALU.mult)
                dve.drain()
                V.tensor_tensor(sw, term[:, 0:2, :], term[:, 2:4, :], ALU.add)
                dve.drain()
                V.tensor_tensor(nxt, nxt, sw, ALU.add)
                dve.drain()


def s5_outputs(nc, k, s5, yd):
    take = k.arena.take
    cas, tsum = take(2, 4 * P), take(2, 2 * P)
    xp = take(2, 4, NJ)
    yst = take(2, 2, NJ)
    dpair = take(2, 2)
    V, SC = nc.vector, nc.scalar
    with Phase(nc) as es:
        sem = lambda n, credit=0: es.semaphore(n, credit)
        ca_in = [sem(f"s5_ca_in{u}") for u in range(2)]
        t_ready = [sem(f"s5_t_ready{u}") for u in range(2)]
        x_ready = [sem(f"s5_x_ready{u}") for u in range(2)]
        y_mm = [sem(f"s5_y_mm{u}", 1) for u in range(2)]
        y_ev = [sem(f"s5_y_ev{u}", 1) for u in range(2)]
        y_act = [sem(f"s5_y_act{u}") for u in range(2)]
        y_out = [sem(f"s5_y_out{u}", 16) for u in range(2)]
        block = es.block()

        @block.sync
        def _(sp):
            with sp.Fori(0, GP // 2) as i:
                for u in range(2):
                    sp.wait_ge(y_mm[u], i + 1)
                    sp.dma_start(cas[:, u, :], dram_tile(s5.cad, i * 2 + u)).then_inc(ca_in[u], 16)

        @block.vector
        def _(dve):
            with dve.Fori(0, GP // 2) as i:
                for u in range(2):
                    gp = i * 2 + u
                    dve.wait_ge(y_mm[u], i + 1)
                    V.tensor_tensor(tsum[:, u, :], s5.T[:, 0, bass.ds(gp * 2, 2), :].rearrange("p a b -> p (a b)"),
                                    s5.T[:, 1, bass.ds(gp * 2, 2), :].rearrange("p a b -> p (a b)"), ALU.add).then_inc(t_ready[u], 1)
                for u in range(2):
                    gp = i * 2 + u
                    dve.wait_ge(y_mm[u], i + 2)
                    dve.wait_ge(y_out[u], i * 16 + 16)
                    for g in range(2):
                        last = V.scalar_tensor_tensor(yst[:, u, g, :], s5.u[:, bass.ds(gp * 2 + g, 1), :].rearrange("p a b -> p (a b)"),
                                                      s5.dsk[:, bass.ds(gp * 2 + g, 1)], k.ps[:, 2 * u + g, 0:NJ],
                                                      ALU.mult, ALU.add)
                    last.then_inc(y_ev[u], 1)

        @block.scalar
        def _(act):
            with act.Fori(0, GP // 2) as i:
                for u in range(2):
                    gp = i * 2 + u
                    act.wait_ge(y_mm[u], i + 1)
                    hold(k, act)
                    SC.copy(xp[:, u, 0:2, :], s5.X[:, :, bass.ds(gp, 1), 0:NJ].rearrange("p r g j -> p r (g j)"))
                    SC.copy(xp[:, u, 2:4, JC - 1::-1], s5.X[:, :, bass.ds(gp + GP, 1), 0:JC].rearrange("p r g j -> p r (g j)"))
                    SC.copy(xp[:, u, 2:4, NJ - 1:JC - 1:-1], s5.X[:, :, bass.ds(gp + GP, 1), JC:NJ].rearrange("p r g j -> p r (g j)"))
                    act.drain().then_inc(x_ready[u], 1)
                for u in range(2):
                    act.wait_ge(y_ev[u], i + 2)
                    SC.activation(yst[:, u], yst[:, u], ACT.Gelu_apprx_tanh).then_inc(y_act[u], 1)
                    act.wait_ge(y_act[u], i + 1)
                    act.dma_start(dram_tile(yd, i * 2 + u), yst[:, u].rearrange("p g j -> p (g j)")).then_inc(y_out[u], 16)
            for u in range(2):
                act.wait_ge(y_out[u], 16 * GP // 2 + 16)

        @block.tensor
        def _(pe):
            with pe.Fori(0, GP // 2) as i:
                for u in range(2):
                    gp = i * 2 + u
                    pe.wait_ge(ca_in[u], i * 16 + 16)
                    pe.wait_ge(t_ready[u], i + 1)
                    pe.wait_ge(x_ready[u], i + 1)
                    pe.wait_ge(y_ev[u], i + 1)
                    for g in range(2):
                        hp = slice(64 * g, 64 * g + 64)
                        o = k.ps[:, 2 * u + g, 0:NJ]
                        nc.tensor.matmul(o, tsum[:, u, g * P:(g + 1) * P],
                                         s5.u[:, bass.ds(gp * 2 + g, 1), :].rearrange("p a b -> p (a b)"), start=True, stop=False)
                        for q in range(4):
                            last = nc.tensor.matmul(o, cas[hp, u, q * P:(q + 1) * P], xp[hp, u, q, :],
                                                    start=False, stop=(q == 3))
                    last.then_inc(y_mm[u], 1)


def s5_glu(nc, k, y, o, weights, z_d, yd):
    strips_, zt, sg, g = (k.arena.take(2, KT * P), k.arena.take(2, T), k.arena.take(2, T), k.arena.take(2, T))
    V, SC = nc.vector, nc.scalar
    with Phase(nc) as es:
        sem = lambda n, credit=0: es.semaphore(n, credit)
        y_in = sem("glu_y_in")
        w_in = [sem(f"glu_w_in{u}") for u in range(2)]
        z_in = [sem(f"glu_z_in{u}") for u in range(2)]
        mm_done = [sem(f"glu_mm_done{u}", 1) for u in range(2)]
        sig = [sem(f"glu_sig{u}", 1) for u in range(2)]
        gated = [sem(f"glu_gated{u}", 1) for u in range(2)]
        block = es.block()

        @block.sync
        def _(sp):
            for g in range(G):
                sp.dma_start(y[16 * (g % 8):16 * (g % 8) + 16, g // 8, :].rearrange("c (t j) -> c t j", t=S),
                             yd[g // 2].rearrange("(t c) (g j) -> g c t j", c=16, g=2)[g % 2]).then_inc(y_in, 16)
            with sp.Fori(0, KT // 2) as i:
                for u in range(2):
                    sp.wait_ge(mm_done[u], i + 1)
                    sp.dma_start(strips_[:, u, :], dram_tile(weights, i * 2 + u)).then_inc(w_in[u], 16)
                    sp.wait_ge(gated[u], i + 1)
                    sp.dma_start(zt[:, u, :], dram_tile(z_d, i * 2 + (KT + u))).then_inc(z_in[u], 16)

        @block.tensor
        def _(pe):
            pe.wait_ge(y_in, 16 * G)
            hold(k, pe)
            with pe.Fori(0, KT // 2) as i:
                for u in range(2):
                    pe.wait_ge(w_in[u], i * 16 + 16)
                    pe.wait_ge(sig[u], i + 1)
                    strip_matmuls(nc, k, u, strips_[:, u, :], y).then_inc(mm_done[u], 1)

        @block.scalar
        def _(act):
            with act.Fori(0, KT // 2) as i:
                for u in range(2):
                    act.wait_ge(z_in[u], i * 16 + 16)
                    act.wait_ge(gated[u], i + 1)
                    SC.activation(g[:, u, :], zt[:, u, :], ACT.Sigmoid)
                    act.wait_ge(mm_done[u], i + 2)
                    SC.activation(sg[:, u, :], acc(k, u), ACT.Sigmoid, bias=k.b_glu[:, bass.ds(i * 2 + u, 1)]).then_inc(sig[u], 1)

        @block.vector
        def _(dve):
            dve.wait_ge(y_in, 16 * G)
            with dve.Fori(0, KT // 2) as i:
                for u in range(2):
                    dve.wait_ge(sig[u], i + 2)
                    dst = o[:, bass.ds(i * 2 + u, 1), :].rearrange("p a b -> p (a b)")
                    V.tensor_tensor(zt[:, u, :], zt[:, u, :], g[:, u, :], ALU.mult)
                    V.tensor_tensor(sg[:, u, :], sg[:, u, :], y[:, bass.ds(i * 2 + u, 1), :].rearrange("p a b -> p (a b)"), ALU.mult)
                    dve.drain()
                    V.tensor_tensor(dst, zt[:, u, :], sg[:, u, :], ALU.mult).then_inc(gated[u], 1)


def s5_layer(nc, k, l, src, dst):
    A, take = k.A, k.arena.take
    h = take(KT, T)
    after_h = k.arena.at
    norm(nc, k, l, h, src)
    k.arena.at = after_h
    dense_to_dram(nc, k, h, A["s5_w_in"], 16, k.proj, chunked=True)
    k.arena.at = k.mark
    s5 = Ctx()
    N = 2 * GP
    s5.kd, s5.cad = k.kd, k.cad
    s5.dsk, s5.coef = take(G), take(2, 2, N)
    s5.u = take(G, NJ)
    s5.X = take(2, N * (NJ + 1)).rearrange("p r (n j) -> p r n j", j=NJ + 1)
    mid = k.arena.at
    s5.br, s5.bi, s5.cr, s5.ci, s5.tmpb = (take(GP, 16) for _ in range(5))
    s5.AR, s5.AI = take(S + 1, N), take(S + 1, N)
    s5.bb = take(2, N * 16).rearrange("p r (n c) -> p r n c", c=16)
    scratch = k.arena.at
    s5_discretise(nc, k, s5)
    k.arena.at = scratch
    s5.pw = take(2, 4 * (S + 1)).rearrange("p u (d r n) -> p u d r n", d=2, r=2)
    s5.cpair, s5.cl = take(2, 2, 16), take(2, 4, P)
    s5_matrices(nc, k, s5, k.proj)
    k.arena.at = mid
    s5.T = take(2, G * P).rearrange("p d (g l) -> p d g l", l=P)
    top = k.arena.at
    s5_scan(nc, k, s5)
    k.arena.at = top
    s5_outputs(nc, k, s5, k.yd)
    k.arena.at = k.mark
    y, o = take(KT, T), take(KT, T)
    after = k.arena.at
    s5_glu(nc, k, y, o, A["s5_w_glu"], k.proj, k.yd)
    k.arena.at = after
    dense_residual(nc, k, l, o, A["s5_w_out"], src, dst, chunked=True)


def rwkv_project(nc, k, j, h, hid):
    take = k.arena.take
    dd, xs = take(KT, T), [take(KT, T), take(KT, T)]
    strips_, stage = take(2, KT * P), take(2, T)
    V = nc.vector
    with Phase(nc) as es:
        sem = lambda n, credit=0: es.semaphore("rp_" + n, credit)
        xs_ready = sem("xs_ready")
        w_in = [sem(f"w_in{u}") for u in range(2)]
        mm_done = [sem(f"mm_done{u}", 1) for u in range(2)]
        ev_done = [sem(f"ev_done{u}", 1) for u in range(2)]
        stored = [sem(f"stored{u}", 16) for u in range(2)]
        block = es.block()

        @block.sync
        def _(sp):
            with sp.Fori(0, 17) as i:
                for u in range(2):
                    sp.wait_ge(mm_done[u], i + 1)
                    sp.dma_start(strips_[:, u, :], dram_tile(k.A["rw_w"], i * 2 + (34 * j + u))).then_inc(w_in[u], 16)

        @block.vector
        def _(dve):
            for c in range(KT):
                V.tensor_tensor(dd[:, c, 1:T - 1], h[:, c, 0:T - 2], h[:, c, 2:T], ALU.add)
            dve.drain()
            for a, b in SEGS:
                V.tensor_copy(dd[:, :, a:a + 1], h[:, :, a + 1:a + 2])
                V.tensor_copy(dd[:, :, b - 1:b], h[:, :, b - 2:b - 1])
            dve.drain()
            for c in range(KT):
                V.scalar_tensor_tensor(dd[:, c, :], dd[:, c, :], 0.5, h[:, c, :], ALU.mult, ALU.subtract)
            dve.drain()
            for n in range(6):
                if n >= 2:
                    dve.wait_ge(mm_done[1], 4 * (n - 1) + 1)
                for c in range(KT):
                    last = V.scalar_tensor_tensor(xs[n % 2][:, c, :], dd[:, c, :], k.mu[:, (j * 6 + n) * KT + c:(j * 6 + n) * KT + c + 1],
                                                  h[:, c, :], ALU.mult, ALU.add)
                last.then_inc(xs_ready, 1)

        @block.tensor
        def _(pe):
            for n in range(4):
                pe.wait_ge(xs_ready, n + 1)
                with pe.Fori(0, 4) as i:
                    for u in range(2):
                        pe.wait_ge(w_in[u], i * 16 + (64 * n + 16))
                        pe.wait_ge(ev_done[u], i + 4 * n + 1)
                        strip_matmuls(nc, k, u, strips_[:, u, :], xs[n % 2]).then_inc(mm_done[u], 1)
            for u in range(2):
                pe.wait_ge(xs_ready, 5 + u)
                pe.wait_ge(w_in[u], 17 * 16)
                pe.wait_ge(ev_done[u], 16 + 1)
                strip_matmuls(nc, k, u, strips_[:, u, :], xs[u]).then_inc(mm_done[u], 1)

        @block.scalar
        def _(act):
            with act.Fori(0, 16) as i:
                for u in range(2):
                    act.wait_ge(mm_done[u], i + 2)
                    act.wait_ge(stored[u], i * 16 + 16)
                    nc.scalar.copy(stage[:, u, :], acc(k, u)).then_inc(ev_done[u], 1)
                    act.wait_ge(ev_done[u], i + 2)
                    act.dma_start(dram_tile(k.proj, i * 2 + u), stage[:, u, :]).then_inc(stored[u], 16)
            act.wait_ge(mm_done[0], 17 + 1)
            nc.scalar.activation(hid[:, 0, :], acc(k, 0), ACT.Tanh)
            act.wait_ge(mm_done[1], 17 + 1)
            nc.scalar.copy(hid[:, 1, :], acc(k, 1))
            for u in range(2):
                act.wait_ge(stored[u], 256 + 16)


KK_, R_, KH_, BH_ = range(4)
NW2 = T // (2 * W)


def rwkv_recur(nc, k, j, o, hid):
    take = k.arena.take
    rkvg, kkn, sg, ic = take(4, T), take(T), take(2, T), take(2, T)
    y, t1, t2 = take(T), take(T), take(T)
    w2t, par = take(2, P), take(NPAR)
    TT, KHs, pc = take(2, NCH, C), take(2, NCH, C), take(2, NCH)
    QT = sg
    ops = take(4, 2, 2 * W)
    tmp = t1.rearrange("p (a b) -> p a b", b=2 * W)
    tmq = t2.rearrange("p (a b) -> p a b", b=2 * W)
    lanes = []
    for L in range(2):
        b = Ctx()
        b.V, b.Kt, b.Bt, b.RH = take(P), take(2, P), take(2, P), take(4, P)
        b.X, b.XT, b.NT, b.F, b.X2, b.X2T, b.X4, b.M1, b.M3, b.M4 = (take(4, P) for _ in range(10))
        b.Di, b.Z, b.ZT, b.Z2, b.Z2T, b.Z4T, b.GH = b.X, b.X2, b.X2T, b.X4, b.XT, b.NT, b.M1
        b.bank = [k.ps[:, 4 * L + n, :] for n in range(4)]
        b.pair = [k.ps[:, 4 * L + n:4 * L + n + 2, :].rearrange("p h (q c) -> p h q c", c=P) for n in (0, 2)]
        b.b4 = [v.rearrange("p (u c) -> p u c", u=4) for v in b.bank]
        lanes.append(b)
    stq, Sst = take(2, 4, C), take(2, 2, C)
    V, SC, PE = nc.vector, nc.scalar, nc.tensor
    r_, k_, v_, g_ = (rkvg[:, n, :] for n in range(4))
    units = [(d, hh) for d in range(2) for hh in range(2)]
    HP = [slice(0, 64), slice(64, 128)]

    v_win, rq, gn = take(2 * W), take(2, 2 * W), take(2)

    with Phase(nc) as es:
        sem = lambda n, credit=0: es.semaphore("rw_" + n, credit)
        tile_in, vg_in = sem("k_r_in"), sem("v_g_in")
        rk_free, tile_done = sem("k_r_free"), sem("tile_done", 1)
        rq_ready = sem("rq_ready")
        sq_ready, norm_mm, norm_root, kk_ready = sem("sq_ready"), sem("norm_mm"), sem("norm_root"), sem("kk_ready")
        lora_mm, lora_ev = sem("lora_mm"), sem("lora_ev")
        cum_ready, decays, ops_ready = sem("cum_ready"), sem("decays"), sem("ops_ready")
        pst = [[sem(f"pe{s}_{L}") for s in range(14)] for L in range(2)]
        ast = [[sem(f"act{s}_{L}", s // 8) for s in range(9)] for L in range(2)]
        dst = [[sem(f"dve{s}_{L}", s // 9) for s in range(10)] for L in range(2)]
        step_q, step_t = [sem(f"step_q{p}") for p in range(2)], [sem(f"step_t{p}") for p in range(2)]
        s_mm, s_ev, y_mm, y_ev = ([sem(f"{n}{p}", 1) for p in range(2)] for n in ("s_mm", "s_ev", "y_mm", "y_ev"))
        start_ev = sem("state_zeroed")
        post_in, post_mm, post_ev, post_sq, post_sig = sem("post_in"), sem("post_mm"), sem("post_ev"), sem("post_sq"), sem("post_sig")
        block = es.block()

        @block.sync
        def _(sp):
            def first_loads(e, off):
                for n in (1, 0):
                    sp.dma_start(rkvg[:, n, :], dram_tile(k.proj, e + (n * KT + off))).then_inc(tile_in, 16)
                sp.dma_start(w2t, dram_tile(k.A["rw_w2"], e + (KT * j + off)).rearrange("p (a b) -> p a b", b=P)).then_inc(tile_in, 16)
                sp.dma_start(par, dram_tile(k.A["rw_par"], e + (KT * j + off))).then_inc(tile_in, 16)

            def last_loads(e):
                sp.wait_ge(tile_done, e + 1)
                for n in (2, 3):
                    sp.dma_start(rkvg[:, n, :], dram_tile(k.proj, e + n * KT)).then_inc(vg_in, 16)

            first_loads(0, 0)
            with sp.Fori(0, KT - 1) as e:
                last_loads(e)
                sp.wait_ge(rk_free, e + 1)
                first_loads(e, 1)
            last_loads(KT - 1)

        @block.tensor
        def _(pe):
            def head_sums(src, half):
                for n, (a, b) in enumerate(CHUNKS):
                    last = PE.matmul(k.ps[:, 3 * half + n, 0:b - a], k.head_ones, src[:, a:b], start=True, stop=True)
                return last

            def lora(which, s, half):
                for n, (a, b) in enumerate(CHUNKS):
                    last = PE.matmul(k.ps[:, 3 * half + n, 0:b - a], w2t[HP[s], which, :], hid[HP[s], which, a:b],
                                     start=True, stop=True)
                return last

            def bonus_sums():
                for n, (a, b) in enumerate(CHUNKS):
                    last = PE.matmul(k.ps[:, 4 + n, 0:b - a], k.head_ones, t2[:, a:b], start=True, stop=True)
                return last

            def four(bank, lhsT, rhs):
                for u in range(4):
                    last = PE.matmul(bank[:, u, :], lhsT(u), rhs(u), start=True, stop=True)
                return last

            with pe.Fori(0, KT) as e:
                pe.wait_ge(sq_ready, e + 1)
                head_sums(t1, 0).then_inc(norm_mm, 1)
                lora(0, 0, 1).then_inc(lora_mm, 1)
                pe.wait_ge(norm_root, e + 1)
                lora(0, 1, 0).then_inc(lora_mm, 1)
                pe.wait_ge(lora_ev, e * 4 + 1)
                lora(1, 0, 1).then_inc(lora_mm, 1)
                pe.wait_ge(lora_ev, e * 4 + 2)
                lora(1, 1, 0).then_inc(lora_mm, 1)
                pe.wait_ge(lora_ev, e * 4 + 4)
                hold(k, pe)

                with pe.Fori(0, NW2) as w:
                    it = e * NW2 + w

                    def op(L, kind, u):
                        d, hh = units[u]
                        return ops[HP[hh], kind, d, L * W:(L + 1) * W]

                    def transposes(L):
                        b = lanes[L]
                        if L == 0:
                            pe.wait_ge(ops_ready, it + 1)
                        pe.wait_ge(dst[L][9], it + 1)
                        pe.wait_ge(ast[L][8], it + 1)
                        PE.transpose(b.bank[0][:, 0:P], v_win[:, L * W:(L + 1) * W], k.ident)
                        for d in range(2):
                            PE.transpose(b.bank[0][:, (1 + d) * P:(2 + d) * P], ops[:, KK_, d, L * W:(L + 1) * W], k.ident)
                        PE.transpose(b.bank[0][:, 3 * P:4 * P], ops[:, KH_, 0, L * W:(L + 1) * W], k.ident)
                        PE.transpose(b.bank[1][:, 0:P], ops[:, KH_, 1, L * W:(L + 1) * W], k.ident)
                        for d in range(2):
                            last = PE.transpose(b.bank[1][:, (1 + d) * P:(2 + d) * P], ops[:, BH_, d, L * W:(L + 1) * W], k.ident)
                        last.then_inc(pst[L][0], 1)

                    def s1(L):
                        b = lanes[L]
                        for hh in range(2):
                            for d in range(2):
                                PE.matmul(b.pair[1][:, hh, d, :], op(L, KK_, 2 * d + hh), op(L, BH_, 2 * d + hh),
                                          start=True, stop=True)
                                last = PE.matmul(b.pair[1][:, hh, 2 + d, :], op(L, BH_, 2 * d + hh), op(L, KK_, 2 * d + hh),
                                                 start=True, stop=True)
                        last.then_inc(pst[L][1], 1)

                    def s2(L):
                        b = lanes[L]
                        pe.wait_ge(ast[L][0], it + 1)
                        hold(k, pe)
                        for hh in range(2):
                            for d in range(2):
                                last = PE.matmul(b.pair[0][:, hh, 2 * d:2 * d + 2, :], op(L, KH_, 2 * d + hh),
                                                 ops[HP[hh], KK_:R_ + 1, d, L * W:(L + 1) * W], start=True, stop=True)
                        last.then_inc(pst[L][2], 1)

                    def s3(L):
                        b = lanes[L]
                        pe.wait_ge(dst[L][1], it + 1)
                        four(b.b4[2], lambda u: b.XT[:, u, :], lambda u: b.X[:, u, :])
                        four(b.b4[3], lambda u: b.X[:, u, :], lambda u: b.XT[:, u, :]).then_inc(pst[L][3], 1)

                    def s4(L):
                        b = lanes[L]
                        pe.wait_ge(dst[L][2], it + 1)
                        hold(k, pe)
                        for hh in range(2):
                            for d in range(2):
                                PE.matmul(b.pair[0][:, hh, d, :], op(L, BH_, 2 * d + hh), op(L, R_, 2 * d + hh), start=True, stop=True)
                        for u, (d, hh) in enumerate(units):
                            last = PE.matmul(b.pair[0][:, hh, 2, d * C:(d + 1) * C], b.M1[:, u, :], b.V[:, HP[hh]], start=True, stop=True)
                        last.then_inc(pst[L][4], 1)

                    def s5(L):
                        b = lanes[L]
                        pe.wait_ge(ast[L][1], it + 1)
                        four(b.b4[2], lambda u: b.X2T[:, u, :], lambda u: b.X2[:, u, :])
                        four(b.b4[3], lambda u: b.X2[:, u, :], lambda u: b.F[:, u, :]).then_inc(pst[L][5], 1)

                    def s6(L):
                        b = lanes[L]
                        pe.wait_ge(ast[L][2], it + 1)
                        pe.wait_ge(dst[L][4], it + 1)
                        four(b.b4[3], lambda u: b.X4[:, u, :], lambda u: b.F[:, u, :]).then_inc(pst[L][6], 1)

                    def s7(L):
                        b = lanes[L]
                        pe.wait_ge(dst[L][5], it + 1)
                        for u in range(4):
                            last = PE.transpose(b.b4[2][:, u, :], b.F[:, u, :], k.ident)
                        last.then_inc(pst[L][7], 1)

                    def s8(L):
                        b = lanes[L]
                        pe.wait_ge(ast[L][3], it + 1)
                        four(b.b4[0], lambda u: b.Di[:, u, :], lambda u: b.NT[:, u, :])
                        four(b.b4[1], lambda u: b.NT[:, u, :], lambda u: b.Di[:, u, :]).then_inc(pst[L][8], 1)

                    def s9(L):
                        b = lanes[L]
                        pe.wait_ge(ast[L][4], it + 1)
                        four(b.b4[2], lambda u: b.Z[:, u, :], lambda u: b.ZT[:, u, :])
                        four(b.b4[3], lambda u: b.ZT[:, u, :], lambda u: b.Z[:, u, :])
                        four(b.b4[0], lambda u: b.ZT[:, u, :], lambda u: b.F[:, u, :]).then_inc(pst[L][9], 1)

                    def s10(L):
                        b = lanes[L]
                        pe.wait_ge(ast[L][5], it + 1)
                        four(b.b4[1], lambda u: b.Z2[:, u, :], lambda u: b.Z2T[:, u, :])
                        pe.wait_ge(dst[L][6], it + 1)
                        four(b.b4[2], lambda u: b.Z2T[:, u, :], lambda u: b.F[:, u, :]).then_inc(pst[L][10], 1)

                    def s11(L):
                        b = lanes[L]
                        pe.wait_ge(ast[L][6], it + 1)
                        pe.wait_ge(dst[L][7], it + 1)
                        four(b.b4[3], lambda u: b.Z4T[:, u, :], lambda u: b.F[:, u, :]).then_inc(pst[L][11], 1)

                    def s12(L):
                        b = lanes[L]
                        pe.wait_ge(dst[L][8], it + 1)
                        four(b.b4[0], lambda u: b.F[:, u, :], lambda u: b.RH[:, u, :]).then_inc(pst[L][12], 1)

                    def s13(L):
                        b = lanes[L]
                        pe.wait_ge(ast[L][7], it + 1)
                        pe.wait_ge(dst[L][3], it + 1)
                        hold(k, pe)
                        for u, (d, hh) in enumerate(units):
                            PE.matmul(b.bank[1][HP[hh], d * P:(d + 1) * P], b.GH[:, u, 0:C], b.M4[:, u, :], start=True, stop=True)
                        for hh in range(2):
                            terms = [(b.V[:, HP[hh]], b.M3[:, 2 * d + hh, :]) for d in range(2)]
                            terms += [(b.GH[:, 2 * d + hh, C:2 * C], b.M4[:, 2 * d + hh, :]) for d in range(2)]
                            for n, (l, r) in enumerate(terms):
                                PE.matmul(b.bank[0][HP[hh], 0:P], l, r, start=(n == 0), stop=(n == 3))
                        for c in range(2):
                            cp = HP[c]
                            for u, (d, hh) in enumerate(units):
                                PE.matmul(b.bank[2 + c][HP[hh], d * C:(d + 1) * C], b.GH[cp, u, 0:C], b.Bt[cp, d, HP[hh]],
                                          start=True, stop=True)
                            for u, (d, hh) in enumerate(units):
                                out = b.bank[2 + c][HP[hh], (2 + d) * C:(3 + d) * C]
                                PE.matmul(out, b.Kt[cp, d, HP[hh]], b.V[cp, HP[hh]], start=True, stop=False)
                                last = PE.matmul(out, b.Bt[cp, d, HP[hh]], b.GH[cp, u, C:2 * C], start=False, stop=True)
                        last.then_inc(pst[L][13], 1)

                    for stage in (transposes, s1, s2, s3, s4, s5, s6, s7, s8, s9, s10, s11, s12, s13):
                        for L in range(2):
                            stage(L)
                for L in range(2):
                    pe.wait_ge(dst[L][9], (e + 1) * NW2 + 1)
                    pe.wait_ge(ast[L][8], (e + 1) * NW2 + 1)
                hold(k, pe)
                pe.wait_ge(post_in, e * 2 + 1)
                bonus_sums().then_inc(post_mm, 1)

                pe.wait_ge(start_ev, e + 1)
                hold(k, pe)
                with pe.Fori(0, NCH // 2) as n:
                    it = e * (NCH // 2) + n
                    for p in range(2):
                        pe.wait_ge(step_t[p], it + 1)
                        pe.wait_ge(step_q[p], it + 1)
                        hold(k, pe)
                        pe.wait_ge(s_ev[1 - p], it + (p + 1))
                        pe.wait_ge(y_ev[p], it + 1)
                        hold(k, pe)
                        for hh in range(2):
                            for d in range(2):
                                last = PE.matmul(k.ps[HP[hh], p, d * C:(d + 1) * C], stq[HP[hh], p, 2 * d, :],
                                                 Sst[HP[hh], p, d, :], start=True, stop=True)
                        last.then_inc(s_mm[p], 1)
                        for hh in range(2):
                            for d in range(2):
                                last = PE.matmul(k.ps[HP[hh], 2 + p, d * C:(d + 1) * C], Sst[HP[hh], p, d, :],
                                                 stq[HP[hh], p, 2 * d + 1, :], start=True, stop=True)
                        last.then_inc(y_mm[p], 1)
                pe.wait_ge(post_in, e * 2 + 2)
                head_sums(y, 0).then_inc(post_mm, 1)
                pe.wait_ge(post_sq, e + 1)
                pe.wait_ge(post_ev, e * 3 + 2)
                head_sums(t1, 1).then_inc(post_mm, 1)

        @block.scalar
        def _(act):
            with act.Fori(0, KT) as e:
                act.wait_ge(cum_ready, e * (NW2 + 1) + 1)
                SC.activation(t1, kkn, ACT.Square).then_inc(sq_ready, 1)
                act.wait_ge(norm_mm, e + 1)
                SC.activation(t2, k.psf[:, 0:T], ACT.Sqrt).then_inc(norm_root, 1)
                for n, (dst_, col) in enumerate(((sg[:, 0, :], P_W0), (sg[:, 1, :], P_W0 + 1),
                                                 (ic[:, 0, :], P_A0), (ic[:, 1, :], P_A0 + 1))):
                    act.wait_ge(lora_mm, e * 4 + n + 1)
                    half = 1 - n % 2
                    SC.activation(dst_, k.psf[:, 3 * half * BANK:3 * half * BANK + T], ACT.Sigmoid,
                                  bias=par[:, col:col + 1]).then_inc(lora_ev, 1)
                def decay(w, off):
                    act.drain()
                    act.wait_ge(cum_ready, e * (NW2 + 1) + w + (off + 2))
                    for d in range(2):
                        SC.activation(ops[:, R_, d, :], tmp[:, d, :], ACT.Exp, scale=-DECAY)
                        SC.activation(ops[:, KH_, d, :], tmp[:, d, :], ACT.Exp, scale=DECAY)
                        SC.activation(ops[:, KK_, d, :], tmp[:, 2 + d, :], ACT.Exp, scale=-DECAY)
                    act.drain().then_inc(decays, 1)

                def window(w, more):
                    it = e * NW2 + w

                    def copies(L, stage, after, pairs):
                        act.wait_ge(pst[L][after], it + 1)
                        for out, in_ in pairs:
                            last = SC.copy(out, in_)
                        last.then_inc(ast[L][stage], 1)

                    def c0(L):
                        b = lanes[L]
                        copies(L, 0, 0, [(b.V, b.bank[0][:, 0:P]),
                                         (b.RH[:, :, 0:C], b.bank[0][:, P:3 * P].rearrange("p (u c) -> p u c", u=4)),
                                         (b.Kt[:, 0, :], b.bank[0][:, 3 * P:4 * P]),
                                         (b.Kt[:, 1, :], b.bank[1][:, 0:P]),
                                         (flat(b.Bt), b.bank[1][:, P:3 * P])])

                    def c1(L):
                        b = lanes[L]
                        copies(L, 1, 3, [(flat(b.X2), b.bank[2]), (flat(b.X2T), b.bank[3])])

                    def c2(L):
                        b = lanes[L]
                        act.wait_ge(dst[L][3], it + 1)
                        SC.copy(b.RH[:, :, C:2 * C].rearrange("p (d h) c -> p h d c", d=2),
                                b.pair[0][:, :, 2, :].rearrange("p h (d c) -> p h d c", d=2))
                        copies(L, 2, 5, [(flat(b.X4), b.bank[2])])

                    def c3(L):
                        copies(L, 3, 7, [(flat(lanes[L].Di), lanes[L].bank[2])])

                    def c4(L):
                        b = lanes[L]
                        copies(L, 4, 8, [(flat(b.Z), b.bank[0]), (flat(b.ZT), b.bank[1])])

                    def c5(L):
                        b = lanes[L]
                        copies(L, 5, 9, [(flat(b.Z2T), b.bank[2]), (flat(b.Z2), b.bank[3])])

                    def c6(L):
                        copies(L, 6, 10, [(flat(lanes[L].Z4T), lanes[L].bank[1])])

                    def c7(L):
                        act.wait_ge(pst[L][12], it + 1)
                        SC.mul(flat(lanes[L].GH), lanes[L].bank[0], -1.0).then_inc(ast[L][7], 1)

                    def c8(L):
                        act.wait_ge(pst[L][13], it + 1)
                        hold(k, act)
                        SC.copy(y[:, bass.ds(w * 2 * W + L * W, W)], lanes[L].bank[0][:, 0:P]).then_inc(ast[L][8], 1)

                    def keep_r():
                        act.wait_ge(dst[1][9], it + 1)
                        SC.copy(rq, ops[:, R_, :, :]).then_inc(rq_ready, 1)

                    for c in (c0, c1, c2, c3, c4, c5, c6, c7, c8):
                        for L in range(2):
                            c(L)
                        if c is c1:
                            keep_r()
                        if c is c2 and more:
                            decay(w, 1)

                decay(0, 0)
                with act.Fori(0, NW2 - 1) as w:
                    window(w, True)
                window(NW2 - 1, False)

                def step_copies(n, last_of):
                    for p in range(2):
                        it = e * (NCH // 2) + n
                        act.wait_ge(y_mm[p], it + 1)
                        act.wait_ge(dst[1][9], (e + 1) * NW2 + 1)
                        hold(k, act)
                        SC.copy(stq[:, p, 1, :], QT[:, 0, bass.ds(n * 2 * C + p * C, C)])
                        SC.copy(stq[:, p, 3, :], QT[:, 1, bass.ds(n * (-2 * C) + (last_of - p) * C, C)])
                        act.drain().then_inc(step_q[p], 1)
                with act.Fori(0, NCTX // C // 2) as n:
                    step_copies(n, NCTX // C - 1)
                with act.Fori(NCTX // C // 2, NCH // 2) as n:
                    step_copies(n, NCH + NCTX // C - 1)
                act.wait_ge(post_ev, e * 3 + 1)
                SC.activation(t1, y, ACT.Square).then_inc(post_sq, 1)
                act.wait_ge(post_ev, e * 3 + 3)
                SC.activation(kkn, kkn, ACT.Sqrt)
                act.wait_ge(vg_in, e * 32 + 32)
                SC.activation(ic[:, 0, :], g_, ACT.Sigmoid)
                act.drain().then_inc(post_sig, 1)

        @block.gpsimd
        def _(pool):
            with pool.Fori(0, KT) as e:
                def step_copies(n, last_of):
                    for p in range(2):
                        it = e * (NCH // 2) + n
                        pool.wait_ge(s_mm[p], it + 1)
                        pool.wait_ge(dst[1][9], (e + 1) * NW2 + 1)
                        hold(k, pool)
                        nc.gpsimd.tensor_copy(stq[:, p, 0, :], TT[:, 0, bass.ds(n * 2 + p, 1), :].rearrange("p a b -> p (a b)"))
                        nc.gpsimd.tensor_copy(stq[:, p, 2, :], TT[:, 1, bass.ds(n * (-2) + (last_of - p), 1), :].rearrange("p a b -> p (a b)"))
                        pool.drain().then_inc(step_t[p], 1)
                with pool.Fori(0, NCTX // C // 2) as n:
                    step_copies(n, NCTX // C - 1)
                with pool.Fori(NCTX // C // 2, NCH // 2) as n:
                    step_copies(n, NCH + NCTX // C - 1)

        @block.vector
        def _(dve):
            with dve.Fori(0, KT) as e:
                dve.wait_ge(tile_in, e * 64 + 64)
                V.tensor_scalar(kkn, k_, par[:, P_KK:P_KK + 1], None, ALU.mult).then_inc(cum_ready, 1)
                dve.wait_ge(norm_root, e + 1)
                V.tensor_scalar(t2, t2, 1e-12, None, ALU.max)
                dve.drain()
                V.reciprocal(t2, t2)
                dve.drain()
                V.tensor_tensor(kkn, kkn, t2, ALU.mult)
                dve.drain()
                dve.wait_ge(lora_ev, e * 4 + 4)
                hold(k, dve)

                def prepare(w, off):
                    def at(v):
                        return v[:, bass.ds(w * (2 * W) + off * 2 * W, 2 * W)]
                    sgw = [at(sg[:, d, :]) for d in range(2)]
                    icw = [at(ic[:, d, :]) for d in range(2)]

                    def sums():
                        V.tensor_tensor_scan(tmp[:, 0, :], k.seq_mask, sgw[0], 0.0, ALU.mult, ALU.add)
                        V.tensor_tensor_scan(tmp[:, 1, :], k.seq_mask, sgw[1], 0.0, ALU.mult, ALU.add)
                        V.tensor_copy(v_win, at(v_))
                        dve.drain()

                    def before():
                        V.tensor_tensor(tmp[:, 2, :], tmp[:, 0, :], sgw[0], ALU.subtract)
                        left = tmp[:, 1, :].rearrange("p (c t) -> p c t", t=C)
                        V.tensor_tensor(tmp[:, 3, :].rearrange("p (c t) -> p c t", t=C),
                                        left[:, :, C - 1:C].to_broadcast([P, 2 * W // C, C]), left, ALU.subtract)
                        dve.drain()
                        V.tensor_tensor(tmp[:, 1, :], tmp[:, 3, :], sgw[1], ALU.add)
                        dve.drain().then_inc(cum_ready, 1)

                    def keys():
                        for d in range(2):
                            V.tensor_scalar(tmq[:, d, :], icw[d], -1.0, par[:, P_KA:P_KA + 1], ALU.add, ALU.mult)
                            V.tensor_tensor(tmq[:, 2 + d, :], at(kkn), icw[d], ALU.mult)
                        dve.drain()

                    def more_keys():
                        for d in range(2):
                            V.scalar_tensor_tensor(tmq[:, d, :], tmq[:, d, :], 1.0, at(k_), ALU.add, ALU.mult)
                        dve.drain()

                    def ends():
                        dve.wait_ge(decays, e * NW2 + w + (off + 1))
                        hold(k, dve)
                        for c in range(4):
                            cc = w * 4 + (off * 4 + c)
                            V.tensor_copy(pc[:, 0, bass.ds(cc, 1)], ops[:, R_, 0, (c + 1) * C - 1:(c + 1) * C])
                            V.tensor_copy(pc[:, 1, bass.ds(cc, 1)], ops[:, R_, 1, c * C:c * C + 1])
                        for d in range(2):
                            V.tensor_tensor(ops[:, BH_, d, :], ops[:, KH_, d, :], tmq[:, 2 + d, :], ALU.mult)
                        dve.drain()

                    def others():
                        for d in range(2):
                            V.tensor_tensor(ops[:, R_, d, :], ops[:, R_, d, :], at(r_), ALU.mult)
                            V.tensor_tensor(ops[:, KH_, d, :], ops[:, KH_, d, :], tmq[:, d, :], ALU.mult)
                            V.tensor_tensor(ops[:, KK_, d, :], ops[:, KK_, d, :], at(kkn), ALU.mult)
                        dve.drain().then_inc(ops_ready, 1)

                    return sums, before, keys, more_keys, ends, others

                def window(w, more):
                    it = e * NW2 + w
                    parts = prepare(w, 1) if more else ()

                    def masked(out, in_, mask):
                        V.tensor_tensor(out.rearrange("p (d h) c -> p h d c", d=2), in_,
                                        mask.unsqueeze(1).to_broadcast([P, 2, 2, P]), ALU.mult)

                    def d1(L):
                        b = lanes[L]
                        dve.wait_ge(pst[L][1], it + 1)
                        hold(k, dve)
                        masked(b.X, b.pair[1][:, :, 0:2, :], k.m_x)
                        masked(b.XT, b.pair[1][:, :, 2:4, :], k.m_xt)
                        masked(b.NT, b.pair[1][:, :, 2:4, :], k.m_nt)
                        dve.drain()
                        V.tensor_tensor(b.F, b.XT, k.ident.unsqueeze(1).to_broadcast([P, 4, P]), ALU.add).then_inc(dst[L][1], 1)

                    def d2(L):
                        b = lanes[L]
                        dve.wait_ge(pst[L][2], it + 1)
                        hold(k, dve)
                        masked(b.M1, b.pair[0][:, :, 0::2, :], k.m_s)
                        masked(b.M3, b.pair[0][:, :, 1::2, :], k.m_i)
                        dve.drain().then_inc(dst[L][2], 1)

                    def d3(L):
                        b = lanes[L]
                        dve.wait_ge(pst[L][4], it + 1)
                        hold(k, dve)
                        masked(b.M4, b.pair[0][:, :, 0:2, :], k.m_i)
                        dve.drain().then_inc(dst[L][3], 1)

                    def addf(L, stage, after, bank, op=ALU.add):
                        b = lanes[L]
                        dve.wait_ge(pst[L][after], it + 1)
                        V.tensor_tensor(b.F, b.F, b.b4[bank], op).then_inc(dst[L][stage], 1)

                    def d9(L):
                        b = lanes[L]
                        dve.wait_ge(pst[L][13], it + 1)
                        dve.wait_ge(rq_ready, it + 1)
                        hold(k, dve)
                        wc = w * 2 * W + L * W
                        V.tensor_tensor(QT[:, :, bass.ds(wc, W)], b.bank[1][:, 0:2 * P].rearrange("p (d c) -> p d c", d=2),
                                        rq[:, :, L * W:(L + 1) * W], ALU.add)
                        for c in range(2):
                            ch = w * 4 + (L * 2 + c)
                            v = b.bank[2 + c].rearrange("p (q c) -> p q c", c=C)
                            V.tensor_tensor(TT[:, :, bass.ds(ch, 1), :].rearrange("p d a c -> p d (a c)"), v[:, 0:2, :],
                                            k.eye2.unsqueeze(1).to_broadcast([P, 2, C]), ALU.add)
                            V.tensor_tensor(KHs[:, :, bass.ds(ch, 1), :].rearrange("p d a c -> p d (a c)"), v[:, 2:4, :],
                                            pc[:, :, bass.ds(ch, 1)].to_broadcast([P, 2, C]), ALU.mult)
                        dve.drain().then_inc(dst[L][9], 1)

                    stages = (d1, d2, d3, lambda L: addf(L, 4, 5, 3), lambda L: addf(L, 5, 6, 3),
                              lambda L: addf(L, 6, 9, 0, ALU.subtract), lambda L: addf(L, 7, 10, 2),
                              lambda L: addf(L, 8, 11, 3), d9)
                    for n, f in enumerate(stages):
                        for L in range(2):
                            f(L)
                        if more and 1 <= n <= 6:
                            parts[n - 1]()

                dve.wait_ge(vg_in, e * 32 + 32)
                hold(k, dve)
                for part in prepare(0, 0):
                    part()
                with dve.Fori(0, NW2 - 1) as w:
                    window(w, True)
                window(NW2 - 1, False)

                V.scalar_tensor_tensor(t2, r_, par[:, P_RK:P_RK + 1], k_, ALU.mult, ALU.mult).then_inc(post_in, 1)
                V.tensor_copy(gn, par[:, P_LNW:P_LNB + 1])
                dve.drain().then_inc(rk_free, 1)

                V.memset(Sst[:, 0, :, :], 0.0).then_inc(start_ev, 1)

                def steps(n, last_of):
                    it = e * (NCH // 2) + n
                    for p in range(2):
                        cf, cb = n * 2 + p, n * (-2) + (last_of - p)
                        dve.wait_ge(s_mm[p], it + 2)
                        dve.wait_ge(y_mm[1 - p], it + (p + 1))
                        hold(k, dve)
                        for d, ch in ((0, cf), (1, cb)):
                            V.scalar_tensor_tensor(Sst[:, 1 - p, d, :], k.ps[:, p, d * C:(d + 1) * C], pc[:, d, bass.ds(ch, 1)],
                                                   KHs[:, d, bass.ds(ch, 1), :].rearrange("p a c -> p (a c)"), ALU.mult, ALU.add)
                        dve.drain().then_inc(s_ev[p], 1)
                        dve.wait_ge(y_mm[p], it + 2)
                        hold(k, dve)
                        for d, ch in ((0, cf), (1, cb)):
                            yc = y[:, bass.ds(ch * C, C)]
                            V.tensor_tensor(yc, yc, k.ps[:, 2 + p, d * C:(d + 1) * C], ALU.add)
                            dve.drain()
                        dve.nop().then_inc(y_ev[p], 1)
                with dve.Fori(0, NCTX // C // 2) as n:
                    steps(n, NCTX // C - 1)
                with dve.Fori(NCTX // C // 2, NCH // 2) as n:
                    steps(n, NCH + NCTX // C - 1)

                dve.drain().then_inc(post_in, 1)
                dve.wait_ge(post_mm, e * 3 + 2)
                V.scalar_tensor_tensor(y, k.psf[:, 0:T], -1.0 / 64, y, ALU.mult, ALU.add).then_inc(post_ev, 1)
                V.tensor_tensor(v_, k.psf[:, 4 * BANK:4 * BANK + T], v_, ALU.mult).then_inc(post_ev, 1)
                dve.wait_ge(post_mm, e * 3 + 3)
                V.tensor_scalar(kkn, k.psf[:, 3 * BANK:3 * BANK + T], 1.0 / 64, GN_EPS, ALU.mult, ALU.add).then_inc(post_ev, 1)
                dve.wait_ge(post_sig, e + 1)
                V.reciprocal(kkn, kkn)
                V.tensor_tensor(g_, g_, ic[:, 0, :], ALU.mult)
                dve.drain()
                V.tensor_tensor(y, y, kkn, ALU.mult)
                dve.drain()
                V.tensor_scalar(y, y, gn[:, 0:1], gn[:, 1:2], ALU.mult, ALU.add)
                dve.drain()
                V.tensor_tensor(y, y, v_, ALU.add)
                dve.drain()
                V.tensor_tensor(o[:, bass.ds(e, 1), :].rearrange("p a b -> p (a b)"), y, g_, ALU.mult)
                dve.drain().then_inc(tile_done, 1)


def rwkv_layer(nc, k, l, src, dst):
    take = k.arena.take
    j = l // 3
    k.mu = take(2 * 6 * KT)
    k.m_x, k.m_xt, k.m_nt, k.m_s, k.m_i = (take(2, P) for _ in range(5))
    k.seq_mask, k.eye2 = take(2 * W), take(C)
    masks = [(flat(v), k.A["m_" + n]) for n, v in
             (("x", k.m_x), ("xt", k.m_xt), ("nt", k.m_nt), ("s", k.m_s), ("i", k.m_i))]
    load_constants(nc, masks + [(k.mu, k.A["mu"]), (k.seq_mask, k.A["seq_mask"]), (k.eye2, k.A["eye2"])])
    h, hid = take(KT, T), take(2, T)
    top = k.arena.at
    norm(nc, k, l, h, src)
    k.arena.at = top
    rwkv_project(nc, k, j, h, hid)
    k.arena.at = top
    rwkv_recur(nc, k, j, h, hid)
    k.arena.at = top
    dense_residual(nc, k, l, h, k.A["rw_w_out"][j * KT:(j + 1) * KT], src, dst)


def program(nc, A, out, layers, depth):
    k = Ctx()
    k.depth, k.n_mod = depth, depth * 24
    with ExitStack() as es:
        cols = (nc.sbuf_bytes_remaining - 64) // 4
        arena_t = es.enter_context(nc.sbuf_tensor("arena", [P, cols], F32))
        k.arena = Arena(arena_t, cols)
        k.ps = es.enter_context(nc.psum_tensor("ps", [P, 8, BANK], F32))
        k.held = es.enter_context(nc.semaphore("waits_held"))
        k.psf = k.ps[:, :, :].rearrange("p a b -> p (a b)")
        take = k.arena.take
        k.ident, k.ones, k.head_ones = take(P), take(P), take(P)
        k.mod, k.b_mod, k.norm_g = take(k.n_mod, 2), take(k.n_mod), take(depth * KT)
        k.na_g, k.b_glu = take(2), take(KT)
        k.A = A
        k.constant_loads = [(k.ident, A["ident"]), (k.ones, A["ones"]), (k.head_ones, A["head_ones"]),
                            (k.b_mod, A["b_mod"]), (k.norm_g, A["norm_g"]), (k.na_g, A["na_g"]),
                            (k.b_glu, A["b_glu"])]
        k.w_mod, k.cond_d, k.na_bias = A["w_mod"], A["cond"], A["na_bias"]
        xres = [nc.dram_tensor(f"xres{i}", (KT, P, T), F32, kind="Internal").ap() for i in range(depth)]
        proj = nc.dram_tensor("proj", (32, P, T), F32, kind="Internal").ap()
        k.proj = proj
        k.kd = nc.dram_tensor("s5_kernel", (2, GP, 2, 16, 2 * P), F32, kind="Internal").ap()
        k.cad = nc.dram_tensor("s5_out_rows", (GP, P, 4 * P), F32, kind="Internal").ap()
        k.yd = nc.dram_tensor("s5_y", (GP, P, 2 * NJ), F32, kind="Internal").ap()
        k.mark = mark = k.arena.at
        load_constants(nc, k.constant_loads)
        modulation(nc, k, mark)
        src = A["x"]
        for l in layers:
            k.arena.at = mark
            dst = out if l == layers[-1] else xres[l]
            if l % 3 != 1:
                (rwkv_layer, None, s5_layer)[l % 3](nc, k, l, src, dst)
                src = dst
                continue
            h = take(KT, T)
            top = k.arena.at
            norm(nc, k, l, h, src)
            k.arena.at = top
            if l % 3 == 1:
                dense_to_dram(nc, k, h, A["na_w_in"], 32, proj)
                k.arena.at = top
                na_attention(nc, k, h, proj)
                k.arena.at = top
                dense_residual(nc, k, l, h, A["na_w_out"], src, dst)
            src = dst


def strips(w):
    e = w.shape[1] // P
    return w.reshape(KT, P, e, P).transpose(2, 1, 0, 3).reshape(e, P, KT * P)


def by_channel(v):
    return v.reshape(-1, KT, P).transpose(2, 0, 1).reshape(P, -1)


def layout(inp):
    I = {n: np.asarray(v) for n, v in inp.items()}
    A = {}
    A["x"] = np.concatenate([I["ctx"][0], I["x"][0]], 0).T.reshape(KT, P, T)
    A["cond"] = np.stack([by_channel(I["c_ctx"]), by_channel(I["c"][0])], -1).reshape(P, KT * 2)
    A["w_mod"] = np.concatenate([strips(w) for w in I["w_mod"]])
    A["b_mod"] = I["b_mod"].reshape(-1, P).T
    A["norm_g"] = by_channel(I["norm_g"])
    A["ident"] = np.eye(P, dtype=np.float32)
    A["ones"] = np.ones((P, P), np.float32)
    half = np.arange(P) // 64
    A["head_ones"] = (half[:, None] == half[None, :]).astype(np.float32)
    A["na_w_in"] = strips(I["na_w_in"][0])
    A["na_w_out"] = strips(I["na_w_out"][0])
    A["na_g"] = np.stack([np.tile(I["na_q_g"][0], 2), np.tile(I["na_k_g"][0], 2)], -1)
    q, c = np.arange(GRID)[:, None], np.arange(GRID)[None, :]
    start = np.clip(q - KW // 2, 0, GRID - KW)
    inside = (c >= start) & (c < start + KW)
    idx = np.clip(c - q + KW - 1, 0, 2 * KW - 2)
    table = I["na_rpb"][0][:, :, idx]
    table = np.where(inside[None, None], table, np.float32(-1e30)).transpose(0, 2, 1, 3)
    A["na_bias"] = table.reshape(KT, P, NA_BIAS)
    first = lambda w: strips(np.concatenate([w[0], w[1]], 1))
    A["rw_w"] = np.concatenate([x for j in range(2) for x in
                                [strips(w) for w in I["rwkv_w_rkvg"][j]] + [first(I["rwkv_w1"][j]), first(I["rwkv_a1"][j])]])
    second = lambda w: w.reshape(P, KT, P).transpose(1, 0, 2)
    A["rw_w2"] = np.concatenate([np.stack([second(I["rwkv_w2"][j]), second(I["rwkv_a2"][j])], 2).reshape(KT, P, 2 * P)
                                 for j in range(2)])
    A["rw_w_out"] = np.concatenate([strips(w) for w in I["rwkv_w_out"]])
    A["mu"] = by_channel(I["rwkv_mu"])
    per_tile = [I["rwkv_mu"][:, n] for n in range(6)] + [I["rwkv_w0"][:, 0], I["rwkv_w0"][:, 1], I["rwkv_a0"][:, 0],
               I["rwkv_a0"][:, 1], I["rwkv_k_k"], I["rwkv_k_a"], I["rwkv_r_k"].reshape(2, D), I["rwkv_ln_w"], I["rwkv_ln_b"]]
    A["rw_par"] = np.stack(per_tile, -1).reshape(2 * KT, P, NPAR)
    a, b = np.arange(P)[:, None], np.arange(P)[None, :]
    chunk, block = a // C == b // C, a // 8 == b // 8
    both = lambda m, m1: np.stack([m, m1], 1).astype(np.float32).reshape(P, 2 * P)
    A["m_x"] = -both(block & (b < a), block & (b > a))
    A["m_xt"] = -both(block & (a < b), block & (a > b))
    A["m_nt"] = both(chunk & ~block & (a < b), chunk & ~block & (a > b))
    A["m_s"] = both(chunk & (a < b), chunk & (a > b))
    A["m_i"] = both(chunk & (a <= b), chunk & (a >= b))
    A["seq_mask"] = np.tile((np.arange(2 * W) % C != 0).astype(np.float32), (P, 1))
    A["eye2"] = np.tile(np.eye(C, dtype=np.float32), (2, 1))
    A["s5_w_in"], A["s5_w_glu"], A["s5_w_out"] = (strips(I["s5_w_" + n][0]) for n in ("in", "glu", "out"))
    A["b_glu"] = by_channel(I["s5_b_glu"])
    per_state = lambda v: v.reshape(2, GP, 2 * NS).transpose(2, 0, 1).reshape(P, 2 * GP)
    A["s5_lr"], A["s5_li"] = per_state(I["s5_lam_re"][0]), per_state(I["s5_lam_im"][0])
    A["s5_dt"] = per_state(np.repeat(I["s5_log_dt"][0][:, :, None], NS, 2))
    for n in ("re", "im"):
        A["s5_b" + n[0]] = I["s5_b_" + n][0].reshape(GP, P, 16).transpose(1, 0, 2).reshape(P, GP * 16)
        A["s5_c" + n[0]] = I["s5_c_" + n][0].reshape(GP, 2, 16, NS).transpose(1, 3, 0, 2).reshape(P, GP * 16)
    A["s5_dsk"] = np.tile(I["s5_d"][0].reshape(G, 16).T, (S, 1))
    return {n: np.ascontiguousarray(a, dtype=np.float32) for n, a in A.items()}


DEPTH = 4


def kernel(**inputs):
    import concourse.bacc as bacc
    from concourse.bass_utils import run_bass_kernel_spmd

    nc = bacc.Bacc("TRN2", target_bir_lowering=False, num_devices=1)
    arrays = layout(inputs)
    A = {n: nc.dram_tensor(n, a.shape, F32, kind="ExternalInput").ap() for n, a in arrays.items()}
    out = nc.dram_tensor("out", (KT, P, T), F32, kind="ExternalOutput").ap()
    program(nc, A, out, list(range(DEPTH)), DEPTH)
    r = run_bass_kernel_spmd(nc, [arrays], core_ids=[0])
    got = r.results[0]["out"].reshape(D, T)
    return np.ascontiguousarray(got[:, NCTX:].T)[None]
```

```python
import numpy as np
import concourse.bass as bass
from concourse import mybir
from contextlib import ExitStack

F32 = mybir.dt.float32
I32 = mybir.dt.int32
ALU = mybir.AluOpType
ACT = mybir.ActivationFunctionType
AXX = mybir.AxisListType.X

D = 1024
P = 128
MODS = 3 * D // P
KT = D // P
NCTX, NLAT = 256, 1024
T = NCTX + NLAT
SEGS = [(0, NCTX), (NCTX, T)]
BANK = 512
CHUNKS = [(0, 512), (512, 1024), (1024, T)]
EPS = 1e-6
GN_EPS = 64e-5
DECAY = float(np.exp(-0.5))
C = 64
NCH = T // C
W = 128
NPAR = 15
(P_MU, P_W0, P_A0, P_KK, P_KA, P_RK, P_LNW, P_LNB) = (0, 6, 8, 10, 11, 12, 13, 14)


class Arena:

    def __init__(self, tensor, cols):
        self.tensor, self.cols, self.at = tensor, cols, 0

    def take(self, *shape):
        n = int(np.prod(shape))
        assert self.at + n <= self.cols, f"arena: {self.at} + {n} > {self.cols}"
        v = self.tensor[:, self.at:self.at + n]
        self.at += n
        if len(shape) == 2:
            v = v.rearrange("p (a b) -> p a b", b=shape[1])
        if len(shape) == 3:
            v = v.rearrange("p (a b c) -> p a b c", b=shape[1], c=shape[2])
        if len(shape) == 4:
            v = v.rearrange("p (a b c d) -> p a b c d", b=shape[1], c=shape[2], d=shape[3])
        return v


class Phase:

    def __init__(self, nc):
        self.nc, self.sems, self.credits, self.stack = nc, [], [], ExitStack()

    def __enter__(self):
        return self

    def semaphore(self, name, credit=0):
        self.sems.append(self.stack.enter_context(self.nc.semaphore(name)))
        if credit:
            self.credits.append((self.sems[-1], credit))
        return self.sems[-1]

    def block(self):
        for s, credit in self.credits:
            self.nc.gpsimd.sem_inc(s, credit)
        self.region = self.nc.Block()
        return self.region.__enter__()

    def __exit__(self, *error):
        self.region.__exit__(*error)
        if error[0] is None:
            for s in self.sems:
                self.nc.gpsimd.sem_clear(s)
        self.stack.__exit__(*error)


class Ctx:
    pass


def hold(k, eng):
    eng.sem_inc(k.held, 1)


def flat(v):
    return v.rearrange("p a b -> p (a b)")


def dram_tile(ap, i):
    return ap[bass.ds(i, 1)].rearrange("o p c -> (o p) c")


def load_constants(nc, loads):
    with Phase(nc) as es:
        loaded = es.semaphore("constants_loaded")
        block = es.block()

        @block.sync
        def _(sp):
            for dst, src in loads:
                sp.dma_start(dst, src).then_inc(loaded, 16)
            sp.wait_ge(loaded, 16 * len(loads))


def scale_ready(nc, k, l):
    for s in range(2):
        sc = k.mod[:, l * MODS + KT:l * MODS + 2 * KT, s]
        nc.vector.scalar_tensor_tensor(sc, sc, 1.0, k.norm_g[:, l * KT:(l + 1) * KT], ALU.add, ALU.mult)


class HiddenModulation:

    def __init__(self, nc, k, es, layer, m):
        self.nc, self.k, self.layer, self.m = nc, k, layer, m
        self.turns = MODS // m
        self.strips = k.arena.take(m, KT * P)
        self.w_in, self.mm, self.ev = es.semaphore("hm_w_in"), es.semaphore("hm_mm", 1), es.semaphore("hm_ev", 1)

    def sync_part(self, sp, i):
        sp.wait_ge(self.mm, i + 1)
        for q in range(self.m):
            sp.dma_start(self.strips[:, q, :],
                         dram_tile(self.k.w_mod, i * self.m + (self.layer * MODS + q))).then_inc(self.w_in, 16)

    def tensor_part(self, pe, i):
        pe.wait_ge(self.w_in, i * (16 * self.m) + 16 * self.m)
        pe.wait_ge(self.ev, i + 1)
        for q in range(self.m):
            for c in range(KT):
                last = self.nc.tensor.matmul(self.k.ps[:, 6, 2 * q:2 * q + 2], self.strips[:, q, c * P:(c + 1) * P],
                                             self.k.cond[:, c, :], start=(c == 0), stop=(c == KT - 1))
        last.then_inc(self.mm, 1)

    def vector_part(self, dve, i):
        dve.wait_ge(self.mm, i + 2)
        hold(self.k, dve)
        at = bass.ds(i * self.m + self.layer * MODS, self.m)
        self.nc.vector.tensor_tensor(self.k.mod[:, at, :], self.k.ps[:, 6, 0:2 * self.m].rearrange("p (q s) -> p q s", s=2),
                                     self.k.b_mod[:, at].unsqueeze(2).to_broadcast([P, self.m, 2]), ALU.add)
        dve.drain().then_inc(self.ev, 1)

    def vector_end(self, dve):
        scale_ready(self.nc, self.k, self.layer)


def modulation(nc, k, mark, layer):
    k.arena.at = mark
    strips = k.arena.take(4, KT * P)
    cond = k.cond
    sig = k.arena.take(KT, 2)
    n_iter = MODS // 4
    with Phase(nc) as es:
        sem = lambda n, credit=0: es.semaphore(n, credit)
        cond_in, sig_done, cond_done = sem("cond_in"), sem("sig_done"), sem("cond_done")
        w_in = [sem(f"mod_w_in{u}") for u in range(4)]
        mm_done = [sem(f"mod_mm_done{u}", 1) for u in range(4)]
        ev_done = [sem(f"mod_ev_done{u}", 1) for u in range(4)]
        block = es.block()

        @block.sync
        def _(sp):
            sp.dma_start(cond, k.cond_d.rearrange("p (a b) -> p a b", b=2)).then_inc(cond_in, 16)
            with sp.Fori(0, n_iter) as i:
                for u in range(4):
                    sp.wait_ge(mm_done[u], i + 1)
                    sp.dma_start(strips[:, u, :], dram_tile(k.w_mod, i * 4 + (layer * MODS + u))).then_inc(w_in[u], 16)

        @block.scalar
        def _(act):
            act.wait_ge(cond_in, 16)
            nc.scalar.activation(sig, cond, ACT.Sigmoid).then_inc(sig_done, 1)

        @block.vector
        def _(dve):
            dve.wait_ge(sig_done, 1)
            nc.vector.tensor_tensor(cond, cond, sig, ALU.mult).then_inc(cond_done, 1)
            with dve.Fori(0, n_iter) as i:
                for u in range(4):
                    dve.wait_ge(mm_done[u], i + 2)
                    nc.vector.tensor_scalar(k.mod[:, bass.ds(i * 4 + (layer * MODS + u), 1), :].rearrange("p a b -> p (a b)"),
                                            k.ps[:, u, 0:2], k.b_mod[:, bass.ds(i * 4 + (layer * MODS + u), 1)], None,
                                            ALU.add).then_inc(ev_done[u], 1)
            dve.drain()
            scale_ready(nc, k, layer)

        @block.tensor
        def _(pe):
            pe.wait_ge(cond_done, 1)
            with pe.Fori(0, n_iter) as i:
                for u in range(4):
                    pe.wait_ge(w_in[u], i * 16 + 16)
                    pe.wait_ge(ev_done[u], i + 1)
                    for c in range(KT):
                        last = nc.tensor.matmul(k.ps[:, u, 0:2], strips[:, u, c * P:(c + 1) * P], cond[:, c, :],
                                                start=(c == 0), stop=(c == KT - 1))
                    last.then_inc(mm_done[u], 1)


def norm(nc, k, layer, h, src):
    sq = k.arena.take(2, T)
    rstd = k.arena.take(T)
    with Phase(nc) as es:
        sem = lambda n: es.semaphore(n)
        x_in = [sem(f"x_in{c}") for c in range(KT)]
        sq_done, mm_done, ms_done, root_done = sem("sq_done"), sem("ss_mm"), sem("ms_done"), sem("root_done")
        scaled, final = sem("scaled"), sem("final")
        block = es.block()

        @block.sync
        def _(sp):
            for c in range(KT):
                sp.dma_start(h[:, c, :], src[c]).then_inc(x_in[c], 16)

        @block.scalar
        def _(act):
            for c in range(KT):
                act.wait_ge(x_in[c], 16)
                if c >= 2:
                    act.wait_ge(mm_done, c - 1)
                nc.scalar.activation(sq[:, c % 2, :], h[:, c, :], ACT.Square).then_inc(sq_done, 1)
            act.wait_ge(ms_done, 1)
            nc.scalar.activation(rstd, rstd, ACT.Sqrt).then_inc(root_done, 1)
            for c in range(KT):
                act.wait_ge(scaled, c + 1)
                for s, (a, b) in enumerate(SEGS):
                    nc.scalar.activation(h[:, c, a:b], h[:, c, a:b], ACT.Identity,
                                         bias=k.mod[:, layer * MODS + c, s:s + 1],
                                         scale=k.mod[:, layer * MODS + 8 + c, s:s + 1]).then_inc(final, 1)

        @block.tensor
        def _(pe):
            for c in range(KT):
                pe.wait_ge(sq_done, c + 1)
                for n, (a, b) in enumerate(CHUNKS):
                    last = nc.tensor.matmul(k.ps[:, n, 0:b - a], k.ones, sq[:, c % 2, a:b],
                                            start=(c == 0), stop=(c == KT - 1))
                last.then_inc(mm_done, 1)

        @block.vector
        def _(dve):
            dve.wait_ge(mm_done, KT)
            nc.vector.tensor_scalar(rstd, k.psf[:, 0:T], 1.0 / D, EPS, ALU.mult, ALU.add).then_inc(ms_done, 1)
            dve.wait_ge(root_done, 1)
            nc.vector.reciprocal(rstd, rstd)
            dve.drain()
            for c in range(KT):
                nc.vector.tensor_tensor(h[:, c, :], h[:, c, :], rstd, ALU.mult).then_inc(scaled, 1)


def strip_matmuls(nc, k, u, w, src, chunks=CHUNKS):
    for n, (a, b) in enumerate(chunks):
        for c in range(KT):
            last = nc.tensor.matmul(k.ps[:, 3 * u + n, 0:b - a], w[:, c * P:(c + 1) * P], src[:, c, a:b],
                                    start=(c == 0), stop=(c == KT - 1))
    return last


def token_sums(nc, k, bank, src):
    for n in range(T // P):
        last = nc.tensor.matmul(k.ps[:, bank, 2 * n:2 * n + 2], src[:, n * P:(n + 1) * P], k.head_ones[:, 0::64],
                                start=True, stop=True)
    return last


def widen(nc, wide, small):
    return nc.vector.tensor_copy(wide.rearrange("p (a b) -> p a b", b=64), small.unsqueeze(2).to_broadcast([P, 2 * T // P, 64]))


def spread(nc, k, bank, wide):
    for n in range(T // P):
        last = nc.tensor.transpose(k.psf[:, bank * BANK + n * P:bank * BANK + (n + 1) * P], wide[:, n * P:(n + 1) * P], k.ident)
    return last


def acc(k, u):
    return k.psf[:, 3 * u * BANK:3 * u * BANK + T]


def dense_to_dram(nc, k, h, weights, n_strips, dst, mod_layer, chunked=False):
    strips, stage = k.arena.take(2, KT * P), k.arena.take(2, T)
    n = n_strips // 2
    per_turn = -(-MODS // n)
    turns = MODS // per_turn if mod_layer < k.depth else 0
    with Phase(nc) as es:
        sem = lambda n, credit=0: es.semaphore(n, credit)
        w_in = [sem(f"w_in{u}") for u in range(2)]
        mm_done = [sem(f"mm_done{u}", 1) for u in range(2)]
        ev_done = [sem(f"ev_done{u}", 1) for u in range(2)]
        stored = [sem(f"stored{u}", 16) for u in range(2)]
        if turns:
            hidden = HiddenModulation(nc, k, es, mod_layer, per_turn)

        def in_turns(eng, turn):
            if turns:
                with eng.Fori(0, turns) as i:
                    turn(i, True)
            if turns < n:
                with eng.Fori(turns, n) as i:
                    turn(i, False)
        block = es.block()

        @block.sync
        def _(sp):
            def turn(i, mod):
                for u in range(2):
                    sp.wait_ge(mm_done[u], i + 1)
                    sp.dma_start(strips[:, u, :], dram_tile(weights, i * 2 + u)).then_inc(w_in[u], 16)
                if mod:
                    hidden.sync_part(sp, i)
            in_turns(sp, turn)

        @block.tensor
        def _(pe):
            def turn(i, mod):
                for u in range(2):
                    pe.wait_ge(w_in[u], i * 16 + 16)
                    pe.wait_ge(ev_done[u], i + 1)
                    strip_matmuls(nc, k, u, strips[:, u, :], h).then_inc(mm_done[u], 1)
                if mod:
                    hidden.tensor_part(pe, i)
            in_turns(pe, turn)

        if turns:
            @block.vector
            def _(dve):
                with dve.Fori(0, turns) as i:
                    hidden.vector_part(dve, i)
                hidden.vector_end(dve)

        @block.scalar
        def _(act):
            with act.Fori(0, n_strips // 2) as i:
                for u in range(2):
                    act.wait_ge(mm_done[u], i + 2)
                    act.wait_ge(stored[u], i * 16 + 16)
                    out, in_ = stage[:, u, :], acc(k, u)
                    if chunked:
                        out = out.rearrange("p (s j) -> p j s", s=S)
                        in_ = in_.rearrange("p (j s) -> p j s", s=S)
                    nc.scalar.copy(out, in_).then_inc(ev_done[u], 1)
                    act.wait_ge(ev_done[u], i + 2)
                    act.dma_start(dram_tile(dst, i * 2 + u), stage[:, u, :]).then_inc(stored[u], 16)
            for u in range(2):
                act.wait_ge(stored[u], n_strips // 2 * 16 + 16)


def dense_residual(nc, k, layer, o, weights, src, dst, chunked=False):
    latents = dst.shape[-1] == NLAT
    first = NCTX if latents else 0
    chunks = [(NCTX, NCTX + BANK), (NCTX + BANK, T)] if latents else CHUNKS
    strips, stage, xin = k.arena.take(2, KT * P), k.arena.take(2, T), k.arena.take(2, T)
    n = KT // 2
    with Phase(nc) as es:
        sem = lambda n, credit=0: es.semaphore(n, credit)
        w_in = [sem(f"w_in{u}") for u in range(2)]
        x_in = [sem(f"x_in{u}") for u in range(2)]
        mm_done = [sem(f"mm_done{u}", 1) for u in range(2)]
        ev_done = [sem(f"ev_done{u}", 1) for u in range(2)]
        stored = [sem(f"stored{u}", 16) for u in range(2)]
        block = es.block()

        @block.sync
        def _(sp):
            with sp.Fori(0, n) as i:
                for u in range(2):
                    sp.wait_ge(mm_done[u], i + 1)
                    sp.dma_start(strips[:, u, :], dram_tile(weights, i * 2 + u)).then_inc(w_in[u], 16)
                    sp.wait_ge(ev_done[u], i + 1)
                    sp.dma_start(xin[:, u, first:T], dram_tile(src, i * 2 + u)[:, first:T]).then_inc(x_in[u], 16)

        @block.tensor
        def _(pe):
            with pe.Fori(0, n) as i:
                for u in range(2):
                    pe.wait_ge(w_in[u], i * 16 + 16)
                    pe.wait_ge(ev_done[u], i + 1)
                    strip_matmuls(nc, k, u, strips[:, u, :], o, chunks).then_inc(mm_done[u], 1)

        @block.vector
        def _(dve):
            with dve.Fori(0, n) as i:
                for u in range(2):
                    dve.wait_ge(mm_done[u], i + 2)
                    dve.wait_ge(x_in[u], i * 16 + 16)
                    dve.wait_ge(stored[u], i * 16 + 16)
                    for s, (a, b) in list(enumerate(SEGS))[int(latents):]:
                        gate = k.mod[:, bass.ds(i * 2 + (layer * MODS + 16 + u), 1), s]
                        out, prod, x = stage[:, u, a:b], acc(k, u)[:, a - first:b - first], xin[:, u, a:b]
                        if chunked:
                            out, x = (v.rearrange("p (j s) -> p j s", s=S) for v in (out, x))
                            prod = acc(k, u).rearrange("p (s j) -> p j s", s=S)[:, a // S:b // S, :]
                        last = nc.vector.scalar_tensor_tensor(out, prod, gate, x, ALU.mult, ALU.add)
                    last.then_inc(ev_done[u], 1)

        @block.scalar
        def _(act):
            with act.Fori(0, n) as i:
                for u in range(2):
                    act.wait_ge(ev_done[u], i + 2)
                    act.dma_start(dram_tile(dst, i * 2 + u), stage[:, u, first:T]).then_inc(stored[u], 16)
            for u in range(2):
                act.wait_ge(stored[u], n * 16 + 16)


GRID, ROWS, KH, KW = 64, NLAT // 64, 8, 16
NA_BIAS = 15 * GRID


def na_windows():
    units = []
    for r in range(ROWS):
        r0 = min(max(r - KH // 2, 0), ROWS - KH)
        units.append((NCTX + r * GRID, NCTX + r0 * GRID, (r0 - r + 7) * GRID))
    return units + [(q * GRID, None, 0) for q in range(NCTX // GRID)]


def na_attention(nc, k, o, qkvz):
    take = k.arena.take
    raws, biases = [take(4, T) for _ in range(2)], [take(NA_BIAS) for _ in range(2)]
    sq, rstd = take(2, T), take(2, T)
    v_even, v_odd = take(10, P), take(7, P)
    s_sb, p_sb = take(2, 768), take(2, 768)
    pt = take(2, 768)
    mx, sm = take(2, 1), take(2, 1)
    small = take(2, 2 * T // P)
    units = na_windows()
    NU = len(units)
    qg, kg = k.na_g[:, 0:1], k.na_g[:, 1:2]

    def value_blocks(key):
        ctx = [v_even[:, b, :] for b in range(2)]
        if key is None:
            return ctx
        b = (key - NCTX) // GRID
        return [(v_odd if b % 2 else v_even[:, 2:10, :])[:, b // 2 + n, :] for n in range(4)] + ctx

    with Phase(nc) as es:
        sem = lambda n, credit=0: es.semaphore(n, credit)
        tile_in = [sem(f"na_tile_in{b}") for b in range(2)]
        sq_ready, ms_mm, ms_ev, root, normed = (sem(x) for x in
            ("na_sq_ready", "na_ms_mm", "na_ms_ev", "na_root", "na_normed"))
        vt_mm, vt_ev, tile_done = sem("na_vt_mm"), sem("na_vt_ev"), sem("na_tile_done", 3)
        s_mm, s_ev, s_ctx, s_max, p_exp, p_ready, o_mm = (sem("na_" + x) for x in
            ("s_mm", "s_ev", "s_ctx", "s_max", "p_exp", "p_ready", "o_mm"))
        pt_mm, pt_ev, o_ev = (sem("na_" + x, 1) for x in ("pt_mm", "pt_ev", "o_ev"))
        gate_sig, wide, spread_mm = sem("na_gate_sig"), sem("na_rms_wide"), sem("na_rms_spread")
        block = es.block()

        @block.sync
        def _(sp):
            with sp.Fori(0, KT // 2) as pair:
                for b in range(2):
                    e, raw, bias = pair * 2 + b, raws[b], biases[b]
                    sp.wait_ge(tile_done, e * 2 + 1)
                    for n in range(4):
                        sp.dma_start(raw[:, n, :], dram_tile(qkvz, e + n * KT)).then_inc(tile_in[b], 16)
                    sp.dma_start(bias, dram_tile(k.na_bias, e)).then_inc(tile_in[b], 16)

        @block.tensor
        def _(pe):
            with pe.Fori(0, KT // 2) as pair:
                for b in range(2):
                    e, raw, bias = pair * 2 + b, raws[b], biases[b]
                    for n in range(2):
                        pe.wait_ge(sq_ready, e * 2 + n + 1)
                        token_sums(nc, k, 6 + n, sq[:, n, :]).then_inc(ms_mm, 1)
                    for n in range(2):
                        pe.wait_ge(wide, e * 2 + n + 1)
                        spread(nc, k, 3 * n, rstd[:, n, :]).then_inc(spread_mm, 1)
                    for n in range(17):
                        t0 = n * P if n < 10 else NCTX + GRID + (n - 10) * P
                        if n >= 2:
                            pe.wait_ge(vt_ev, e * 17 + n - 1)
                        if n == 0:
                            pe.wait_ge(tile_in[b], pair * 80 + 80)
                            pe.wait_ge(o_ev, e * NU + 1)
                        nc.tensor.transpose(k.ps[:, 6 + n % 2, 0:P], raw[:, 2, t0:t0 + P], k.ident).then_inc(vt_mm, 1)
                    pe.wait_ge(vt_ev, e * 17 + 17)
                    pe.wait_ge(normed, e * 2 + 2)

                    def scores(n):
                        q, key, _ = units[n]
                        if n >= 2:
                            pe.wait_ge(s_ev, e * ROWS + min(n - 1, ROWS))
                            pe.wait_ge(s_ctx, e * NU + n - 1)
                            hold(k, pe)
                        for h in range(2):
                            hp = slice(64 * h, 64 * h + 64)
                            if key is not None:
                                nc.tensor.matmul(k.ps[hp, 2 * (n % 2), :], raw[hp, 0, q:q + 64], raw[hp, 1, key:key + 512],
                                                 start=True, stop=True)
                            last = nc.tensor.matmul(k.ps[hp, 2 * (n % 2) + 1, 0:NCTX], raw[hp, 0, q:q + 64],
                                                    raw[hp, 1, 0:NCTX], start=True, stop=True)
                        last.then_inc(s_mm, 1)

                    def attend(n):
                        key = units[n][1]
                        vb = value_blocks(key)
                        off = 0 if key is not None else 512
                        pe.wait_ge(p_ready, e * NU + n + 1)
                        if n >= 1:
                            pe.wait_ge(pt_ev, e * NU + n + 1)
                        for m in range(len(vb)):
                            last = nc.tensor.transpose(k.psf[:, 4 * BANK + m * P:4 * BANK + (m + 1) * P],
                                                       p_sb[:, n % 2, off + m * P:off + (m + 1) * P], k.ident)
                        last.then_inc(pt_mm, 1)
                        if n + 2 < NU:
                            scores(n + 2)
                        pe.wait_ge(pt_ev, e * NU + n + 2)
                        if n >= 2:
                            pe.wait_ge(o_ev, e * NU + n)
                        for m, v in enumerate(vb):
                            last = nc.tensor.matmul(k.ps[:, 6 + n % 2, 0:P], v, pt[:, n % 2, m * P:(m + 1) * P],
                                                    start=(m == 0), stop=(m == len(vb) - 1))
                        last.then_inc(o_mm, 1)

                    pe.wait_ge(ms_ev, e * 2 + 2)
                    hold(k, pe)
                    scores(0)
                    scores(1)
                    for n in range(NU):
                        attend(n)
                    pe.drain().then_inc(tile_done, 1)

        @block.scalar
        def _(act):
            with act.Fori(0, KT // 2) as pair:
                for b in range(2):
                    e, raw, bias = pair * 2 + b, raws[b], biases[b]
                    act.wait_ge(tile_in[b], pair * 80 + 80)
                    act.wait_ge(o_ev, e * NU + 1)
                    for n in range(2):
                        nc.scalar.activation(sq[:, n, :], raw[:, n, :], ACT.Square).then_inc(sq_ready, 1)
                    act.wait_ge(ms_ev, e * 2 + 2)
                    nc.scalar.activation(small, small, ACT.Sqrt).then_inc(root, 1)
                    act.wait_ge(normed, e * 2 + 2)
                    nc.scalar.activation(rstd[:, 0, :], raw[:, 3, :], ACT.Sigmoid).then_inc(gate_sig, 1)
                    for n in range(17):
                        dst = v_even[:, n, :] if n < 10 else v_odd[:, n - 10, :]
                        act.wait_ge(vt_mm, e * 17 + n + 1)
                        nc.scalar.copy(dst, k.ps[:, 6 + n % 2, 0:P]).then_inc(vt_ev, 1)
                    def ctx_scores(n):
                        act.wait_ge(s_mm, e * NU + n + 1)
                        nc.scalar.mul(s_sb[:, n % 2, 512:768], k.ps[:, 2 * (n % 2) + 1, 0:NCTX], NA_SCALE).then_inc(s_ctx, 1)

                    def exponentials(n):
                        off = 0 if units[n][1] is not None else 512
                        act.wait_ge(s_max, e * NU + n + 1)
                        if n >= 2:
                            act.wait_ge(pt_mm, e * NU + n)
                        nc.scalar.activation(p_sb[:, n % 2, off:768], s_sb[:, n % 2, off:768], ACT.Exp, bias=mx[:, n % 2, :],
                                             accum_out=sm[:, n % 2, :]).then_inc(p_exp, 1)

                    ctx_scores(0)
                    ctx_scores(1)
                    exponentials(0)
                    for n in range(NU):
                        if n + 1 < NU:
                            exponentials(n + 1)
                        act.wait_ge(pt_mm, e * NU + n + 2)
                        nb = 768 if units[n][1] is not None else 256
                        if n >= 2:
                            act.wait_ge(o_mm, e * NU + n - 1)
                        nc.scalar.copy(pt[:, n % 2, 0:nb], k.psf[:, 4 * BANK:4 * BANK + nb]).then_inc(pt_ev, 1)
                        if n + 2 < NU:
                            ctx_scores(n + 2)

        @block.vector
        def _(dve):
            with dve.Fori(0, KT // 2) as pair:
                for b in range(2):
                    e, raw, bias = pair * 2 + b, raws[b], biases[b]
                    for n in range(2):
                        dve.wait_ge(ms_mm, e * 2 + n + 1)
                        nc.vector.tensor_scalar(small[:, n, :], k.ps[:, 6 + n, 0:2 * T // P], 1.0 / 64, EPS,
                                                ALU.mult, ALU.add).then_inc(ms_ev, 1)
                    dve.wait_ge(root, e + 1)
                    nc.vector.reciprocal(small, small)
                    dve.drain()
                    for n in range(2):
                        widen(nc, rstd[:, n, :], small[:, n, :]).then_inc(wide, 1)
                    for n, g in enumerate((qg, kg)):
                        dve.wait_ge(spread_mm, e * 2 + n + 1)
                        nc.vector.scalar_tensor_tensor(raw[:, n, :], raw[:, n, :], g, k.psf[:, 3 * n * BANK:3 * n * BANK + T],
                                                       ALU.mult, ALU.mult)
                        dve.drain().then_inc(normed, 1)
                    dve.wait_ge(gate_sig, e + 1)
                    nc.vector.tensor_tensor(raw[:, 3, :], raw[:, 3, :], rstd[:, 0, :], ALU.mult)
                    dve.drain()

                    def outputs(n):
                        q = units[n][0]
                        dve.wait_ge(o_mm, e * NU + n + 1)
                        for h in range(2):
                            hp = slice(64 * h, 64 * h + 64)
                            last = nc.vector.tensor_tensor(o[hp, bass.ds(e, 1), q:q + 64].rearrange("p a b -> p (a b)"),
                                                           k.ps[hp, 6 + n % 2, 64 * h:64 * h + 64], raw[hp, 3, q:q + 64], ALU.mult)
                        last.then_inc(o_ev, 1)

                    def maxima(n):
                        key, bcol = units[n][1:]
                        off = 0 if key is not None else 512
                        dve.wait_ge(s_mm, e * NU + n + 1)
                        if n >= 2:
                            dve.wait_ge(p_exp, e * NU + n - 1)
                        if key is not None:
                            nc.vector.scalar_tensor_tensor(s_sb[:, n % 2, 0:512], k.ps[:, 2 * (n % 2), :], NA_SCALE,
                                                           bias[:, bcol:bcol + 512], ALU.mult, ALU.add).then_inc(s_ev, 1)
                            dve.drain()
                        dve.wait_ge(s_ctx, e * NU + n + 1)
                        nc.vector.reduce_max(mx[:, n % 2, :], s_sb[:, n % 2, off:768], AXX)
                        dve.drain()
                        nc.vector.tensor_scalar(mx[:, n % 2, :], mx[:, n % 2, :], -1.0, None, ALU.mult).then_inc(s_max, 1)

                    maxima(0)
                    for n in range(NU):
                        off = 0 if units[n][1] is not None else 512
                        if n + 1 < NU:
                            maxima(n + 1)
                        dve.wait_ge(p_exp, e * NU + n + 1)
                        nc.vector.reciprocal(sm[:, n % 2, :], sm[:, n % 2, :])
                        dve.drain()
                        nc.vector.tensor_scalar(p_sb[:, n % 2, off:768], p_sb[:, n % 2, off:768], sm[:, n % 2, :], None,
                                                ALU.mult).then_inc(p_ready, 1)
                        if n >= 1:
                            outputs(n - 1)
                    outputs(NU - 1)
                    dve.drain().then_inc(tile_done, 1)


NA_SCALE = 64 ** -0.5


S = 8
NJ = T // S
JC = NCTX // S
G, GP, NS = 64, 32, 64
TWO_PI = 2 * np.pi
PI_A, PI_B = 6.28125, float(np.float32(TWO_PI - 6.28125) // 2 ** -21 * 2 ** -21)
PI_C = float(TWO_PI - PI_A - PI_B)




def s5_discretise(nc, k, s5):
    take = k.arena.take
    N = 2 * GP
    t = [take(N) for _ in range(12)]
    (lr, li, step, th, y, em, mag, sn, cs, hs, den, tmp) = t
    turns = take(N)
    qr, qi, ar1, ai = (take(N) for _ in range(4))
    V = nc.vector
    with Phase(nc) as es:
        sem = lambda n: es.semaphore(n)
        par_in, stepped, angle, waves, disc = (sem("s5_" + x) for x in ("par_in", "stepped", "angle", "waves", "disc"))
        block = es.block()

        @block.sync
        def _(sp):
            for dst, src in ((lr, "s5_lr"), (li, "s5_li"), (step, "s5_dt"), (flat(s5.br), "s5_br"),
                             (flat(s5.bi), "s5_bi"), (flat(s5.cr), "s5_cr"), (flat(s5.ci), "s5_ci"), (s5.dsk, "s5_dsk")):
                sp.dma_start(dst, k.A[src]).then_inc(par_in, 16)

        @block.scalar
        def _(act):
            act.wait_ge(par_in, 128)
            nc.scalar.activation(step, step, ACT.Exp).then_inc(stepped, 1)
            act.wait_ge(angle, 1)
            nc.scalar.activation(mag, y, ACT.Exp).then_inc(waves, 1)
            nc.scalar.activation(sn, th, ACT.Sin).then_inc(waves, 1)
            nc.scalar.activation(cs, tmp, ACT.Sin).then_inc(waves, 1)
            nc.scalar.activation(hs, th, ACT.Sin, scale=0.5).then_inc(waves, 1)

        @block.vector
        def _(dve):
            def tt(out, a, b, op):
                V.tensor_tensor(out, a, b, op)
                dve.drain()

            def ts(out, a, s1, s2, o1, o2=ALU.bypass):
                V.tensor_scalar(out, a, s1, s2, o1, o2)
                dve.drain()

            def stt(out, a, s, b, o1, o2):
                V.scalar_tensor_tensor(out, a, s, b, o1, o2)
                dve.drain()

            def wrap(x, scratch):
                ts(scratch, x, float(np.pi), TWO_PI, ALU.is_gt, ALU.mult)
                tt(x, x, scratch, ALU.subtract)
                ts(scratch, x, -float(np.pi), TWO_PI, ALU.is_lt, ALU.mult)
                tt(x, x, scratch, ALU.add)

            dve.wait_ge(stepped, 1)
            tt(y, lr, step, ALU.mult)
            tt(th, li, step, ALU.mult)
            ts(tmp, th, 1 / TWO_PI, None, ALU.mult)
            V.tensor_copy(turns.bitcast(I32), tmp)
            dve.drain()
            V.tensor_copy(tmp, turns.bitcast(I32))
            dve.drain()
            for part in (PI_A, PI_B, PI_C):
                stt(th, tmp, -part, th, ALU.mult, ALU.add)
            wrap(th, tmp)
            ts(tmp, th, float(np.pi / 2), None, ALU.add)
            wrap(tmp, den)
            lim = float(np.float32(3.1415925))
            ts(th, th, lim, -lim, ALU.min, ALU.max)
            V.tensor_scalar(tmp, tmp, lim, -lim, ALU.min, ALU.max).then_inc(angle, 1)
            V.memset(em, 1.0)
            dve.drain()
            for n in range(9, 1, -1):
                tt(em, em, y, ALU.mult)
                ts(em, em, 1.0 / n, 1.0, ALU.mult, ALU.add)
            tt(em, em, y, ALU.mult)
            dve.wait_ge(waves, 4)
            ts(mag, mag, -1.0, None, ALU.add)
            tt(den, y, y, ALU.mult)
            ts(turns.bitcast(I32), den, 0.25, None, ALU.is_ge)
            V.copy_predicated(em, turns.bitcast(I32), mag)
            dve.drain()
            ts(mag, em, 1.0, None, ALU.add)
            tt(ai, mag, sn, ALU.mult)
            tt(hs, hs, hs, ALU.mult)
            tt(ar1, em, cs, ALU.mult)
            stt(ar1, hs, -2.0, ar1, ALU.mult, ALU.add)
            tt(den, lr, lr, ALU.mult)
            tt(tmp, li, li, ALU.mult)
            tt(den, den, tmp, ALU.add)
            V.reciprocal(den, den)
            dve.drain()
            tt(qr, ar1, lr, ALU.mult)
            tt(tmp, ai, li, ALU.mult)
            tt(qr, qr, tmp, ALU.add)
            tt(qr, qr, den, ALU.mult)
            tt(qi, ai, lr, ALU.mult)
            tt(tmp, ar1, li, ALU.mult)
            tt(qi, qi, tmp, ALU.subtract)
            tt(qi, qi, den, ALU.mult)
            V.memset(s5.AR[:, 0, :], 1.0)
            V.memset(s5.AI[:, 0, :], 0.0)
            ts(s5.AR[:, 1, :], ar1, 1.0, None, ALU.add)
            V.tensor_copy(s5.AI[:, 1, :], ai)
            dve.drain()
            for n in range(2, S + 1):
                a, b = n // 2, n - n // 2
                tt(s5.AR[:, n, :], s5.AR[:, a, :], s5.AR[:, b, :], ALU.mult)
                tt(tmp, s5.AI[:, a, :], s5.AI[:, b, :], ALU.mult)
                tt(s5.AR[:, n, :], s5.AR[:, n, :], tmp, ALU.subtract)
                tt(s5.AI[:, n, :], s5.AR[:, a, :], s5.AI[:, b, :], ALU.mult)
                tt(tmp, s5.AI[:, a, :], s5.AR[:, b, :], ALU.mult)
                tt(s5.AI[:, n, :], s5.AI[:, n, :], tmp, ALU.add)
            V.tensor_copy(s5.coef[:, 0, 0, :], s5.AR[:, S, :])
            V.tensor_copy(s5.coef[:, 0, 1, :], s5.AR[:, S, :])
            V.tensor_copy(s5.coef[:, 1, 0, :], s5.AI[:, S, :])
            ts(s5.coef[:, 1, 1, :], s5.AI[:, S, :], -1.0, None, ALU.mult)
            for d in range(2):
                q_r = qr[:, d * GP:(d + 1) * GP].unsqueeze(2).to_broadcast([P, GP, 16])
                q_i = qi[:, d * GP:(d + 1) * GP].unsqueeze(2).to_broadcast([P, GP, 16])
                bbr, bbi = s5.bb[:, 0, d * GP:(d + 1) * GP, :], s5.bb[:, 1, d * GP:(d + 1) * GP, :]
                tt(bbr, s5.br, q_r, ALU.mult)
                tt(s5.tmpb, s5.bi, q_i, ALU.mult)
                tt(bbr, bbr, s5.tmpb, ALU.subtract)
                tt(bbi, s5.bi, q_r, ALU.mult)
                tt(s5.tmpb, s5.br, q_i, ALU.mult)
                tt(bbi, bbi, s5.tmpb, ALU.add)


def s5_matrices(nc, k, s5, u_d):
    take = k.arena.take
    ca, zb, zbt = take(2, 4, P), take(2, 4, P), take(2, 4, P)
    prod = take(2, P)
    prod2 = take(2, P)
    carried = take(2, 4, 16)
    kst = take(2, BANK)
    upair = take(2, 2, NJ)
    zero = take(P)
    V, SC = nc.vector, nc.scalar
    with Phase(nc) as es:
        sem = lambda n, credit=0: es.semaphore(n, credit)
        u_in, zeroed, zero_out = sem("s5_u_in"), sem("s5_zeroed"), sem("s5_zero_out")
        par = [sem(f"s5_pair_par{u}") for u in range(2)]
        ca_ready = [sem(f"s5_ca_ready{u}") for u in range(2)]
        zb_ready = [sem(f"s5_zb_ready{u}", 1) for u in range(2)]
        ca_out = [sem(f"s5_ca_out{u}", 16) for u in range(2)]
        k_mm = [sem(f"s5_k_mm{u}", 1) for u in range(2)]
        k_ev = [sem(f"s5_k_ev{u}", 1) for u in range(2)]
        k_out = [sem(f"s5_k_out{u}", 32) for u in range(2)]
        zt_mm = [sem(f"s5_zt_mm{u}", 1) for u in range(2)]
        zt_ev = [sem(f"s5_zt_ev{u}", 1) for u in range(2)]
        z_mm = [sem(f"s5_z_mm{u}", 1) for u in range(2)]
        z_ev = [sem(f"s5_z_ev{u}", 1) for u in range(2)]
        block = es.block()

        @block.sync
        def _(sp):
            for s in range(S):
                sp.dma_start(s5.u[16 * s:16 * s + 16, :, :],
                             u_d[0:KT].rearrange("k q t -> (k q) t").rearrange("(g c) (s j) -> s c g j", c=16, s=S)[s]).then_inc(u_in, 16)
            sp.wait_ge(zeroed, 1)
            for d in range(2):
                side = s5.kd[d][:, :, :, d * P:(d + 1) * P]
                sp.dma_start(side.rearrange("q h c l -> (q h c) l").rearrange("(a b) l -> b a l", b=P),
                             zero.unsqueeze(1).to_broadcast([P, GP * 2 * 16 // P, P])).then_inc(zero_out, 16)
            with sp.Fori(0, GP // 2) as i:
                for u in range(2):
                    sp.wait_ge(ca_ready[u], i + 1)
                    sp.dma_start(dram_tile(s5.cad, i * 2 + u), ca[:, u].rearrange("p a b -> p (a b)")).then_inc(ca_out[u], 16)
                    sp.wait_ge(k_ev[u], i + 2)
                    for d in range(2):
                        sp.dma_start(s5.kd[d][bass.ds(i * 2 + u, 1), :, :, (1 - d) * P:(2 - d) * P]
                                     .rearrange("q h c l -> (q c) h l"),
                                     kst[0:16, u, d * 2 * P:(d + 1) * 2 * P].rearrange("c (h l) -> c h l", h=2)).then_inc(k_out[u], 16)
            for u in range(2):
                sp.wait_ge(ca_out[u], 16 * GP // 2 + 16)
                sp.wait_ge(k_out[u], 32 * GP // 2 + 32)
            sp.wait_ge(zero_out, 32)

        def row(v, n):
            return v.unsqueeze(1).to_broadcast([P, n, 16])

        def lag(v):
            return v.unsqueeze(2).to_broadcast([P, v.shape[1], 16])

        @block.vector
        def _(dve):
            V.memset(zero, 0.0).then_inc(zeroed, 1)
            with dve.Fori(0, GP // 2) as i:
                for u in range(2):
                    dve.wait_ge(par[u], i + 1)
                    dve.wait_ge(ca_out[u], i * 16 + 16)
                    dve.wait_ge(k_mm[u], i + 1)
                    for d in range(2):
                        pr = s5.pw[:, u, d, 0, :]
                        pi = s5.pw[:, u, d, 1, :]
                        e_r, e_i = (pr[:, 1:9], pi[:, 1:9]) if d == 0 else (pr[:, 8:0:-1], pi[:, 8:0:-1])
                        cr, ci = row(s5.cpair[:, u, 0, :], S), row(s5.cpair[:, u, 1, :], S)
                        o_r = ca[:, u, 2 * d, :].rearrange("p (s c) -> p s c", c=16)
                        o_i = ca[:, u, 2 * d + 1, :].rearrange("p (s c) -> p s c", c=16)
                        t0 = prod[:, 0, :].rearrange("p (s c) -> p s c", c=16)
                        t1 = prod[:, 1, :].rearrange("p (s c) -> p s c", c=16)
                        t2 = prod2[:, 0, :].rearrange("p (s c) -> p s c", c=16)
                        t3 = prod2[:, 1, :].rearrange("p (s c) -> p s c", c=16)
                        V.tensor_tensor(t0, cr, lag(e_r), ALU.mult)
                        V.tensor_tensor(t1, ci, lag(e_i), ALU.mult)
                        V.tensor_tensor(t2, cr, lag(e_i), ALU.mult)
                        V.tensor_tensor(t3, ci, lag(e_r), ALU.mult)
                        dve.drain()
                        V.tensor_tensor(o_r, t0, t1, ALU.subtract)
                        V.scalar_tensor_tensor(o_i, t2, -1.0, t3, ALU.mult, ALU.subtract)
                        dve.drain()
                        e_r, e_i = (pr[:, 0:8], pi[:, 0:8]) if d == 0 else (pr[:, 7::-1], pi[:, 7::-1])
                        o_r = s5.cl[:, u, 2 * d, :].rearrange("p (s c) -> p s c", c=16)
                        o_i = s5.cl[:, u, 2 * d + 1, :].rearrange("p (s c) -> p s c", c=16)
                        V.tensor_tensor(t0, cr, lag(e_r), ALU.mult)
                        V.tensor_tensor(t1, ci, lag(e_i), ALU.mult)
                        V.tensor_tensor(t2, cr, lag(e_i), ALU.mult)
                        V.tensor_tensor(t3, ci, lag(e_r), ALU.mult)
                        dve.drain()
                        V.tensor_tensor(o_r, t0, t1, ALU.subtract)
                        V.scalar_tensor_tensor(o_i, t2, -1.0, t3, ALU.mult, ALU.subtract)
                        dve.drain()
                    dve.nop().then_inc(ca_ready[u], 1)
                    dve.wait_ge(zt_mm[u], i + 1)
                    for d in range(2):
                        pr = s5.pw[:, u, d, 0, :]
                        pi = s5.pw[:, u, d, 1, :]
                        e_r, e_i = (pr[:, 7::-1], pi[:, 7::-1]) if d == 0 else (pr[:, 0:8], pi[:, 0:8])
                        br, bi = row(carried[:, u, 2 * d, :], S), row(carried[:, u, 2 * d + 1, :], S)
                        o_r = zb[:, u, 2 * d, :].rearrange("p (s c) -> p s c", c=16)
                        o_i = zb[:, u, 2 * d + 1, :].rearrange("p (s c) -> p s c", c=16)
                        t0 = prod[:, 0, :].rearrange("p (s c) -> p s c", c=16)
                        t1 = prod[:, 1, :].rearrange("p (s c) -> p s c", c=16)
                        t2 = prod2[:, 0, :].rearrange("p (s c) -> p s c", c=16)
                        t3 = prod2[:, 1, :].rearrange("p (s c) -> p s c", c=16)
                        V.tensor_tensor(t0, br, lag(e_r), ALU.mult)
                        V.tensor_tensor(t1, bi, lag(e_i), ALU.mult)
                        V.tensor_tensor(t2, br, lag(e_i), ALU.mult)
                        V.tensor_tensor(t3, bi, lag(e_r), ALU.mult)
                        dve.drain()
                        V.tensor_tensor(o_r, t0, t1, ALU.subtract)
                        V.tensor_tensor(o_i, t2, t3, ALU.add)
                        dve.drain()
                    dve.nop().then_inc(zb_ready[u], 1)

        @block.scalar
        def _(act):
            def pair_parameters(i, u):
                gp = i * 2 + u
                for d in range(2):
                    for r in range(2):
                        SC.copy(carried[:, u, 2 * d + r, :], s5.bb[:, r, bass.ds(gp + d * GP, 1), :].rearrange("p a b -> p (a b)"))
                        SC.copy(s5.pw[:, u, d, r, :], (s5.AR, s5.AI)[r][:, :, bass.ds(gp + d * GP, 1)].rearrange("p a b -> p (a b)"))
                SC.copy(s5.cpair[:, u, 0, :], s5.cr[:, bass.ds(gp, 1), :].rearrange("p a b -> p (a b)"))
                SC.copy(s5.cpair[:, u, 1, :], s5.ci[:, bass.ds(gp, 1), :].rearrange("p a b -> p (a b)"))
                SC.copy(upair[:, u], s5.u[:, bass.ds(gp * 2, 2), :])
                act.drain().then_inc(par[u], 1)

            act.wait_ge(u_in, 16 * S)
            hold(k, act)
            def next_parameters(i, u):
                act.wait_ge(zb_ready[u], i + 1)
                act.wait_ge(k_mm[u], i + 1)
                act.wait_ge(z_mm[u], i + 1)
                hold(k, act)
                pair_parameters(i, u)

            def evict(i, u):
                gp = i * 2 + u
                act.wait_ge(k_mm[u], i + 2)
                act.wait_ge(k_out[u], i * 32 + 32)
                for g in range(2):
                    last = SC.copy(kst[0:16, u, :].rearrange("p (d h l) -> p d h l", d=2, h=2)[:, :, g, :],
                                   k.ps[0:16, 4 * u + g, 0:2 * P].rearrange("p (d l) -> p d l", d=2))
                last.then_inc(k_ev[u], 1)
                act.wait_ge(zt_mm[u], i + 2)
                SC.copy(zbt[:, u, :, :].rearrange("p a b -> p (a b)"), k.ps[:, 4 * u + 1, :]).then_inc(zt_ev[u], 1)
                act.wait_ge(z_mm[u], i + 2)
                zf = k.ps[:, 4 * u + 2, 0:2 * NJ].rearrange("p (r j) -> p r j", r=2)
                zr = k.ps[:, 4 * u + 3, 0:2 * NJ].rearrange("p (r j) -> p r j", r=2)
                hold(k, act)
                SC.copy(s5.X[:, :, bass.ds(gp, 1), 1:NJ + 1].rearrange("p r g j -> p r (g j)"), zf)
                SC.copy(s5.X[:, :, bass.ds(gp + GP, 1), 1:JC + 1].rearrange("p r g j -> p r (g j)"), zr[:, :, JC - 1::-1])
                SC.copy(s5.X[:, :, bass.ds(gp + GP, 1), JC + 1:NJ + 1].rearrange("p r g j -> p r (g j)"),
                        zr[:, :, NJ - 1:JC - 1:-1])
                act.drain().then_inc(z_ev[u], 1)

            for u in range(2):
                next_parameters(0, u)
            with act.Fori(0, GP // 2 - 1) as i:
                for u in range(2):
                    evict(i, u)
                    next_parameters(i + 1, u)
            for u in range(2):
                evict(GP // 2 - 1, u)

        @block.tensor
        def _(pe):
            pe.wait_ge(u_in, 16 * S)
            with pe.Fori(0, GP // 2) as i:
                for u in range(2):
                    gp = i * 2 + u
                    pe.wait_ge(ca_ready[u], i + 1)
                    pe.wait_ge(k_ev[u], i + 1)
                    pe.wait_ge(zt_ev[u], i + 1)
                    hold(k, pe)
                    for d in range(2):
                        for g in range(2):
                            hp = slice(64 * g, 64 * g + 64)
                            for r in range(2):
                                last = nc.tensor.matmul(k.ps[0:16, 4 * u + g, d * P:(d + 1) * P],
                                                        carried[hp, u, 2 * d + r, :], s5.cl[hp, u, 2 * d + r, :],
                                                        start=(r == 0), stop=(r == 1))
                    last.then_inc(k_mm[u], 1)
                    pe.wait_ge(zb_ready[u], i + 2)
                    pe.wait_ge(k_ev[u], i + 2)
                    for q in range(4):
                        last = nc.tensor.transpose(k.ps[:, 4 * u + 1, q * P:(q + 1) * P], zb[:, u, q, :], k.ident)
                    last.then_inc(zt_mm[u], 1)
                    pe.wait_ge(zt_ev[u], i + 2)
                    pe.wait_ge(z_ev[u], i + 1)
                    hold(k, pe)
                    for d in range(2):
                        for r in range(2):
                            for g in range(2):
                                last = nc.tensor.matmul(
                                    k.ps[64 * g:64 * g + 64, 4 * u + 2 + d, r * NJ:(r + 1) * NJ],
                                    zbt[:, u, 2 * d + r, 64 * g:64 * g + 64],
                                    upair[:, u, g, :], start=True, stop=True)
                    last.then_inc(z_mm[u], 1)


def s5_scan(nc, k, s5):
    term = k.arena.take(4, 2 * GP)
    sw = k.arena.take(2, 2 * GP)
    V = nc.vector
    with Phase(nc) as es:
        t_in = es.semaphore("s5_toeplitz_in")
        block = es.block()

        @block.sync
        def _(sp):
            for d in range(2):
                for s in range(S):
                    at = (S - s if d == 0 else S - 1 - s) * 16
                    sp.dma_start(s5.T[16 * s:16 * s + 16, d],
                                 s5.kd[d][:, :, :, at:at + P].rearrange("q h c l -> c (q h) l")).then_inc(t_in, 16)
            sp.wait_ge(t_in, 16 * 2 * S)

        @block.vector
        def _(dve):
            V.memset(s5.X[:, :, :, 0:1], 0.0)
            dve.drain()
            with dve.Fori(0, NJ) as i:
                prev = s5.X[:, :, :, bass.ds(i, 1)].rearrange("p r g j -> p r (g j)")
                nxt = s5.X[:, :, :, bass.ds(i + 1, 1)].rearrange("p r g j -> p r (g j)")
                V.tensor_tensor(term.rearrange("p (a b) c -> p a b c", a=2), prev.unsqueeze(1).to_broadcast([P, 2, 2, prev.shape[2]]),
                                s5.coef, ALU.mult)
                dve.drain()
                V.tensor_tensor(sw, term[:, 0:2, :], term[:, 3:1:-1, :], ALU.add)
                dve.drain()
                V.tensor_tensor(nxt, nxt, sw, ALU.add)
                dve.drain()


def s5_outputs(nc, k, s5, yd):
    take = k.arena.take
    cas, tsum = take(2, 4 * P), take(2, 2 * P)
    xp = take(2, 4, NJ)
    yst = take(2, 2, NJ)
    dpair = take(2, 2)
    V, SC = nc.vector, nc.scalar
    with Phase(nc) as es:
        sem = lambda n, credit=0: es.semaphore(n, credit)
        ca_in = [sem(f"s5_ca_in{u}") for u in range(2)]
        t_ready = [sem(f"s5_t_ready{u}") for u in range(2)]
        x_ready = [sem(f"s5_x_ready{u}") for u in range(2)]
        y_mm = [sem(f"s5_y_mm{u}", 1) for u in range(2)]
        y_ev = [sem(f"s5_y_ev{u}", 1) for u in range(2)]
        y_act = [sem(f"s5_y_act{u}") for u in range(2)]
        y_out = [sem(f"s5_y_out{u}", 16) for u in range(2)]
        block = es.block()

        @block.sync
        def _(sp):
            with sp.Fori(0, GP // 2) as i:
                for u in range(2):
                    sp.wait_ge(y_mm[u], i + 1)
                    sp.dma_start(cas[:, u, :], dram_tile(s5.cad, i * 2 + u)).then_inc(ca_in[u], 16)

        @block.vector
        def _(dve):
            with dve.Fori(0, GP // 2) as i:
                for u in range(2):
                    gp = i * 2 + u
                    dve.wait_ge(y_mm[u], i + 1)
                    V.tensor_tensor(tsum[:, u, :], s5.T[:, 0, bass.ds(gp * 2, 2), :].rearrange("p a b -> p (a b)"),
                                    s5.T[:, 1, bass.ds(gp * 2, 2), :].rearrange("p a b -> p (a b)"), ALU.add).then_inc(t_ready[u], 1)
                for u in range(2):
                    gp = i * 2 + u
                    dve.wait_ge(y_mm[u], i + 2)
                    dve.wait_ge(y_out[u], i * 16 + 16)
                    for g in range(2):
                        last = V.scalar_tensor_tensor(yst[:, u, g, :], s5.u[:, bass.ds(gp * 2 + g, 1), :].rearrange("p a b -> p (a b)"),
                                                      s5.dsk[:, bass.ds(gp * 2 + g, 1)], k.ps[:, 2 * u + g, 0:NJ],
                                                      ALU.mult, ALU.add)
                    last.then_inc(y_ev[u], 1)

        @block.scalar
        def _(act):
            with act.Fori(0, GP // 2) as i:
                for u in range(2):
                    gp = i * 2 + u
                    act.wait_ge(y_mm[u], i + 1)
                    hold(k, act)
                    SC.copy(xp[:, u, 0:2, :], s5.X[:, :, bass.ds(gp, 1), 0:NJ].rearrange("p r g j -> p r (g j)"))
                    SC.copy(xp[:, u, 2:4, JC - 1::-1], s5.X[:, :, bass.ds(gp + GP, 1), 0:JC].rearrange("p r g j -> p r (g j)"))
                    SC.copy(xp[:, u, 2:4, NJ - 1:JC - 1:-1], s5.X[:, :, bass.ds(gp + GP, 1), JC:NJ].rearrange("p r g j -> p r (g j)"))
                    act.drain().then_inc(x_ready[u], 1)
                for u in range(2):
                    act.wait_ge(y_ev[u], i + 2)
                    SC.activation(yst[:, u], yst[:, u], ACT.Gelu_apprx_tanh).then_inc(y_act[u], 1)
                    act.wait_ge(y_act[u], i + 1)
                    act.dma_start(dram_tile(yd, i * 2 + u), yst[:, u].rearrange("p g j -> p (g j)")).then_inc(y_out[u], 16)
            for u in range(2):
                act.wait_ge(y_out[u], 16 * GP // 2 + 16)

        @block.tensor
        def _(pe):
            with pe.Fori(0, GP // 2) as i:
                for u in range(2):
                    gp = i * 2 + u
                    pe.wait_ge(ca_in[u], i * 16 + 16)
                    pe.wait_ge(t_ready[u], i + 1)
                    pe.wait_ge(x_ready[u], i + 1)
                    pe.wait_ge(y_ev[u], i + 1)
                    for g in range(2):
                        hp = slice(64 * g, 64 * g + 64)
                        o = k.ps[:, 2 * u + g, 0:NJ]
                        nc.tensor.matmul(o, tsum[:, u, g * P:(g + 1) * P],
                                         s5.u[:, bass.ds(gp * 2 + g, 1), :].rearrange("p a b -> p (a b)"), start=True, stop=False)
                        for q in range(4):
                            last = nc.tensor.matmul(o, cas[hp, u, q * P:(q + 1) * P], xp[hp, u, q, :],
                                                    start=False, stop=(q == 3))
                    last.then_inc(y_mm[u], 1)


def s5_glu(nc, k, y, o, weights, z_d, yd):
    strips_, zt, sg, g = (k.arena.take(2, KT * P), k.arena.take(2, T), k.arena.take(2, T), k.arena.take(2, T))
    V, SC = nc.vector, nc.scalar
    with Phase(nc) as es:
        sem = lambda n, credit=0: es.semaphore(n, credit)
        y_in = sem("glu_y_in")
        w_in = [sem(f"glu_w_in{u}") for u in range(2)]
        z_in = [sem(f"glu_z_in{u}") for u in range(2)]
        mm_done = [sem(f"glu_mm_done{u}", 1) for u in range(2)]
        sig = [sem(f"glu_sig{u}", 1) for u in range(2)]
        gated = [sem(f"glu_gated{u}", 1) for u in range(2)]
        block = es.block()

        @block.sync
        def _(sp):
            for g in range(G):
                sp.dma_start(y[16 * (g % 8):16 * (g % 8) + 16, g // 8, :].rearrange("c (t j) -> c t j", t=S),
                             yd[g // 2].rearrange("(t c) (g j) -> g c t j", c=16, g=2)[g % 2]).then_inc(y_in, 16)
            with sp.Fori(0, KT // 2) as i:
                for u in range(2):
                    sp.wait_ge(mm_done[u], i + 1)
                    sp.dma_start(strips_[:, u, :], dram_tile(weights, i * 2 + u)).then_inc(w_in[u], 16)
                    sp.wait_ge(gated[u], i + 1)
                    sp.dma_start(zt[:, u, :], dram_tile(z_d, i * 2 + (KT + u))).then_inc(z_in[u], 16)

        @block.tensor
        def _(pe):
            pe.wait_ge(y_in, 16 * G)
            hold(k, pe)
            with pe.Fori(0, KT // 2) as i:
                for u in range(2):
                    pe.wait_ge(w_in[u], i * 16 + 16)
                    pe.wait_ge(sig[u], i + 1)
                    strip_matmuls(nc, k, u, strips_[:, u, :], y).then_inc(mm_done[u], 1)

        @block.scalar
        def _(act):
            with act.Fori(0, KT // 2) as i:
                for u in range(2):
                    act.wait_ge(z_in[u], i * 16 + 16)
                    act.wait_ge(gated[u], i + 1)
                    SC.activation(g[:, u, :], zt[:, u, :], ACT.Sigmoid)
                    act.wait_ge(mm_done[u], i + 2)
                    SC.activation(sg[:, u, :], acc(k, u), ACT.Sigmoid, bias=k.b_glu[:, bass.ds(i * 2 + u, 1)]).then_inc(sig[u], 1)

        @block.vector
        def _(dve):
            dve.wait_ge(y_in, 16 * G)
            with dve.Fori(0, KT // 2) as i:
                for u in range(2):
                    dve.wait_ge(sig[u], i + 2)
                    dst = o[:, bass.ds(i * 2 + u, 1), :].rearrange("p a b -> p (a b)")
                    V.tensor_tensor(zt[:, u, :], zt[:, u, :], g[:, u, :], ALU.mult)
                    V.tensor_tensor(sg[:, u, :], sg[:, u, :], y[:, bass.ds(i * 2 + u, 1), :].rearrange("p a b -> p (a b)"), ALU.mult)
                    dve.drain()
                    V.tensor_tensor(dst, zt[:, u, :], sg[:, u, :], ALU.mult).then_inc(gated[u], 1)


def s5_layer(nc, k, l, src, dst):
    A, take = k.A, k.arena.take
    h = take(KT, T)
    after_h = k.arena.at
    norm(nc, k, l, h, src)
    k.arena.at = after_h
    dense_to_dram(nc, k, h, A["s5_w_in"], 16, k.proj, l + 1, chunked=True)
    k.arena.at = k.mark
    s5 = Ctx()
    N = 2 * GP
    s5.kd, s5.cad = k.kd, k.cad
    s5.dsk, s5.coef = take(G), take(2, 2, N)
    s5.u = take(G, NJ)
    s5.X = take(2, N * (NJ + 1)).rearrange("p r (n j) -> p r n j", j=NJ + 1)
    mid = k.arena.at
    s5.br, s5.bi, s5.cr, s5.ci, s5.tmpb = (take(GP, 16) for _ in range(5))
    s5.AR, s5.AI = take(S + 1, N), take(S + 1, N)
    s5.bb = take(2, N * 16).rearrange("p r (n c) -> p r n c", c=16)
    scratch = k.arena.at
    s5_discretise(nc, k, s5)
    k.arena.at = scratch
    s5.pw = take(2, 4 * (S + 1)).rearrange("p u (d r n) -> p u d r n", d=2, r=2)
    s5.cpair, s5.cl = take(2, 2, 16), take(2, 4, P)
    s5_matrices(nc, k, s5, k.proj)
    k.arena.at = mid
    s5.T = take(2, G * P).rearrange("p d (g l) -> p d g l", l=P)
    top = k.arena.at
    s5_scan(nc, k, s5)
    k.arena.at = top
    s5_outputs(nc, k, s5, k.yd)
    k.arena.at = k.mark
    y, o = take(KT, T), take(KT, T)
    after = k.arena.at
    s5_glu(nc, k, y, o, A["s5_w_glu"], k.proj, k.yd)
    k.arena.at = after
    dense_residual(nc, k, l, o, A["s5_w_out"], src, dst, chunked=True)


def rwkv_project(nc, k, j, h, hid, mod_layer):
    take = k.arena.take
    dd, xs = take(KT, T), [take(KT, T), take(KT, T)]
    strips_, stage = take(2, KT * P), take(2, T)
    V = nc.vector
    with Phase(nc) as es:
        sem = lambda n, credit=0: es.semaphore("rp_" + n, credit)
        xs_ready = sem("xs_ready")
        w_in = [sem(f"w_in{u}") for u in range(2)]
        mm_done = [sem(f"mm_done{u}", 1) for u in range(2)]
        ev_done = [sem(f"ev_done{u}", 1) for u in range(2)]
        stored = [sem(f"stored{u}", 16) for u in range(2)]
        hidden = HiddenModulation(nc, k, es, mod_layer, 2) if mod_layer < k.depth else None
        block = es.block()

        @block.sync
        def _(sp):
            def turn(i):
                for u in range(2):
                    sp.wait_ge(mm_done[u], i + 1)
                    sp.dma_start(strips_[:, u, :], dram_tile(k.A["rw_w"], i * 2 + (34 * j + u))).then_inc(w_in[u], 16)
            turns = hidden.turns if hidden else 0
            if hidden:
                with sp.Fori(0, turns) as i:
                    turn(i)
                    hidden.sync_part(sp, i)
            with sp.Fori(turns, 17) as i:
                turn(i)

        @block.vector
        def _(dve):
            for c in range(KT):
                V.tensor_tensor(dd[:, c, 1:T - 1], h[:, c, 0:T - 2], h[:, c, 2:T], ALU.add)
            dve.drain()
            for a, b in SEGS:
                V.tensor_copy(dd[:, :, a:a + 1], h[:, :, a + 1:a + 2])
                V.tensor_copy(dd[:, :, b - 1:b], h[:, :, b - 2:b - 1])
            dve.drain()
            for c in range(KT):
                V.scalar_tensor_tensor(dd[:, c, :], dd[:, c, :], 0.5, h[:, c, :], ALU.mult, ALU.subtract)
            dve.drain()
            for n in range(6):
                if hidden and 2 <= n < 5:
                    with dve.Fori(4 * (n - 2), 4 * (n - 1)) as i:
                        hidden.vector_part(dve, i)
                if n >= 2:
                    dve.wait_ge(mm_done[1], 4 * (n - 1) + 1)
                for c in range(KT):
                    last = V.scalar_tensor_tensor(xs[n % 2][:, c, :], dd[:, c, :], k.mu[:, (j * 6 + n) * KT + c:(j * 6 + n) * KT + c + 1],
                                                  h[:, c, :], ALU.mult, ALU.add)
                last.then_inc(xs_ready, 1)
            if hidden:
                dve.drain()
                hidden.vector_end(dve)

        @block.tensor
        def _(pe):
            for n in range(4):
                pe.wait_ge(xs_ready, n + 1)
                with pe.Fori(0, 4) as i:
                    for u in range(2):
                        pe.wait_ge(w_in[u], i * 16 + (64 * n + 16))
                        pe.wait_ge(ev_done[u], i + 4 * n + 1)
                        strip_matmuls(nc, k, u, strips_[:, u, :], xs[n % 2]).then_inc(mm_done[u], 1)
                    if hidden and n < 3:
                        hidden.tensor_part(pe, i + 4 * n)
            for u in range(2):
                pe.wait_ge(xs_ready, 5 + u)
                pe.wait_ge(w_in[u], 17 * 16)
                pe.wait_ge(ev_done[u], 16 + 1)
                strip_matmuls(nc, k, u, strips_[:, u, :], xs[u]).then_inc(mm_done[u], 1)

        @block.scalar
        def _(act):
            with act.Fori(0, 16) as i:
                for u in range(2):
                    act.wait_ge(mm_done[u], i + 2)
                    act.wait_ge(stored[u], i * 16 + 16)
                    nc.scalar.copy(stage[:, u, :], acc(k, u)).then_inc(ev_done[u], 1)
                    act.wait_ge(ev_done[u], i + 2)
                    act.dma_start(dram_tile(k.proj, i * 2 + u), stage[:, u, :]).then_inc(stored[u], 16)
            act.wait_ge(mm_done[0], 17 + 1)
            nc.scalar.activation(hid[:, 0, :], acc(k, 0), ACT.Tanh)
            act.wait_ge(mm_done[1], 17 + 1)
            nc.scalar.copy(hid[:, 1, :], acc(k, 1))
            for u in range(2):
                act.wait_ge(stored[u], 256 + 16)


KK_, R_, KH_, BH_ = range(4)
NW2 = T // (2 * W)


def rwkv_recur(nc, k, j, o, hid):
    take = k.arena.take
    rkvg, kkn, sg, ic = take(4, T), take(T), take(2, T), take(2, T)
    y, t1, t2 = take(T), take(T), take(T)
    w2t, par = take(4, P), take(NPAR)
    TT, KHs, pc = take(2, NCH, C), take(2, NCH, C), take(2, NCH)
    QT = sg
    ops = take(4, 2, 2 * W)
    tmp = t1.rearrange("p (a b) -> p a b", b=2 * W)
    tmq = t2.rearrange("p (a b) -> p a b", b=2 * W)
    lanes = []
    for L in range(2):
        b = Ctx()
        b.V, b.Kt, b.Bt, b.RH = take(P), take(2, P), take(2, P), take(4, P)
        b.X, b.XT, b.NT, b.F, b.X2, b.X2T, b.X4, b.M1, b.M3, b.M4 = (take(4, P) for _ in range(10))
        b.Di, b.Z, b.ZT, b.Z2, b.Z2T, b.Z4T, b.GH = b.X, b.X2, b.X2T, b.X4, b.XT, b.NT, b.M1
        b.bank = [k.ps[:, 4 * L + n, :] for n in range(4)]
        b.pair = [k.ps[:, 4 * L + n:4 * L + n + 2, :].rearrange("p h (q c) -> p h q c", c=P) for n in (0, 2)]
        b.b4 = [v.rearrange("p (u c) -> p u c", u=4) for v in b.bank]
        lanes.append(b)
    stq, Sst = take(2, 4, C), take(2, 2, C)
    V, SC, PE = nc.vector, nc.scalar, nc.tensor
    r_, k_, v_, g_ = (rkvg[:, n, :] for n in range(4))
    units = [(d, hh) for d in range(2) for hh in range(2)]
    HP = [slice(0, 64), slice(64, 128)]

    v_win, rq, gn = take(2 * W), take(2, 2 * W), take(2)
    small = take(2 * T // P)

    with Phase(nc) as es:
        sem = lambda n, credit=0: es.semaphore("rw_" + n, credit)
        tile_in, vg_in = sem("k_r_in"), sem("v_g_in")
        rk_free, tile_done = sem("k_r_free"), sem("tile_done", 1)
        rq_ready = sem("rq_ready")
        sq_ready, norm_mm, norm_root = sem("sq_ready"), sem("norm_mm"), sem("norm_root")
        norm_wide, norm_spread, post_wide = sem("norm_wide"), sem("norm_spread"), sem("post_wide")
        banks_free = sem("banks_free", 1)
        lora_mm, lora_ev = sem("lora_mm"), sem("lora_ev")
        cum_ready, decays, ops_ready = sem("cum_ready"), sem("decays"), sem("ops_ready")
        pst = [[sem(f"pe{s}_{L}") for s in range(14)] for L in range(2)]
        ast = [[sem(f"act{s}_{L}", s // 8) for s in range(9)] for L in range(2)]
        dst = [[sem(f"dve{s}_{L}", s // 9) for s in range(10)] for L in range(2)]
        step_q, step_t = [sem(f"step_q{p}") for p in range(2)], [sem(f"step_t{p}") for p in range(2)]
        y_mm, y_ev = ([sem(f"{n}{p}", 1) for p in range(2)] for n in ("y_mm", "y_ev"))
        s_mm, s_ev = ([[sem(f"{n}{d}_{p}", 1) for p in range(2)] for d in range(2)] for n in ("s_mm", "s_ev"))
        start_ev = sem("state_zeroed")
        post_in, post_mm, post_ev, post_sq, post_sig = sem("post_in"), sem("post_mm"), sem("post_ev"), sem("post_sq"), sem("post_sig")
        block = es.block()

        @block.sync
        def _(sp):
            def first_loads(e, off):
                for n in (1, 0):
                    sp.dma_start(rkvg[:, n, :], dram_tile(k.proj, e + (n * KT + off))).then_inc(tile_in, 16)
                sp.dma_start(w2t, dram_tile(k.A["rw_w2"], e + (KT * j + off)).rearrange("p (a b) -> p a b", b=P)).then_inc(tile_in, 16)
                sp.dma_start(par, dram_tile(k.A["rw_par"], e + (KT * j + off))).then_inc(tile_in, 16)

            def last_loads(e):
                sp.wait_ge(tile_done, e + 1)
                for n in (2, 3):
                    sp.dma_start(rkvg[:, n, :], dram_tile(k.proj, e + n * KT)).then_inc(vg_in, 16)

            first_loads(0, 0)
            with sp.Fori(0, KT - 1) as e:
                last_loads(e)
                sp.wait_ge(rk_free, e + 1)
                first_loads(e, 1)
            last_loads(KT - 1)

        @block.tensor
        def _(pe):
            def head_sums(src, half):
                for n, (a, b) in enumerate(CHUNKS):
                    last = PE.matmul(k.ps[:, 3 * half + n, 0:b - a], k.head_ones, src[:, a:b], start=True, stop=True)
                return last

            def lora(which, s, half):
                for n, (a, b) in enumerate(CHUNKS):
                    last = PE.matmul(k.ps[:, 3 * half + n, 0:b - a], w2t[:, 2 * which + s, :], hid[:, which, a:b],
                                     start=True, stop=True)
                return last

            def bonus_sums():
                for n, (a, b) in enumerate(CHUNKS):
                    last = PE.matmul(k.ps[:, 4 + n, 0:b - a], k.head_ones, t2[:, a:b], start=True, stop=True)
                return last

            def four(bank, lhsT, rhs):
                for u in range(4):
                    last = PE.matmul(bank[:, u, :], lhsT(u), rhs(u), start=True, stop=True)
                return last

            with pe.Fori(0, KT) as e:
                pe.wait_ge(tile_in, e * 64 + 64)
                pe.wait_ge(banks_free, e + 1)
                lora(0, 0, 1).then_inc(lora_mm, 1)
                lora(0, 1, 0).then_inc(lora_mm, 1)
                pe.wait_ge(sq_ready, e + 1)
                token_sums(nc, k, 6, t2).then_inc(norm_mm, 1)
                pe.wait_ge(lora_ev, e * 4 + 1)
                lora(1, 0, 1).then_inc(lora_mm, 1)
                pe.wait_ge(lora_ev, e * 4 + 2)
                pe.wait_ge(norm_wide, e + 1)
                spread(nc, k, 0, t2).then_inc(norm_spread, 1)
                pe.wait_ge(lora_ev, e * 4 + 3)
                lora(1, 1, 1).then_inc(lora_mm, 1)
                pe.wait_ge(lora_ev, e * 4 + 4)
                hold(k, pe)

                with pe.Fori(0, NW2) as w:
                    it = e * NW2 + w

                    def op(L, kind, u):
                        d, hh = units[u]
                        return ops[HP[hh], kind, d, L * W:(L + 1) * W]

                    def transposes(L):
                        b = lanes[L]
                        if L == 0:
                            pe.wait_ge(ops_ready, it + 1)
                        pe.wait_ge(dst[L][9], it + 1)
                        pe.wait_ge(ast[L][8], it + 1)
                        PE.transpose(b.bank[0][:, 0:P], v_win[:, L * W:(L + 1) * W], k.ident)
                        for d in range(2):
                            PE.transpose(b.bank[0][:, (1 + d) * P:(2 + d) * P], ops[:, KK_, d, L * W:(L + 1) * W], k.ident)
                        PE.transpose(b.bank[0][:, 3 * P:4 * P], ops[:, KH_, 0, L * W:(L + 1) * W], k.ident)
                        PE.transpose(b.bank[1][:, 0:P], ops[:, KH_, 1, L * W:(L + 1) * W], k.ident)
                        for d in range(2):
                            last = PE.transpose(b.bank[1][:, (1 + d) * P:(2 + d) * P], ops[:, BH_, d, L * W:(L + 1) * W], k.ident)
                        last.then_inc(pst[L][0], 1)

                    def s1(L):
                        b = lanes[L]
                        for hh in range(2):
                            for d in range(2):
                                PE.matmul(b.pair[1][:, hh, d, :], op(L, KK_, 2 * d + hh), op(L, BH_, 2 * d + hh),
                                          start=True, stop=True)
                                last = PE.matmul(b.pair[1][:, hh, 2 + d, :], op(L, BH_, 2 * d + hh), op(L, KK_, 2 * d + hh),
                                                 start=True, stop=True)
                        last.then_inc(pst[L][1], 1)

                    def s2(L):
                        b = lanes[L]
                        pe.wait_ge(ast[L][0], it + 1)
                        hold(k, pe)
                        for hh in range(2):
                            for d in range(2):
                                last = PE.matmul(b.pair[0][:, hh, 2 * d:2 * d + 2, :], op(L, KH_, 2 * d + hh),
                                                 ops[HP[hh], KK_:R_ + 1, d, L * W:(L + 1) * W], start=True, stop=True)
                        last.then_inc(pst[L][2], 1)

                    def s3(L):
                        b = lanes[L]
                        pe.wait_ge(dst[L][1], it + 1)
                        four(b.b4[2], lambda u: b.XT[:, u, :], lambda u: b.X[:, u, :])
                        four(b.b4[3], lambda u: b.X[:, u, :], lambda u: b.XT[:, u, :]).then_inc(pst[L][3], 1)

                    def s4(L):
                        b = lanes[L]
                        pe.wait_ge(dst[L][2], it + 1)
                        hold(k, pe)
                        for hh in range(2):
                            for d in range(2):
                                PE.matmul(b.pair[0][:, hh, d, :], op(L, BH_, 2 * d + hh), op(L, R_, 2 * d + hh), start=True, stop=True)
                        for u, (d, hh) in enumerate(units):
                            last = PE.matmul(b.pair[0][:, hh, 2, d * C:(d + 1) * C], b.M1[:, u, :], b.V[:, HP[hh]], start=True, stop=True)
                        last.then_inc(pst[L][4], 1)

                    def s5(L):
                        b = lanes[L]
                        pe.wait_ge(ast[L][1], it + 1)
                        four(b.b4[2], lambda u: b.X2T[:, u, :], lambda u: b.X2[:, u, :])
                        four(b.b4[3], lambda u: b.X2[:, u, :], lambda u: b.F[:, u, :]).then_inc(pst[L][5], 1)

                    def s6(L):
                        b = lanes[L]
                        pe.wait_ge(ast[L][2], it + 1)
                        pe.wait_ge(dst[L][4], it + 1)
                        four(b.b4[3], lambda u: b.X4[:, u, :], lambda u: b.F[:, u, :]).then_inc(pst[L][6], 1)

                    def s7(L):
                        b = lanes[L]
                        pe.wait_ge(dst[L][5], it + 1)
                        for u in range(4):
                            last = PE.transpose(b.b4[2][:, u, :], b.F[:, u, :], k.ident)
                        last.then_inc(pst[L][7], 1)

                    def s8(L):
                        b = lanes[L]
                        pe.wait_ge(ast[L][3], it + 1)
                        four(b.b4[0], lambda u: b.Di[:, u, :], lambda u: b.NT[:, u, :])
                        four(b.b4[1], lambda u: b.NT[:, u, :], lambda u: b.Di[:, u, :]).then_inc(pst[L][8], 1)

                    def s9(L):
                        b = lanes[L]
                        pe.wait_ge(ast[L][4], it + 1)
                        four(b.b4[2], lambda u: b.Z[:, u, :], lambda u: b.ZT[:, u, :])
                        four(b.b4[3], lambda u: b.ZT[:, u, :], lambda u: b.Z[:, u, :])
                        four(b.b4[0], lambda u: b.ZT[:, u, :], lambda u: b.F[:, u, :]).then_inc(pst[L][9], 1)

                    def s10(L):
                        b = lanes[L]
                        pe.wait_ge(ast[L][5], it + 1)
                        four(b.b4[1], lambda u: b.Z2[:, u, :], lambda u: b.Z2T[:, u, :])
                        pe.wait_ge(dst[L][6], it + 1)
                        four(b.b4[2], lambda u: b.Z2T[:, u, :], lambda u: b.F[:, u, :]).then_inc(pst[L][10], 1)

                    def s11(L):
                        b = lanes[L]
                        pe.wait_ge(ast[L][6], it + 1)
                        pe.wait_ge(dst[L][7], it + 1)
                        four(b.b4[3], lambda u: b.Z4T[:, u, :], lambda u: b.F[:, u, :]).then_inc(pst[L][11], 1)

                    def s12(L):
                        b = lanes[L]
                        pe.wait_ge(dst[L][8], it + 1)
                        four(b.b4[0], lambda u: b.F[:, u, :], lambda u: b.RH[:, u, :]).then_inc(pst[L][12], 1)

                    def s13(L):
                        b = lanes[L]
                        pe.wait_ge(ast[L][7], it + 1)
                        pe.wait_ge(dst[L][3], it + 1)
                        hold(k, pe)
                        for u, (d, hh) in enumerate(units):
                            PE.matmul(b.bank[1][HP[hh], d * P:(d + 1) * P], b.GH[:, u, 0:C], b.M4[:, u, :], start=True, stop=True)
                        for hh in range(2):
                            terms = [(b.V[:, HP[hh]], b.M3[:, 2 * d + hh, :]) for d in range(2)]
                            terms += [(b.GH[:, 2 * d + hh, C:2 * C], b.M4[:, 2 * d + hh, :]) for d in range(2)]
                            for n, (l, r) in enumerate(terms):
                                PE.matmul(b.bank[0][HP[hh], 0:P], l, r, start=(n == 0), stop=(n == 3))
                        for c in range(2):
                            cp = HP[c]
                            for u, (d, hh) in enumerate(units):
                                PE.matmul(b.bank[2 + c][HP[hh], d * C:(d + 1) * C], b.GH[cp, u, 0:C], b.Bt[cp, d, HP[hh]],
                                          start=True, stop=True)
                            for u, (d, hh) in enumerate(units):
                                out = b.bank[2 + c][HP[hh], (2 + d) * C:(3 + d) * C]
                                PE.matmul(out, b.Kt[cp, d, HP[hh]], b.V[cp, HP[hh]], start=True, stop=False)
                                last = PE.matmul(out, b.Bt[cp, d, HP[hh]], b.GH[cp, u, C:2 * C], start=False, stop=True)
                        last.then_inc(pst[L][13], 1)

                    for stage in (transposes, s1, s2, s3, s4, s5, s6, s7, s8, s9, s10, s11, s12, s13):
                        for L in range(2):
                            stage(L)
                for L in range(2):
                    pe.wait_ge(dst[L][9], (e + 1) * NW2 + 1)
                    pe.wait_ge(ast[L][8], (e + 1) * NW2 + 1)
                hold(k, pe)
                pe.wait_ge(post_in, e * 2 + 1)
                bonus_sums().then_inc(post_mm, 1)

                pe.wait_ge(start_ev, e + 1)
                hold(k, pe)
                with pe.Fori(0, NCH // 2) as n:
                    it = e * (NCH // 2) + n
                    for p in range(2):
                        pe.wait_ge(step_t[p], it + 1)
                        pe.wait_ge(step_q[p], it + 1)
                        hold(k, pe)
                        for d in range(2):
                            pe.wait_ge(s_ev[d][1 - p], it + (p + 1))
                            hold(k, pe)
                            for hh in range(2):
                                last = PE.matmul(k.ps[HP[hh], d, 0:C], stq[HP[hh], p, 2 * d, :],
                                                 Sst[HP[hh], p, d, :], start=True, stop=True)
                            last.then_inc(s_mm[d][p], 1)
                        pe.wait_ge(y_ev[p], it + 1)
                        hold(k, pe)
                        for hh in range(2):
                            for d in range(2):
                                last = PE.matmul(k.ps[HP[hh], 2 + p, d * C:(d + 1) * C], Sst[HP[hh], p, d, :],
                                                 stq[HP[hh], p, 2 * d + 1, :], start=True, stop=True)
                        last.then_inc(y_mm[p], 1)
                pe.wait_ge(post_in, e * 2 + 2)
                head_sums(y, 0).then_inc(post_mm, 1)
                pe.wait_ge(post_sq, e + 1)
                token_sums(nc, k, 7, t1).then_inc(post_mm, 1)
                pe.wait_ge(post_ev, e * 3 + 2)
                pe.wait_ge(post_wide, e + 1)
                spread(nc, k, 3, t2).then_inc(post_mm, 1)

        @block.scalar
        def _(act):
            with act.Fori(0, KT) as e:
                act.wait_ge(tile_in, e * 64 + 64)

                def lora_sigmoid(n):
                    dst_, col, half = ((sg[:, 0, :], P_W0, 1), (sg[:, 1, :], P_W0 + 1, 0),
                                       (ic[:, 0, :], P_A0, 1), (ic[:, 1, :], P_A0 + 1, 1))[n]
                    act.wait_ge(lora_mm, e * 4 + n + 1)
                    SC.activation(dst_, k.psf[:, 3 * half * BANK:3 * half * BANK + T], ACT.Sigmoid,
                                  bias=par[:, col:col + 1]).then_inc(lora_ev, 1)

                act.wait_ge(cum_ready, e * (NW2 + 1) + 1)
                SC.activation(t2, kkn, ACT.Square).then_inc(sq_ready, 1)
                lora_sigmoid(0)
                lora_sigmoid(1)
                act.wait_ge(norm_mm, e + 1)
                SC.activation(small, k.ps[:, 6, 0:2 * T // P], ACT.Sqrt).then_inc(norm_root, 1)
                lora_sigmoid(2)
                lora_sigmoid(3)
                def decay(w, off):
                    act.drain()
                    act.wait_ge(cum_ready, e * (NW2 + 1) + w + (off + 2))
                    for d in range(2):
                        SC.activation(ops[:, R_, d, :], tmp[:, d, :], ACT.Exp, scale=-DECAY)
                        SC.activation(ops[:, KH_, d, :], tmp[:, d, :], ACT.Exp, scale=DECAY)
                        SC.activation(ops[:, KK_, d, :], tmp[:, 2 + d, :], ACT.Exp, scale=-DECAY)
                    act.drain().then_inc(decays, 1)

                def window(w, more):
                    it = e * NW2 + w

                    def copies(L, stage, after, pairs):
                        act.wait_ge(pst[L][after], it + 1)
                        for out, in_ in pairs:
                            last = SC.copy(out, in_)
                        last.then_inc(ast[L][stage], 1)

                    def c0(L):
                        b = lanes[L]
                        copies(L, 0, 0, [(b.V, b.bank[0][:, 0:P]),
                                         (b.RH[:, :, 0:C], b.bank[0][:, P:3 * P].rearrange("p (u c) -> p u c", u=4)),
                                         (b.Kt[:, 0, :], b.bank[0][:, 3 * P:4 * P]),
                                         (b.Kt[:, 1, :], b.bank[1][:, 0:P]),
                                         (flat(b.Bt), b.bank[1][:, P:3 * P])])

                    def c1(L):
                        b = lanes[L]
                        copies(L, 1, 3, [(flat(b.X2), b.bank[2]), (flat(b.X2T), b.bank[3])])

                    def c2(L):
                        b = lanes[L]
                        act.wait_ge(dst[L][3], it + 1)
                        SC.copy(b.RH[:, :, C:2 * C].rearrange("p (d h) c -> p h d c", d=2),
                                b.pair[0][:, :, 2, :].rearrange("p h (d c) -> p h d c", d=2))
                        copies(L, 2, 5, [(flat(b.X4), b.bank[2])])

                    def c3(L):
                        copies(L, 3, 7, [(flat(lanes[L].Di), lanes[L].bank[2])])

                    def c4(L):
                        b = lanes[L]
                        copies(L, 4, 8, [(flat(b.Z), b.bank[0]), (flat(b.ZT), b.bank[1])])

                    def c5(L):
                        b = lanes[L]
                        copies(L, 5, 9, [(flat(b.Z2T), b.bank[2]), (flat(b.Z2), b.bank[3])])

                    def c6(L):
                        copies(L, 6, 10, [(flat(lanes[L].Z4T), lanes[L].bank[1])])

                    def c7(L):
                        act.wait_ge(pst[L][12], it + 1)
                        SC.mul(flat(lanes[L].GH), lanes[L].bank[0], -1.0).then_inc(ast[L][7], 1)

                    def c8(L):
                        act.wait_ge(pst[L][13], it + 1)
                        hold(k, act)
                        SC.copy(y[:, bass.ds(w * 2 * W + L * W, W)], lanes[L].bank[0][:, 0:P]).then_inc(ast[L][8], 1)

                    def keep_r():
                        act.wait_ge(dst[1][9], it + 1)
                        SC.copy(rq, ops[:, R_, :, :]).then_inc(rq_ready, 1)

                    for c in (c0, c1, c2, c3, c4, c5, c6, c7, c8):
                        for L in range(2):
                            c(L)
                        if c is c1:
                            keep_r()
                        if c is c2 and more:
                            decay(w, 1)

                decay(0, 0)
                with act.Fori(0, NW2 - 1) as w:
                    window(w, True)
                window(NW2 - 1, False)

                def step_copies(n, last_of):
                    for p in range(2):
                        it = e * (NCH // 2) + n
                        act.wait_ge(y_mm[p], it + 1)
                        act.wait_ge(dst[1][9], (e + 1) * NW2 + 1)
                        hold(k, act)
                        SC.copy(stq[:, p, 1, :], QT[:, 0, bass.ds(n * 2 * C + p * C, C)])
                        SC.copy(stq[:, p, 3, :], QT[:, 1, bass.ds(n * (-2 * C) + (last_of - p) * C, C)])
                        act.drain().then_inc(step_q[p], 1)
                with act.Fori(0, NCTX // C // 2) as n:
                    step_copies(n, NCTX // C - 1)
                with act.Fori(NCTX // C // 2, NCH // 2) as n:
                    step_copies(n, NCH + NCTX // C - 1)
                act.wait_ge(post_ev, e * 3 + 1)
                SC.activation(t1, y, ACT.Square).then_inc(post_sq, 1)
                act.wait_ge(vg_in, e * 32 + 32)
                SC.activation(ic[:, 0, :], g_, ACT.Sigmoid)
                act.wait_ge(post_ev, e * 3 + 3)
                SC.activation(small, small, ACT.Sqrt)
                act.drain().then_inc(post_sig, 1)

        @block.gpsimd
        def _(pool):
            with pool.Fori(0, KT) as e:
                def step_copies(n, last_of):
                    for p in range(2):
                        it = e * (NCH // 2) + n
                        pool.wait_ge(s_mm[1][p], it + 1)
                        pool.wait_ge(dst[1][9], (e + 1) * NW2 + 1)
                        hold(k, pool)
                        nc.gpsimd.tensor_copy(stq[:, p, 0, :], TT[:, 0, bass.ds(n * 2 + p, 1), :].rearrange("p a b -> p (a b)"))
                        nc.gpsimd.tensor_copy(stq[:, p, 2, :], TT[:, 1, bass.ds(n * (-2) + (last_of - p), 1), :].rearrange("p a b -> p (a b)"))
                        pool.drain().then_inc(step_t[p], 1)
                with pool.Fori(0, NCTX // C // 2) as n:
                    step_copies(n, NCTX // C - 1)
                with pool.Fori(NCTX // C // 2, NCH // 2) as n:
                    step_copies(n, NCH + NCTX // C - 1)

        @block.vector
        def _(dve):
            with dve.Fori(0, KT) as e:
                dve.wait_ge(tile_in, e * 64 + 64)
                V.tensor_scalar(kkn, k_, par[:, P_KK:P_KK + 1], None, ALU.mult).then_inc(cum_ready, 1)
                def prepare(w, off):
                    def at(v):
                        return v[:, bass.ds(w * (2 * W) + off * 2 * W, 2 * W)]
                    sgw = [at(sg[:, d, :]) for d in range(2)]
                    icw = [at(ic[:, d, :]) for d in range(2)]

                    def sums():
                        V.tensor_tensor_scan(tmp[:, 0, :], k.seq_mask, sgw[0], 0.0, ALU.mult, ALU.add)
                        V.tensor_tensor_scan(tmp[:, 1, :], k.seq_mask, sgw[1], 0.0, ALU.mult, ALU.add)
                        dve.drain()

                    def before():
                        V.tensor_tensor(tmp[:, 2, :], tmp[:, 0, :], sgw[0], ALU.subtract)
                        left = tmp[:, 1, :].rearrange("p (c t) -> p c t", t=C)
                        V.tensor_tensor(tmp[:, 3, :].rearrange("p (c t) -> p c t", t=C),
                                        left[:, :, C - 1:C].to_broadcast([P, 2 * W // C, C]), left, ALU.subtract)
                        dve.drain()
                        V.tensor_tensor(tmp[:, 1, :], tmp[:, 3, :], sgw[1], ALU.add)
                        dve.drain().then_inc(cum_ready, 1)

                    def keys():
                        for d in range(2):
                            V.tensor_scalar(tmq[:, d, :], icw[d], -1.0, par[:, P_KA:P_KA + 1], ALU.add, ALU.mult)
                            V.tensor_tensor(tmq[:, 2 + d, :], at(kkn), icw[d], ALU.mult)
                        dve.drain()

                    def more_keys():
                        for d in range(2):
                            V.scalar_tensor_tensor(tmq[:, d, :], tmq[:, d, :], 1.0, at(k_), ALU.add, ALU.mult)
                        dve.drain()

                    def ends():
                        dve.wait_ge(decays, e * NW2 + w + (off + 1))
                        hold(k, dve)
                        for c in range(4):
                            cc = w * 4 + (off * 4 + c)
                            V.tensor_copy(pc[:, 0, bass.ds(cc, 1)], ops[:, R_, 0, (c + 1) * C - 1:(c + 1) * C])
                            V.tensor_copy(pc[:, 1, bass.ds(cc, 1)], ops[:, R_, 1, c * C:c * C + 1])
                        for d in range(2):
                            V.tensor_tensor(ops[:, BH_, d, :], ops[:, KH_, d, :], tmq[:, 2 + d, :], ALU.mult)
                        dve.drain()

                    def others():
                        V.tensor_copy(v_win, at(v_))
                        for d in range(2):
                            V.tensor_tensor(ops[:, R_, d, :], ops[:, R_, d, :], at(r_), ALU.mult)
                            V.tensor_tensor(ops[:, KH_, d, :], ops[:, KH_, d, :], tmq[:, d, :], ALU.mult)
                            V.tensor_tensor(ops[:, KK_, d, :], ops[:, KK_, d, :], at(kkn), ALU.mult)
                        dve.drain().then_inc(ops_ready, 1)

                    return sums, before, keys, more_keys, ends, others

                sums, before, *rest = prepare(0, 0)
                dve.wait_ge(lora_ev, e * 4 + 2)
                sums()
                before()
                dve.wait_ge(norm_root, e + 1)
                V.tensor_scalar(small, small, 1e-12, None, ALU.max)
                dve.drain()
                V.reciprocal(small, small)
                dve.drain()
                widen(nc, t2, small).then_inc(norm_wide, 1)

                def window(w, more):
                    it = e * NW2 + w
                    parts = prepare(w, 1) if more else ()

                    def masked(out, in_, mask):
                        V.tensor_tensor(out.rearrange("p (d h) c -> p h d c", d=2), in_,
                                        mask.unsqueeze(1).to_broadcast([P, 2, 2, P]), ALU.mult)

                    def d1(L):
                        b = lanes[L]
                        dve.wait_ge(pst[L][1], it + 1)
                        hold(k, dve)
                        masked(b.X, b.pair[1][:, :, 0:2, :], k.m_x)
                        masked(b.XT, b.pair[1][:, :, 2:4, :], k.m_xt)
                        masked(b.NT, b.pair[1][:, :, 2:4, :], k.m_nt)
                        dve.drain()
                        V.tensor_tensor(b.F, b.XT, k.ident.unsqueeze(1).to_broadcast([P, 4, P]), ALU.add).then_inc(dst[L][1], 1)

                    def d2(L):
                        b = lanes[L]
                        dve.wait_ge(pst[L][2], it + 1)
                        hold(k, dve)
                        masked(b.M1, b.pair[0][:, :, 0::2, :], k.m_s)
                        masked(b.M3, b.pair[0][:, :, 1::2, :], k.m_i)
                        dve.drain().then_inc(dst[L][2], 1)

                    def d3(L):
                        b = lanes[L]
                        dve.wait_ge(pst[L][4], it + 1)
                        hold(k, dve)
                        masked(b.M4, b.pair[0][:, :, 0:2, :], k.m_i)
                        dve.drain().then_inc(dst[L][3], 1)

                    def addf(L, stage, after, bank, op=ALU.add):
                        b = lanes[L]
                        dve.wait_ge(pst[L][after], it + 1)
                        V.tensor_tensor(b.F, b.F, b.b4[bank], op).then_inc(dst[L][stage], 1)

                    def d9(L):
                        b = lanes[L]
                        dve.wait_ge(pst[L][13], it + 1)
                        dve.wait_ge(rq_ready, it + 1)
                        hold(k, dve)
                        wc = w * 2 * W + L * W
                        V.tensor_tensor(QT[:, :, bass.ds(wc, W)], b.bank[1][:, 0:2 * P].rearrange("p (d c) -> p d c", d=2),
                                        rq[:, :, L * W:(L + 1) * W], ALU.add)
                        for c in range(2):
                            ch = w * 4 + (L * 2 + c)
                            v = b.bank[2 + c].rearrange("p (q c) -> p q c", c=C)
                            V.tensor_tensor(TT[:, :, bass.ds(ch, 1), :].rearrange("p d a c -> p d (a c)"), v[:, 0:2, :],
                                            k.eye2.unsqueeze(1).to_broadcast([P, 2, C]), ALU.add)
                            V.tensor_tensor(KHs[:, :, bass.ds(ch, 1), :].rearrange("p d a c -> p d (a c)"), v[:, 2:4, :],
                                            pc[:, :, bass.ds(ch, 1)].to_broadcast([P, 2, C]), ALU.mult)
                        dve.drain().then_inc(dst[L][9], 1)

                    stages = (d1, d2, d3, lambda L: addf(L, 4, 5, 3), lambda L: addf(L, 5, 6, 3),
                              lambda L: addf(L, 6, 9, 0, ALU.subtract), lambda L: addf(L, 7, 10, 2),
                              lambda L: addf(L, 8, 11, 3), d9)
                    for n, f in enumerate(stages):
                        for L in range(2):
                            f(L)
                        if more and 1 <= n <= 6:
                            parts[n - 1]()

                dve.wait_ge(norm_spread, e + 1)
                V.tensor_tensor(kkn, kkn, k.psf[:, 0:T], ALU.mult)
                dve.drain()
                dve.wait_ge(lora_ev, e * 4 + 4)
                dve.wait_ge(vg_in, e * 32 + 32)
                hold(k, dve)
                for part in rest:
                    part()
                with dve.Fori(0, NW2 - 1) as w:
                    window(w, True)
                window(NW2 - 1, False)

                V.scalar_tensor_tensor(t2, r_, par[:, P_RK:P_RK + 1], k_, ALU.mult, ALU.mult).then_inc(post_in, 1)
                V.tensor_copy(gn, par[:, P_LNW:P_LNB + 1])
                dve.drain().then_inc(rk_free, 1)

                V.memset(Sst[:, 0, :, :], 0.0).then_inc(start_ev, 1)

                def steps(n, last_of):
                    it = e * (NCH // 2) + n
                    for p in range(2):
                        cf, cb = n * 2 + p, n * (-2) + (last_of - p)
                        dve.wait_ge(y_mm[1 - p], it + (p + 1))
                        for d, ch in ((0, cf), (1, cb)):
                            dve.wait_ge(s_mm[d][p], it + 2)
                            hold(k, dve)
                            V.scalar_tensor_tensor(Sst[:, 1 - p, d, :], k.ps[:, d, 0:C], pc[:, d, bass.ds(ch, 1)],
                                                   KHs[:, d, bass.ds(ch, 1), :].rearrange("p a c -> p (a c)"), ALU.mult,
                                                   ALU.add).then_inc(s_ev[d][p], 1)
                        dve.wait_ge(y_mm[p], it + 2)
                        hold(k, dve)
                        for d, ch in ((0, cf), (1, cb)):
                            yc = y[:, bass.ds(ch * C, C)]
                            V.tensor_tensor(yc, yc, k.ps[:, 2 + p, d * C:(d + 1) * C], ALU.add)
                        dve.drain().then_inc(y_ev[p], 1)
                with dve.Fori(0, NCTX // C // 2) as n:
                    steps(n, NCTX // C - 1)
                with dve.Fori(NCTX // C // 2, NCH // 2) as n:
                    steps(n, NCH + NCTX // C - 1)

                dve.drain().then_inc(post_in, 1)
                dve.wait_ge(post_mm, e * 4 + 2)
                V.scalar_tensor_tensor(y, k.psf[:, 0:T], -1.0 / 64, y, ALU.mult, ALU.add).then_inc(post_ev, 1)
                V.tensor_tensor(v_, k.psf[:, 4 * BANK:4 * BANK + T], v_, ALU.mult).then_inc(post_ev, 1)
                dve.wait_ge(post_mm, e * 4 + 3)
                V.tensor_scalar(small, k.ps[:, 7, 0:2 * T // P], 1.0 / 64, GN_EPS, ALU.mult, ALU.add).then_inc(post_ev, 1)
                dve.wait_ge(post_sig, e + 1)
                V.reciprocal(small, small)
                dve.drain()
                widen(nc, t2, small).then_inc(post_wide, 1)
                V.tensor_tensor(g_, g_, ic[:, 0, :], ALU.mult)
                dve.drain()
                dve.wait_ge(post_mm, e * 4 + 4)
                V.tensor_tensor(y, y, k.psf[:, 3 * BANK:3 * BANK + T], ALU.mult).then_inc(banks_free, 1)
                dve.drain()
                V.tensor_scalar(y, y, gn[:, 0:1], gn[:, 1:2], ALU.mult, ALU.add)
                dve.drain()
                V.tensor_tensor(y, y, v_, ALU.add)
                dve.drain()
                V.tensor_tensor(o[:, bass.ds(e, 1), :].rearrange("p a b -> p (a b)"), y, g_, ALU.mult)
                dve.drain().then_inc(tile_done, 1)


def rwkv_layer(nc, k, l, src, dst):
    take = k.arena.take
    j = l // 3
    k.mu = take(2 * 6 * KT)
    k.m_x, k.m_xt, k.m_nt, k.m_s, k.m_i = (take(2, P) for _ in range(5))
    k.seq_mask, k.eye2 = take(2 * W), take(C)
    masks = [(flat(v), k.A["m_" + n]) for n, v in
             (("x", k.m_x), ("xt", k.m_xt), ("nt", k.m_nt), ("s", k.m_s), ("i", k.m_i))]
    load_constants(nc, masks + [(k.mu, k.A["mu"]), (k.seq_mask, k.A["seq_mask"]), (k.eye2, k.A["eye2"])])
    h, hid = take(KT, T), take(2, T)
    top = k.arena.at
    norm(nc, k, l, h, src)
    k.arena.at = top
    rwkv_project(nc, k, j, h, hid, l + 1)
    k.arena.at = top
    rwkv_recur(nc, k, j, h, hid)
    k.arena.at = top
    dense_residual(nc, k, l, h, k.A["rw_w_out"][j * KT:(j + 1) * KT], src, dst)


def program(nc, A, out, layers, depth):
    k = Ctx()
    k.depth, k.n_mod = depth, depth * MODS
    with ExitStack() as es:
        cols = (nc.sbuf_bytes_remaining - 64) // 4
        arena_t = es.enter_context(nc.sbuf_tensor("arena", [P, cols], F32))
        k.arena = Arena(arena_t, cols)
        k.ps = es.enter_context(nc.psum_tensor("ps", [P, 8, BANK], F32))
        k.held = es.enter_context(nc.semaphore("waits_held"))
        k.psf = k.ps[:, :, :].rearrange("p a b -> p (a b)")
        take = k.arena.take
        k.ident, k.ones, k.head_ones = take(P), take(P), take(P)
        k.mod, k.b_mod, k.norm_g = take(k.n_mod, 2), take(k.n_mod), take(depth * KT)
        k.na_g, k.b_glu, k.cond = take(2), take(KT), take(KT, 2)
        k.A = A
        k.constant_loads = [(k.ident, A["ident"]), (k.ones, A["ones"]), (k.head_ones, A["head_ones"]),
                            (k.b_mod, A["b_mod"]), (k.norm_g, A["norm_g"]), (k.na_g, A["na_g"]),
                            (k.b_glu, A["b_glu"])]
        k.w_mod, k.cond_d, k.na_bias = A["w_mod"], A["cond"], A["na_bias"]
        xres = [nc.dram_tensor(f"xres{i}", (KT, P, T), F32, kind="Internal").ap() for i in range(depth)]
        proj = nc.dram_tensor("proj", (32, P, T), F32, kind="Internal").ap()
        k.proj = proj
        k.kd = nc.dram_tensor("s5_kernel", (2, GP, 2, 16, 2 * P), F32, kind="Internal").ap()
        k.cad = nc.dram_tensor("s5_out_rows", (GP, P, 4 * P), F32, kind="Internal").ap()
        k.yd = nc.dram_tensor("s5_y", (GP, P, 2 * NJ), F32, kind="Internal").ap()
        k.mark = mark = k.arena.at
        load_constants(nc, k.constant_loads)
        modulation(nc, k, mark, layers[0])
        src = A["x"]
        for l in layers:
            k.arena.at = mark
            dst = out if l == layers[-1] else xres[l]
            if l % 3 != 1:
                (rwkv_layer, None, s5_layer)[l % 3](nc, k, l, src, dst)
                src = dst
                continue
            h = take(KT, T)
            top = k.arena.at
            norm(nc, k, l, h, src)
            k.arena.at = top
            if l % 3 == 1:
                dense_to_dram(nc, k, h, A["na_w_in"], 32, proj, l + 1)
                k.arena.at = top
                na_attention(nc, k, h, proj)
                k.arena.at = top
                dense_residual(nc, k, l, h, A["na_w_out"], src, dst)
            src = dst


def strips(w):
    e = w.shape[1] // P
    return w.reshape(KT, P, e, P).transpose(2, 1, 0, 3).reshape(e, P, KT * P)


def by_channel(v):
    return v.reshape(-1, KT, P).transpose(2, 0, 1).reshape(P, -1)


def layout(inp):
    I = {n: np.asarray(v) for n, v in inp.items()}
    A = {}
    A["x"] = np.concatenate([I["ctx"][0], I["x"][0]], 0).T.reshape(KT, P, T)
    A["cond"] = np.stack([by_channel(I["c_ctx"]), by_channel(I["c"][0])], -1).reshape(P, KT * 2)
    A["w_mod"] = np.concatenate([strips(w) for w in I["w_mod"]])
    A["b_mod"] = I["b_mod"].reshape(-1, P).T
    A["norm_g"] = by_channel(I["norm_g"])
    A["ident"] = np.eye(P, dtype=np.float32)
    A["ones"] = np.ones((P, P), np.float32)
    half = np.arange(P) // 64
    A["head_ones"] = (half[:, None] == half[None, :]).astype(np.float32)
    A["na_w_in"] = strips(I["na_w_in"][0])
    A["na_w_out"] = strips(I["na_w_out"][0])
    A["na_g"] = np.stack([np.tile(I["na_q_g"][0], 2), np.tile(I["na_k_g"][0], 2)], -1)
    q, c = np.arange(GRID)[:, None], np.arange(GRID)[None, :]
    start = np.clip(q - KW // 2, 0, GRID - KW)
    inside = (c >= start) & (c < start + KW)
    idx = np.clip(c - q + KW - 1, 0, 2 * KW - 2)
    table = I["na_rpb"][0][:, :, idx]
    table = np.where(inside[None, None], table, np.float32(-1e30)).transpose(0, 2, 1, 3)
    A["na_bias"] = table.reshape(KT, P, NA_BIAS)
    first = lambda w: strips(np.concatenate([w[0], w[1]], 1))
    A["rw_w"] = np.concatenate([x for j in range(2) for x in
                                [strips(w) for w in I["rwkv_w_rkvg"][j]] + [first(I["rwkv_w1"][j]), first(I["rwkv_a1"][j])]])
    second = lambda w: w.reshape(2, 64, KT, P).transpose(2, 0, 1, 3)
    w2 = np.zeros((2, KT, 2, 64, 2, 2, P), np.float32)
    for j in range(2):
        for n, name in enumerate(("rwkv_w2", "rwkv_a2")):
            for s in range(2):
                w2[j, :, s, :, n, s, :] = second(I[name][j])[:, s]
    A["rw_w2"] = w2.reshape(2 * KT, P, 4 * P)
    A["rw_w_out"] = np.concatenate([strips(w) for w in I["rwkv_w_out"]])
    A["mu"] = by_channel(I["rwkv_mu"])
    per_tile = [I["rwkv_mu"][:, n] for n in range(6)] + [I["rwkv_w0"][:, 0], I["rwkv_w0"][:, 1], I["rwkv_a0"][:, 0],
               I["rwkv_a0"][:, 1], I["rwkv_k_k"], I["rwkv_k_a"], I["rwkv_r_k"].reshape(2, D), I["rwkv_ln_w"], I["rwkv_ln_b"]]
    A["rw_par"] = np.stack(per_tile, -1).reshape(2 * KT, P, NPAR)
    a, b = np.arange(P)[:, None], np.arange(P)[None, :]
    chunk, block = a // C == b // C, a // 8 == b // 8
    both = lambda m, m1: np.stack([m, m1], 1).astype(np.float32).reshape(P, 2 * P)
    A["m_x"] = -both(block & (b < a), block & (b > a))
    A["m_xt"] = -both(block & (a < b), block & (a > b))
    A["m_nt"] = both(chunk & ~block & (a < b), chunk & ~block & (a > b))
    A["m_s"] = both(chunk & (a < b), chunk & (a > b))
    A["m_i"] = both(chunk & (a <= b), chunk & (a >= b))
    A["seq_mask"] = np.tile((np.arange(2 * W) % C != 0).astype(np.float32), (P, 1))
    A["eye2"] = np.tile(np.eye(C, dtype=np.float32), (2, 1))
    A["s5_w_in"], A["s5_w_glu"], A["s5_w_out"] = (strips(I["s5_w_" + n][0]) for n in ("in", "glu", "out"))
    A["b_glu"] = by_channel(I["s5_b_glu"])
    per_state = lambda v: v.reshape(2, GP, 2 * NS).transpose(2, 0, 1).reshape(P, 2 * GP)
    A["s5_lr"], A["s5_li"] = per_state(I["s5_lam_re"][0]), per_state(I["s5_lam_im"][0])
    A["s5_dt"] = per_state(np.repeat(I["s5_log_dt"][0][:, :, None], NS, 2))
    for n in ("re", "im"):
        A["s5_b" + n[0]] = I["s5_b_" + n][0].reshape(GP, P, 16).transpose(1, 0, 2).reshape(P, GP * 16)
        A["s5_c" + n[0]] = I["s5_c_" + n][0].reshape(GP, 2, 16, NS).transpose(1, 3, 0, 2).reshape(P, GP * 16)
    A["s5_dsk"] = np.tile(I["s5_d"][0].reshape(G, 16).T, (S, 1))
    return {n: np.ascontiguousarray(a, dtype=np.float32) for n, a in A.items()}


DEPTH = 4


def kernel(**inputs):
    import concourse.bacc as bacc
    from concourse.bass_utils import run_bass_kernel_spmd

    nc = bacc.Bacc("TRN2", target_bir_lowering=False, num_devices=1)
    arrays = layout(inputs)
    A = {n: nc.dram_tensor(n, a.shape, F32, kind="ExternalInput").ap() for n, a in arrays.items()}
    out = nc.dram_tensor("out", (KT, P, NLAT), F32, kind="ExternalOutput").ap()
    program(nc, A, out, list(range(DEPTH)), DEPTH)
    r = run_bass_kernel_spmd(nc, [arrays], core_ids=[0])
    got = r.results[0]["out"].reshape(D, NLAT)
    return np.ascontiguousarray(got.T)[None]
```
